# Optimizing a Trainium2 kernel written in Bass

```python
import jax, jax.numpy as jnp
from jax import lax
import numpy as np

D_MODEL = 1024
BATCH = 1
SEQ = 256
DEPTH = 2

GRID_W = 64
CTX_LEN = 256
HEAD_DIM = 128
A_HEADS = 4
A_KV_HEADS = 2
B_HEADS = 4
B_KV_HEADS = 2
Q_WIDTH = (A_HEADS + B_HEADS) * HEAD_DIM
KV_WIDTH = 2 * (A_KV_HEADS + B_KV_HEADS) * HEAD_DIM
BLOCK = 128
WINDOW = 128
ROPE_THETA = 10000.0
FNET_GROUPS = 4
D_FF = 2816
CONV_W = 3
N_MOD = 6
N_ATTN_LAYERS = (DEPTH + 1) // 2
N_FOURIER_LAYERS = DEPTH // 2
EPS = 1e-6


F32 = jnp.float32

def rms_norm(x, g):
    xf = x.astype(F32)
    y = xf * lax.rsqrt(jnp.mean(xf * xf, axis=-1, keepdims=True) + EPS)
    return (y * g.astype(F32)).astype(x.dtype)

def modulate(h, shift, scale):
    return h * (1 + scale) + shift

def adaln_params(cond, w, bias):
    m = jax.nn.silu(cond) @ w + bias
    return jnp.split(m[..., None, :], N_MOD, axis=-1)

def axial_rope_tables(row, col):
    n_freq = HEAD_DIM // 4
    inv = ROPE_THETA ** (-jnp.arange(n_freq, dtype=F32) / n_freq)
    ang = jnp.stack([row.astype(F32)[:, None] * inv, col.astype(F32)[:, None] * inv], axis=1)
    return jnp.cos(ang), jnp.sin(ang)

def apply_rope(x, cos, sin):
    b, l, h, dh = x.shape
    xs = x.reshape(b, l, h, 2, 2, dh // 4)
    x1, x2 = xs[..., 0, :], xs[..., 1, :]
    cs = cos[None, :, None].astype(x.dtype)
    sn = sin[None, :, None].astype(x.dtype)
    out = jnp.stack([x1 * cs - x2 * sn, x2 * cs + x1 * sn], axis=-2)
    return out.reshape(b, l, h, dh)

def group_heads(q, n_kv):
    b, l, h, dh = q.shape
    return q.reshape(b, l, n_kv, h // n_kv, dh)

def split_kv(kv):
    b, l, _ = kv.shape
    a = A_KV_HEADS * HEAD_DIM
    bb = B_KV_HEADS * HEAD_DIM
    k_a, v_a, k_b, v_b = jnp.split(kv, [a, 2 * a, 2 * a + bb], axis=-1)
    return (k_a.reshape(b, l, A_KV_HEADS, HEAD_DIM), v_a.reshape(b, l, A_KV_HEADS, HEAD_DIM),
            k_b.reshape(b, l, B_KV_HEADS, HEAD_DIM), v_b.reshape(b, l, B_KV_HEADS, HEAD_DIM))

def attend(q, k, v, sink=None):
    s = jnp.einsum('bqkgd,bskd->bkgqs', q, k, preferred_element_type=F32) * (HEAD_DIM ** -0.5)
    if sink is not None:
        s_sink = jnp.broadcast_to(sink.astype(F32)[None, :, :, None, None], s.shape[:-1] + (1,))
        p = jax.nn.softmax(jnp.concatenate([s_sink, s], axis=-1), axis=-1)[..., 1:]
    else:
        p = jax.nn.softmax(s, axis=-1)
    return jnp.einsum('bkgqs,bskd->bqkgd', p.astype(v.dtype), v)

def global_attention(q, k, v, k_ctx, v_ctx):
    b, l, hkv, g, dh = q.shape
    k_all = jnp.concatenate([k_ctx, k], axis=1)
    v_all = jnp.concatenate([v_ctx, v], axis=1)
    qb = jnp.moveaxis(q.reshape(b, l // BLOCK, BLOCK, hkv, g, dh), 1, 0)
    o = lax.map(lambda qblk: attend(qblk, k_all, v_all), qb)
    return jnp.moveaxis(o, 0, 1).reshape(b, l, hkv * g * dh)

def window_attention(q, k, v, k_ctx, v_ctx, sink):
    b, l, hkv, g, dh = q.shape
    nb = l // BLOCK
    zpad = jnp.zeros((b, BLOCK, hkv, dh), k.dtype)

    def band(t):
        tp = jnp.concatenate([zpad, t, zpad], axis=1).reshape(b, nb + 2, BLOCK, hkv, dh)
        return jnp.concatenate([tp[:, :-2], tp[:, 1:-1], tp[:, 2:]], axis=2)

    kb, vb = band(k), band(v)
    qb = q.reshape(b, nb, BLOCK, hkv, g, dh)
    scale = HEAD_DIM ** -0.5
    s_loc = jnp.einsum('bnqkgd,bnskd->bnkgqs', qb, kb, preferred_element_type=F32) * scale
    s_ctx = jnp.einsum('bnqkgd,bskd->bnkgqs', qb, k_ctx, preferred_element_type=F32) * scale
    qi = jnp.arange(BLOCK)[:, None]
    si = jnp.arange(3 * BLOCK)[None, :]
    in_window = jnp.abs(si - BLOCK - qi) <= WINDOW
    kpos = (jnp.arange(nb)[:, None] - 1) * BLOCK + jnp.arange(3 * BLOCK)[None, :]
    in_range = (kpos >= 0) & (kpos < l)
    valid = in_window[None] & in_range[:, None, :]
    s_loc = jnp.where(valid[None, :, None, None], s_loc, -jnp.inf)
    s_sink = jnp.broadcast_to(sink.astype(F32)[None, None, :, :, None, None], s_ctx.shape[:-1] + (1,))
    p = jax.nn.softmax(jnp.concatenate([s_sink, s_ctx, s_loc], axis=-1), axis=-1)
    c_len = k_ctx.shape[1]
    p_ctx = p[..., 1:1 + c_len].astype(v.dtype)
    p_loc = p[..., 1 + c_len:].astype(v.dtype)
    o = (jnp.einsum('bnkgqs,bskd->bnqkgd', p_ctx, v_ctx)
         + jnp.einsum('bnkgqs,bnskd->bnqkgd', p_loc, vb))
    return o.reshape(b, l, hkv * g * dh)

def attention_mixers(h, hc, w_in, w_out, q_g, k_g, sink, cos, sin, with_ctx_queries):
    b, l, _ = h.shape
    c_len = hc.shape[1]
    proj = h @ w_in
    q_all, kv = proj[..., :Q_WIDTH], proj[..., Q_WIDTH:]
    q_a = q_all[..., :A_HEADS * HEAD_DIM].reshape(b, l, A_HEADS, HEAD_DIM)
    q_b = q_all[..., A_HEADS * HEAD_DIM:].reshape(b, l, B_HEADS, HEAD_DIM)
    k_a, v_a, k_b, v_b = split_kv(kv)
    q_a = apply_rope(rms_norm(q_a, q_g), cos, sin)
    k_a = apply_rope(rms_norm(k_a, k_g), cos, sin)
    q_b = apply_rope(q_b, cos, sin)
    k_b = apply_rope(k_b, cos, sin)
    k_ac, v_ac, k_bc, v_bc = split_kv(hc @ w_in[:, Q_WIDTH:])
    k_ac = rms_norm(k_ac, k_g)
    sink_hg = sink.reshape(B_KV_HEADS, B_HEADS // B_KV_HEADS)
    o_a = global_attention(group_heads(q_a, A_KV_HEADS), k_a, v_a, k_ac, v_ac)
    o_b = window_attention(group_heads(q_b, B_KV_HEADS), k_b, v_b, k_bc, v_bc, sink_hg)
    y = jnp.concatenate([o_a, o_b], axis=-1) @ w_out
    if not with_ctx_queries:
        return y, None
    qc = hc @ w_in[:, :Q_WIDTH]
    qc_a = rms_norm(qc[..., :A_HEADS * HEAD_DIM].reshape(b, c_len, A_HEADS, HEAD_DIM), q_g)
    qc_b = qc[..., A_HEADS * HEAD_DIM:].reshape(b, c_len, B_HEADS, HEAD_DIM)
    oc_a = attend(group_heads(qc_a, A_KV_HEADS), k_ac, v_ac).reshape(b, c_len, -1)
    oc_b = attend(group_heads(qc_b, B_KV_HEADS), k_bc, v_bc, sink_hg).reshape(b, c_len, -1)
    yc = jnp.concatenate([oc_a, oc_b], axis=-1) @ w_out
    return y, yc

def fourier_mix(h):
    b, l, d = h.shape
    hg = h.reshape(b, l, FNET_GROUPS, d // FNET_GROUPS).astype(F32)
    f = jnp.fft.fft2(hg, axes=(1, 3), norm="ortho").real
    return f.reshape(b, l, d).astype(h.dtype)

def conv_ffn(h, w_up, conv_w, conv_b, w_down):
    u = h @ w_up
    up = jnp.pad(u, ((0, 0), (1, 1), (0, 0)))
    u = up[:, :-2] * conv_w[0] + up[:, 1:-1] * conv_w[1] + up[:, 2:] * conv_w[2] + conv_b
    gate, val = jnp.split(u, 2, axis=-1)
    return (jax.nn.silu(gate) * val) @ w_down

def first_inputs(seed: int = 0) -> dict:
    key = jax.random.key(seed)
    ks = jax.random.split(key, 17)

    def nrm(k, shape, scale):
        return jax.random.normal(k, shape, F32) * scale

    return {
        "x": nrm(ks[0], (BATCH, SEQ, D_MODEL), 1.0),
        "c": nrm(ks[1], (BATCH, D_MODEL), 1.0),
        "ctx": nrm(ks[2], (BATCH, CTX_LEN, D_MODEL), 1.0),
        "c_ctx": nrm(ks[3], (D_MODEL,), 1.0),
        "mod_w": nrm(ks[4], (DEPTH, D_MODEL, N_MOD * D_MODEL), 0.5 * D_MODEL ** -0.5),
        "mod_b": nrm(ks[5], (DEPTH, N_MOD * D_MODEL), 0.02),
        "norm_g": 1.0 + nrm(ks[6], (DEPTH, 4, D_MODEL), 0.02),
        "attn_w_in": nrm(ks[7], (N_ATTN_LAYERS, D_MODEL, Q_WIDTH + KV_WIDTH), D_MODEL ** -0.5),
        "attn_w_out": nrm(ks[8], (N_ATTN_LAYERS, Q_WIDTH, D_MODEL), Q_WIDTH ** -0.5),
        "q_norm_g": 1.0 + nrm(ks[9], (N_ATTN_LAYERS, HEAD_DIM), 0.02),
        "k_norm_g": 1.0 + nrm(ks[10], (N_ATTN_LAYERS, HEAD_DIM), 0.02),
        "sink": nrm(ks[11], (N_ATTN_LAYERS, B_HEADS), 0.5),
        "fourier_w_out": nrm(ks[12], (N_FOURIER_LAYERS, D_MODEL, D_MODEL), D_MODEL ** -0.5),
        "ffn_w_up": nrm(ks[13], (DEPTH, D_MODEL, 2 * D_FF), D_MODEL ** -0.5),
        "ffn_conv_w": nrm(ks[14], (DEPTH, CONV_W, 2 * D_FF), CONV_W ** -0.5),
        "ffn_conv_b": nrm(ks[15], (DEPTH, 2 * D_FF), 0.02),
        "ffn_w_down": nrm(ks[16], (DEPTH, D_FF, D_MODEL), D_FF ** -0.5),
    }

def first_block(x, c, ctx, c_ctx, mod_w, mod_b, norm_g, attn_w_in, attn_w_out, q_norm_g, k_norm_g, sink,
              fourier_w_out, ffn_w_up, ffn_conv_w, ffn_conv_b, ffn_w_down):
    b, l, d = x.shape
    rows = l // GRID_W
    row = jnp.repeat(jnp.arange(rows), GRID_W)
    col = jnp.tile(jnp.arange(GRID_W), rows)
    cos, sin = axial_rope_tables(row, col)

    for i in range(DEPTH):
        ctx_next = any(j % 2 == 0 for j in range(i + 1, DEPTH))
        need_hc = (i % 2 == 0) or ctx_next
        sh1, sc1, g1, sh2, sc2, g2 = adaln_params(c, mod_w[i], mod_b[i])
        h = modulate(rms_norm(x, norm_g[i, 0]), sh1, sc1)
        if need_hc:
            csh1, csc1, cg1, csh2, csc2, cg2 = adaln_params(c_ctx, mod_w[i], mod_b[i])
            hc = modulate(rms_norm(ctx, norm_g[i, 0]), csh1, csc1)
        if i % 2 == 0:
            a = i // 2
            y, yc = attention_mixers(h, hc, attn_w_in[a], attn_w_out[a], q_norm_g[a], k_norm_g[a], sink[a],
                                     cos, sin, ctx_next)
        else:
            w_f = fourier_w_out[i // 2]
            y = fourier_mix(h) @ w_f
            yc = fourier_mix(hc) @ w_f if ctx_next else None
        x = x + g1 * rms_norm(y, norm_g[i, 1])
        h = modulate(rms_norm(x, norm_g[i, 2]), sh2, sc2)
        x = x + g2 * rms_norm(conv_ffn(h, ffn_w_up[i], ffn_conv_w[i], ffn_conv_b[i], ffn_w_down[i]), norm_g[i, 3])
        if ctx_next:
            ctx = ctx + cg1 * rms_norm(yc, norm_g[i, 1])
            hc = modulate(rms_norm(ctx, norm_g[i, 2]), csh2, csc2)
            ctx = ctx + cg2 * rms_norm(conv_ffn(hc, ffn_w_up[i], ffn_conv_w[i], ffn_conv_b[i], ffn_w_down[i]),
                                       norm_g[i, 3])
    return x


N_META = 16
DEEPNORM_ALPHA = (2 * DEPTH) ** 0.25
DEEPNORM_BETA = (8 * DEPTH) ** -0.25
LN_EPS = 1e-5
RG_WIDTH = 1344
RG_BLOCKS = 8
RG_BLOCK_W = RG_WIDTH // RG_BLOCKS
RG_CONV_W = 4
RG_C = 8.0
GLA_HEADS = 4
GLA_DK = D_MODEL // 2 // GLA_HEADS
GLA_DV = D_MODEL // GLA_HEADS
GLA_QK = GLA_HEADS * GLA_DK
GLA_VD = GLA_HEADS * GLA_DV
GLA_RANK = 16
GLA_TAU = 16.0
GLA_CHUNK = 64
GLA_PAD = (-N_META) % GLA_CHUNK
D_FF_2 = 3584
N_EXPERTS = 8
TOP_K = 2
N_REC = (DEPTH + 1) // 2
N_GLA = DEPTH // 2


def _normalize(x):
    xf = x.astype(jnp.float32)
    mu = jnp.mean(xf, axis=-1, keepdims=True)
    xc = xf - mu
    var = jnp.mean(xc * xc, axis=-1, keepdims=True)
    return xc * lax.rsqrt(var + LN_EPS)

def layer_norm(x, g, b):
    return (_normalize(x) * g + b).astype(x.dtype)

def swiglu(h, w_in, w_out):
    gate, up = jnp.split(h @ w_in, 2, axis=-1)
    return (jax.nn.silu(gate) * up) @ w_out

def _linear_scan_combine(c1, c2):
    a1, b1 = c1
    a2, b2 = c2
    return a1 * a2, a2 * b1 + b2

def rglru_block(h, w_in, conv_w, conv_b, w_gates, b_gates, lam, w_out):
    Bsz, T, _ = h.shape
    proj = h @ w_in
    gate_branch, xr = jnp.split(proj, 2, axis=-1)
    xp = jnp.pad(xr, ((0, 0), (RG_CONV_W - 1, 0), (0, 0)))
    xc = conv_b
    for tap in range(RG_CONV_W):
        xc = xc + xp[:, tap:tap + T] * conv_w[tap]
    gates = jnp.einsum('btnc,gncd->gbtnd', xc.reshape(Bsz, T, RG_BLOCKS, RG_BLOCK_W), w_gates)
    gates = gates.reshape(2, Bsz, T, RG_WIDTH) + b_gates[:, None, None, :]
    gates = jax.nn.sigmoid(gates.astype(jnp.float32))
    r_t, i_t = gates[0], gates[1]
    log_a = -RG_C * r_t * jax.nn.softplus(-lam.astype(jnp.float32))
    a_t = jnp.exp(log_a)
    u_t = jnp.sqrt(-jnp.expm1(2.0 * log_a)) * (i_t * xc)
    _, hs = lax.associative_scan(_linear_scan_combine, (a_t, u_t), axis=1)
    y = hs * jax.nn.gelu(gate_branch.astype(jnp.float32))
    return (y @ w_out).astype(h.dtype)

def gla_block(h, w_in, w_gate_up, b_gate, norm_g, w_out):
    Bsz, T, _ = h.shape
    proj = h @ w_in
    q, k, v, r, z = jnp.split(
        proj, [GLA_QK, 2 * GLA_QK, 2 * GLA_QK + GLA_VD, 2 * GLA_QK + 2 * GLA_VD], axis=-1)
    log_g = jax.nn.log_sigmoid((z @ w_gate_up + b_gate).astype(jnp.float32)) / GLA_TAU
    L = T + GLA_PAD
    nc = L // GLA_CHUNK

    def to_chunks(t, d):
        t = jnp.pad(t, ((0, 0), (GLA_PAD, 0), (0, 0)))
        return t.reshape(Bsz, nc, GLA_CHUNK, GLA_HEADS, d).transpose(0, 3, 1, 2, 4)

    qc = to_chunks(q, GLA_DK) * (GLA_DK ** -0.5)
    kc = to_chunks(k, GLA_DK)
    vc = to_chunks(v, GLA_DV)
    gc = to_chunks(log_g, GLA_DK)
    b = jnp.cumsum(gc, axis=3)
    b_mid = b[:, :, :, GLA_CHUNK // 2 - 1:GLA_CHUNK // 2]
    b_last = b[:, :, :, -1:]
    scores = jnp.einsum('bhncd,bhnsd->bhncs', qc * jnp.exp(b - b_mid), kc * jnp.exp(b_mid - b))
    causal = jnp.tril(jnp.ones((GLA_CHUNK, GLA_CHUNK), dtype=bool))
    scores = jnp.where(causal, scores, 0.0)
    o_intra = jnp.einsum('bhncs,bhnse->bhnce', scores, vc)
    q_in = qc * jnp.exp(b)
    k_out = kc * jnp.exp(b_last - b)
    decay = jnp.exp(b_last[:, :, :, 0])

    def step(S, xs):
        qn, kn, vn, dn = xs
        o = jnp.einsum('bhcd,bhde->bhce', qn, S)
        S = dn[..., None] * S + jnp.einsum('bhcd,bhce->bhde', kn, vn)
        return S, o

    S0 = jnp.zeros((Bsz, GLA_HEADS, GLA_DK, GLA_DV), jnp.float32)
    xs = (jnp.moveaxis(q_in, 2, 0), jnp.moveaxis(k_out, 2, 0),
          jnp.moveaxis(vc, 2, 0), jnp.moveaxis(decay, 2, 0))
    _, o_inter = lax.scan(step, S0, xs)
    o = o_intra + jnp.moveaxis(o_inter, 0, 2)
    o = o.transpose(0, 2, 3, 1, 4).reshape(Bsz, L, GLA_HEADS, GLA_DV)[:, GLA_PAD:]
    o = _normalize(o) * norm_g
    o = o.reshape(Bsz, T, GLA_VD) * jax.nn.silu(r.astype(jnp.float32))
    return (o @ w_out).astype(h.dtype)

def moe_swiglu(h, router, w_in, w_out):
    Bsz, T, D = h.shape
    hf = h.reshape(Bsz * T, D)
    logits = (hf @ router).astype(jnp.float32)
    top_logit, top_idx = lax.top_k(logits, TOP_K)
    top_w = jax.nn.softmax(top_logit, axis=-1)
    gates = jnp.einsum('nk,nke->ne', top_w, jax.nn.one_hot(top_idx, N_EXPERTS, dtype=jnp.float32))
    y = jnp.zeros((Bsz * T, D), jnp.float32)
    for e in range(N_EXPERTS):
        y = y + gates[:, e:e + 1] * swiglu(hf, w_in[e], w_out[e])
    return y.reshape(Bsz, T, D).astype(h.dtype)

def second_inputs(seed: int = 0) -> dict:
    key = jax.random.key(seed)
    ks = jax.random.split(key, 24)
    f32 = jnp.float32

    def nrm(k, shape, fan_in, scale=1.0):
        return jax.random.normal(k, shape, f32) * (scale * fan_in ** -0.5)

    x = jax.random.normal(ks[0], (BATCH, SEQ, D_MODEL), f32)
    meta_tokens = jax.random.normal(ks[1], (N_META, D_MODEL), f32)
    ln_gain = 1.0 + 0.02 * jax.random.normal(ks[2], (DEPTH, 2, D_MODEL), f32)
    ln_bias = 0.02 * jax.random.normal(ks[3], (DEPTH, 2, D_MODEL), f32)
    rg_w_in = nrm(ks[4], (N_REC, D_MODEL, 2 * RG_WIDTH), D_MODEL)
    rg_conv_w = nrm(ks[5], (N_REC, RG_CONV_W, RG_WIDTH), RG_CONV_W)
    rg_conv_b = 0.02 * jax.random.normal(ks[6], (N_REC, RG_WIDTH), f32)
    rg_w_gates = nrm(ks[7], (N_REC, 2, RG_BLOCKS, RG_BLOCK_W, RG_BLOCK_W), RG_BLOCK_W)
    rg_b_gates = 0.02 * jax.random.normal(ks[8], (N_REC, 2, RG_WIDTH), f32)
    a_pow_c = jax.random.uniform(ks[9], (N_REC, RG_WIDTH), f32, minval=0.9, maxval=0.999)
    a_base = a_pow_c ** (1.0 / RG_C)
    rg_lambda = jnp.log(a_base) - jnp.log1p(-a_base)
    rg_w_out = nrm(ks[10], (N_REC, RG_WIDTH, D_MODEL), RG_WIDTH, DEEPNORM_BETA)
    gla_w_in = nrm(ks[11], (N_GLA, D_MODEL, 2 * GLA_QK + 2 * GLA_VD + GLA_RANK), D_MODEL)
    gla_w_gate_up = nrm(ks[12], (N_GLA, GLA_RANK, GLA_QK), GLA_RANK)
    gla_b_gate = 2.0 + 0.1 * jax.random.normal(ks[13], (N_GLA, GLA_QK), f32)
    gla_norm_g = 1.0 + 0.02 * jax.random.normal(ks[14], (N_GLA, GLA_HEADS, GLA_DV), f32)
    gla_w_out = nrm(ks[15], (N_GLA, GLA_VD, D_MODEL), GLA_VD, DEEPNORM_BETA)
    ffn_w_in = nrm(ks[16], (N_REC, D_MODEL, 2 * D_FF_2), D_MODEL)
    ffn_w_out = nrm(ks[17], (N_REC, D_FF_2, D_MODEL), D_FF_2, DEEPNORM_BETA)
    moe_router = nrm(ks[18], (N_GLA, D_MODEL, N_EXPERTS), D_MODEL)
    moe_w_in = nrm(ks[19], (N_GLA, N_EXPERTS, D_MODEL, 2 * D_FF_2), D_MODEL)
    moe_w_out = nrm(ks[20], (N_GLA, N_EXPERTS, D_FF_2, D_MODEL), D_FF_2, DEEPNORM_BETA)
    return {
        "x": x, "meta_tokens": meta_tokens, "ln_gain": ln_gain, "ln_bias": ln_bias,
        "rg_w_in": rg_w_in, "rg_conv_w": rg_conv_w, "rg_conv_b": rg_conv_b,
        "rg_w_gates": rg_w_gates, "rg_b_gates": rg_b_gates, "rg_lambda": rg_lambda,
        "rg_w_out": rg_w_out,
        "gla_w_in": gla_w_in, "gla_w_gate_up": gla_w_gate_up, "gla_b_gate": gla_b_gate,
        "gla_norm_g": gla_norm_g, "gla_w_out": gla_w_out,
        "ffn_w_in": ffn_w_in, "ffn_w_out": ffn_w_out,
        "moe_router": moe_router, "moe_w_in": moe_w_in, "moe_w_out": moe_w_out,
    }

def second_block(x, meta_tokens, ln_gain, ln_bias,
              rg_w_in, rg_conv_w, rg_conv_b, rg_w_gates, rg_b_gates, rg_lambda, rg_w_out,
              gla_w_in, gla_w_gate_up, gla_b_gate, gla_norm_g, gla_w_out,
              ffn_w_in, ffn_w_out, moe_router, moe_w_in, moe_w_out):
    Bsz = x.shape[0]
    meta = jnp.broadcast_to(meta_tokens.astype(x.dtype)[None], (Bsz, N_META, D_MODEL))
    h = jnp.concatenate([meta, x], axis=1)
    for i in range(DEPTH):
        j = i // 2
        if i % 2 == 0:
            mix = rglru_block(h, rg_w_in[j], rg_conv_w[j], rg_conv_b[j], rg_w_gates[j],
                              rg_b_gates[j], rg_lambda[j], rg_w_out[j])
        else:
            mix = gla_block(h, gla_w_in[j], gla_w_gate_up[j], gla_b_gate[j],
                            gla_norm_g[j], gla_w_out[j])
        h = layer_norm(DEEPNORM_ALPHA * h + mix, ln_gain[i, 0], ln_bias[i, 0])
        if i % 2 == 0:
            ff = swiglu(h, ffn_w_in[j], ffn_w_out[j]).astype(h.dtype)
        else:
            ff = moe_swiglu(h, moe_router[j], moe_w_in[j], moe_w_out[j])
        h = layer_norm(DEEPNORM_ALPHA * h + ff, ln_gain[i, 1], ln_bias[i, 1])
    return h[:, N_META:]


def setup_inputs(seed=0):
    out = dict(first_inputs(seed))
    for name, value in second_inputs(seed + 1).items():
        if name != "x":
            out[name + "_2"] = value
    return out


def reference(
    x, c, ctx, c_ctx, mod_w, mod_b, norm_g, attn_w_in, attn_w_out, q_norm_g, k_norm_g, sink,
    fourier_w_out, ffn_w_up, ffn_conv_w, ffn_conv_b, ffn_w_down, meta_tokens_2, ln_gain_2,
    ln_bias_2, rg_w_in_2, rg_conv_w_2, rg_conv_b_2, rg_w_gates_2, rg_b_gates_2, rg_lambda_2,
    rg_w_out_2, gla_w_in_2, gla_w_gate_up_2, gla_b_gate_2, gla_norm_g_2, gla_w_out_2,
    ffn_w_in_2, ffn_w_out_2, moe_router_2, moe_w_in_2, moe_w_out_2,
):
    x = first_block(
        x, c, ctx, c_ctx, mod_w, mod_b, norm_g, attn_w_in, attn_w_out, q_norm_g, k_norm_g, sink,
        fourier_w_out, ffn_w_up, ffn_conv_w, ffn_conv_b, ffn_w_down,
    )
    return second_block(
        x, meta_tokens_2, ln_gain_2, ln_bias_2, rg_w_in_2, rg_conv_w_2, rg_conv_b_2,
        rg_w_gates_2, rg_b_gates_2, rg_lambda_2, rg_w_out_2, gla_w_in_2, gla_w_gate_up_2,
        gla_b_gate_2, gla_norm_g_2, gla_w_out_2, ffn_w_in_2, ffn_w_out_2, moe_router_2,
        moe_w_in_2, moe_w_out_2,
    )


_drawn_inputs = setup_inputs


def setup_inputs(seed=0):
    import zlib

    import numpy as np

    out = dict(_drawn_inputs(seed))
    spreads = {}
    factors = {'q_norm_g': 8.0,
     'k_norm_g': 8.0,
     'sink': 22.936,
     'ffn_conv_b': 3.286,
     'rg_b_gates_2': 7.722,
     'gla_b_gate_2': 35.6,
     'gla_norm_g_2': 8.0,
     'gla_w_gate_up_2': 8.0}
    for name, (base, spread) in spreads.items():
        noise = np.random.default_rng([zlib.crc32(name.encode()), seed]).standard_normal(out[name].shape)
        drawn = base * np.exp(spread * noise) if base else spread * noise
        out[name] = __import__('jax').numpy.asarray(drawn.astype(out[name].dtype))
    for name, factor in factors.items():
        out[name] = (out[name] * factor).astype(out[name].dtype)
    return out
```

```python
from contextlib import ExitStack

import numpy as np
import concourse.bass as bass
from concourse import mybir

F32 = mybir.dt.float32
I32 = mybir.dt.int32
F32R = mybir.dt.float32r
ACT = mybir.ActivationFunctionType
ALU = mybir.AluOpType
AX = mybir.AxisListType

P = 128
D = 1024
KT = D // P
SEQ, CTX, META = 256, 256, 16
HEADS, HD = 8, 128
FF1, FF1T = 2816, 2816 // P
FF2, FF2T = 3584, 3584 // P
RGW, RGT = 1344, 84
RGN = RGW // RGT
RGB = 8
GH, GDV, GCH = 4, 256, 64
NE = 8
PADT = 48
TOK = PADT + META + SEQ
M0, X0 = PADT, PADT + META
T2 = META + SEQ
NCH = TOK // GCH
EPS, LN_EPS = 1e-6, 1e-5
ALPHA = (2 * 2) ** 0.25
SCALE = HD ** -0.5
CHUNK = 4096
RING = 3
BLK = CHUNK // P
PAIRS = CHUNK // (2 * D)
MOE_UP, MOE_DOWN = FF2 // 256, FF2 * D // P // CHUNK
MOE_CH = MOE_UP + MOE_DOWN
MOE_ORDER = []
for _c in range(MOE_UP):
    MOE_ORDER.append(("up", _c))
    if _c % 2 == 1 and _c >= 3:
        MOE_ORDER.append(("down", (_c - 3) // 2))
MOE_ORDER.append(("down", MOE_DOWN - 1))
HALF = CHUNK // 2
HALVES = 2 * MOE_CH
SPLIT = 3
OVER = 3
ITEMS = NE + OVER

PCOLS = {}


def _cols():
    at = 0
    for name, n in [("cvec", 2 * KT), ("mod_b", 2 * 48), ("norm_g", 2 * 4 * KT), ("qg", 1), ("kg", 1),
                    ("sink", 4), ("conv_w0", 3 * 2 * FF1T), ("conv_b0", 2 * FF1T),
                    ("conv_w1", 3 * 2 * FF1T), ("conv_b1", 2 * FF1T), ("ln_g", 4 * KT), ("ln_b", 4 * KT),
                    ("rg_conv", 4 * RGN), ("rg_cb", RGN), ("rg_gb", 2 * RGN), ("rg_lam", RGN),
                    ("gla_bg", GH), ("gla_ng", KT), ("router", KT * NE), ("gla_wz", KT * 16),
                    ("gla_wg", GH * P)]:
        PCOLS[name] = (at, n)
        at += n
    return at


NPAR = _cols()

SHARED = {}


def _share(family, stages, **signals):
    for kind, times in signals.items():
        for n, stage in enumerate(stages):
            SHARED[f"{stage}_{kind}"] = (f"{family}_{kind}", n * times)


_share("rms", ["n0x", "n0c", "n0y", "n0f", "n0g", "n1x", "n1y", "n1f", "n1g"], sq=KT, sum=1, var=1, std=1, scaled=KT)
_share("rms", ["n0x", "n0c", "n0f", "n1x", "n1f"], out=KT)
_share("rms", ["n0y", "n0g", "n1y", "n1g"], res=KT)
_share("ln", ["ln0", "ln1", "ln2", "ln3"], mean=1, centred=4, sq=4, sum=1, var=1, std=1, scaled=4, out=KT)
_share("ffn", ["ffn0", "ffn1"], up=FF1T, tap1=FF1T, tap0=2 * FF1T, conv=FF1T, silu=FF1T, act=FF1T, down=KT, read=KT)
_share("mix", ["mix0", "mix1", "mix2", "mix3"], tile=KT, read=KT)


def block_program(nc, A, OUT, last=None):
    ctx = ExitStack()
    with ctx:
        def sb(name, shape, dt=F32):
            return ctx.enter_context(nc.sbuf_tensor(name, shape, dt))

        sems = {}

        def sem(name):
            name = SHARED.get(name, (name, 0))[0]
            if name not in sems:
                sems[name] = ctx.enter_context(nc.semaphore(name))
            return sems[name]

        def at(name, value):
            return sem(name), value + SHARED.get(name, (name, 0))[1]

        ring = sb("ring", [P, RING, CHUNK])
        WHI = sb("WHI", [P, SPLIT, HALF], F32R)
        WLO = sb("WLO", [P, SPLIT, HALF], F32R)
        HGH, HGL = sb("HGH", [P, KT, P], F32R), sb("HGL", [P, KT, P], F32R)
        AHI, ALO = sb("AHI", [P, 2, 4, P], F32R), sb("ALO", [P, 2, 4, P], F32R)
        X = sb("X", [P, KT, TOK])
        HB = sb("HB", [P, 4096])
        Y = sb("Y", [P, 2560])
        BIG = sb("BIG", [P, 8704])
        SCR = sb("SCR", [P, 3072])
        PAR = sb("PAR", [P, NPAR])
        STAT = sb("STAT", [P, 3, 320])
        ONES = sb("ONES", [P, P])
        IDENT = sb("IDENT", [P, P])
        ROPE = sb("ROPE", [P, 2, SEQ])
        MOD = sb("MOD", [P, 2, 48, 2])
        COEF = sb("COEF", [P, 2, 5, KT])
        SM = sb("SM", [P, 64])
        bank = [ctx.enter_context(nc.psum_tensor(f"bank{i}", [P, 512], F32)) for i in range(8)]

        def par(name, a=0, n=None):
            at, size = PCOLS[name]
            return PAR[:, at + a:at + (size if n is None else a + n)]

        def view(buf, at, *dims):
            n = int(np.prod(dims))
            v = buf[:, at:at + n]
            if len(dims) == 2:
                return v.rearrange("p (a b) -> p a b", b=dims[1])
            if len(dims) == 3:
                return v.rearrange("p (a b c) -> p a b c", b=dims[1], c=dims[2])
            return v

        xs = X[:, :, X0:TOK]

        plan, where = [], {}

        def weights(name, n, rows, words, used, value):
            for c in range(n):
                slot, turn = len(plan) % RING, len(plan) // RING + 1
                where[name, c] = (slot, 16 * turn)
                plan.append((A[name][c, 0:rows, 0:words(c)], slot, rows, words(c), used, value(c)))

        def one(name, c, rows=P, words=lambda c: CHUNK, used=None, value=None):
            slot, turn = len(plan) % RING, len(plan) // RING + 1
            where[name, c] = (slot, 16 * turn)
            plan.append((A[name][c, 0:rows, 0:words(c)], slot, rows, words(c), used, value(c)))

        def down_words(c):
            return min(CHUNK, FF1T * KT * P - c * CHUNK)

        def rg_words(c):
            return min(6, 2 * RGN - 6 * c) * KT * RGT

        mod_jobs = [(0, c, v) for c in range(4) for v in range(2)] + [(0, c, 0) for c in range(4, 12)] + \
                   [(1, c, 0) for c in range(12)]
        mod_number = {job: n for n, job in enumerate(mod_jobs)}

        def mod_used(l):
            return lambda c: mod_number[l, c, 1 if l == 0 and c < 4 else 0] + 1

        for c in range(4):
            one("mod0", c, used="mod_sum", value=mod_used(0))
        weights("attn_in", 4, P, lambda c: CHUNK, "qkv_tile", lambda c: [4, 8, 12, 16][c])
        for c in range(4, 12):
            one("mod0", c, used="mod_sum", value=mod_used(0))
        weights("attn_out", 2, P, lambda c: CHUNK, "mix0_tile", lambda c: 4 * c + 4)

        def plan_ffn(l):
            for c in range(FF1T // PAIRS):
                one(f"up{l}", c, used=f"ffn{l}_up", value=lambda c: PAIRS * (c + 1))
                if l == 0:
                    one("mod1", c, used="mod_sum", value=mod_used(1))
            if l == 0:
                one("mod1", 11, used="mod_sum", value=mod_used(1))
            weights(f"down{l}", 6, P, down_words, f"ffn{l}_down",
                    lambda c: min(KT, (BLK * (c + 1) - 1) // FF1T + 1))

        plan_ffn(0)
        weights("four_out", 2, P, lambda c: CHUNK, "mix1_tile", lambda c: 4 * c + 4)
        plan_ffn(1)
        for name, c in [("rg_in", 0), ("rg_in", 1), ("rg_in", 2), ("rg_gates", 0), ("rg_gates", 1),
                        ("rg_in", 3), ("rg_in", 4), ("rg_in", 5)]:
            if name == "rg_in":
                one(name, c, words=rg_words, used="rg_proj", value=lambda c: min(2 * RGN, 6 * c + 6))
            else:
                one(name, c, rows=RGT, words=lambda c: 48 * RGT if c < 1 else 16 * RGT,
                    used="rg_gate", value=lambda c: 24 if c < 1 else 32)
        weights("rg_out", 4, RGT, lambda c: CHUNK, "mix2_tile", lambda c: 2 * c + 2)
        weights("ffn_in", FF2T // PAIRS, P, lambda c: CHUNK, "ffn2_up", lambda c: PAIRS * (c + 1))
        weights("ffn_out", FF2T * KT // BLK, P, lambda c: CHUNK, "ffn2_down",
                lambda c: min(KT, (BLK * (c + 1) - 1) // FF2T + 1))
        for c, (used, value) in enumerate([("gla_proj", 4), ("gla_proj", 8), ("gla_v", 3), ("gla_v", 6),
                                           ("gla_r", 4), ("gla_r", 8)]):
            one("gla_in", c, used=used, value=lambda c, v=value: v)
        weights("gla_out", 2, P, lambda c: CHUNK, "mix3_tile", lambda c: 4 * c + 4)
        MOE0 = len(plan)

        stages = ["norm0", "attn", "ffn0", "norm1", "four", "ffn1", "rg", "ffn2", "gla", "moe"]
        stages = stages[:stages.index(last) + 1] if last else stages

        def on(s):
            return s in stages

        def take(pe, name, c):
            slot, value = where[name, c]
            pe.wait_ge(*at(f"weights_in{slot}", value))
            return ring[:, slot, :]

        def rms_act(act, p, src, T, after, shift, dst):
            name, value, each = after
            for j in range(KT):
                act.wait_ge(*at(name, value + each * j))
                nc.scalar.activation(view(SCR, 0, KT, T)[:, j, :], src[:, j, :], ACT.Square)\
                    .then_inc(sem(p + "_sq"), 1)
            root_act(act, p, T)
            for j in range(KT):
                act.wait_ge(*at(p + "_scaled", j + 1))
                nc.scalar.activation(dst[:, j, :], dst[:, j, :], ACT.Identity, bias=shift(j))\
                    .then_inc(sem(p + "_out"), 1)

        def root_act(act, p, T):
            act.wait_ge(*at(p + "_var", 1))
            nc.scalar.activation(STAT[:, 1, 0:T], STAT[:, 0, 0:T], ACT.Sqrt).then_inc(sem(p + "_std"), 1)

        def out_act(act, norm, n, src, read):
            nc.scalar.activation(view(SCR, 0, KT, SEQ)[:, n, :], src, ACT.Square).then_inc(sem(norm + "_sq"), 1)
            nc.scalar.activation(view(Y, 0, KT, SEQ)[:, n, :], src, ACT.Copy).then_inc(sem(read), 1)

        def square_pe(pe, p, k, T, stat):
            pe.wait_ge(*at(p + "_sq", k + 1))
            mm = nc.tensor.matmul(stat[:, 0:T], ONES[:, :], view(SCR, 0, KT, T)[:, k, :],
                                  start=(k == 0), stop=(k == KT - 1))
            if k == KT - 1:
                mm.then_inc(sem(p + "_sum"), 1)

        def rms_pe(pe, p, T, stat):
            for k in range(KT):
                square_pe(pe, p, k, T, stat)

        def rms_dve(dve, link, p, src, T, stat, scale, dst, add=None):
            dve.wait_ge(*at(p + "_sum", 1))
            nc.vector.tensor_scalar(STAT[:, 0, 0:T], stat[:, 0:T], 1.0 / D, EPS, ALU.mult, ALU.add)\
                .then_inc(sem(p + "_var"), 1)
            dve.wait_ge(*at(p + "_std", 1))
            link(nc.vector.reciprocal(STAT[:, 2, 0:T], STAT[:, 1, 0:T]))
            for j in range(KT):
                nc.vector.scalar_tensor_tensor(dst[:, j, :], src[:, j, :], scale(j), STAT[:, 2, 0:T],
                                               ALU.mult, ALU.mult).then_inc(sem(p + "_scaled"), 1)
                if add is not None and j >= 1:
                    add(j - 1)
            if add is not None:
                add(KT - 1)

        def res_dve(dve, link, p, stat, l, g):
            yv = view(Y, 0, KT, SEQ)

            def add(j):
                dve.wait_ge(*at(p + "_scaled", j + 1))
                nc.vector.tensor_tensor(xs[:, j, :], xs[:, j, :], yv[:, j, :], ALU.add).then_inc(sem(p + "_res"), 1)

            rms_dve(dve, link, p, yv, SEQ, stat, lambda j: COEF[:, l, g, j:j + 1], yv, add)

        def proj_pe(pe, name, p, rhs, T, banks, ready, norm=None):
            for n in range(KT):
                if n % 4 == 0:
                    w = take(pe, name, n // 4)
                if n >= len(banks):
                    pe.wait_ge(*at(p + "_read", n - len(banks) + 1))
                if n == 0:
                    ready()
                for k in range(KT):
                    b = (n % 4) * KT + k
                    mm = nc.tensor.matmul(bank[banks[n % len(banks)]][:, 0:T], w[:, b * P:(b + 1) * P],
                                          rhs[:, k, :], start=(k == 0), stop=(k == KT - 1))
                mm.then_inc(sem(p + "_tile"), 1)
                if norm is not None and n >= 1:
                    square_pe(pe, norm, n - 1, T, bank[7])
            if norm is not None:
                square_pe(pe, norm, KT - 1, T, bank[7])

        def proj_act(act, p, banks, norm):
            for n in range(KT):
                act.wait_ge(*at(p + "_tile", n + 1))
                out_act(act, norm, n, bank[banks[n % len(banks)]][:, 0:SEQ], p + "_read")
            root_act(act, norm, SEQ)

        def add_dve(dve, p, cols, T, banks, tile="_tile", read="_read"):
            for n in range(KT):
                dve.wait_ge(*at(p + tile, n + 1))
                nc.vector.scalar_tensor_tensor(X[:, n, cols:TOK], X[:, n, cols:TOK], ALPHA,
                                               bank[banks[n % len(banks)]][:, 0:T], ALU.mult, ALU.add)\
                    .then_inc(sem(p + read), 1)

        def ln_pe(pe, p, cols, added, b=(0, 1)):
            T = TOK - cols
            for k in range(KT):
                pe.wait_ge(*at(added, k + 1))
                mm = nc.tensor.matmul(bank[b[0]][:, 0:T], ONES[:, :], X[:, k, cols:TOK],
                                      start=(k == 0), stop=(k == KT - 1))
            mm.then_inc(sem(p + "_mean"), 1)
            for k in range(KT):
                if k % 2 == 0:
                    pe.wait_ge(*at(p + "_sq", k // 2 + 1))
                mm = nc.tensor.matmul(bank[b[1]][:, 0:T], ONES[:, :], view(SCR, 0, KT, T)[:, k, :],
                                      start=(k == 0), stop=(k == KT - 1))
            mm.then_inc(sem(p + "_sum"), 1)

        def ln_act(act, p, cols, which):
            T = TOK - cols
            for h in range(4):
                act.wait_ge(*at(p + "_centred", h + 1))
                nc.scalar.activation(view(SCR, 0, KT, T)[:, 2 * h:2 * h + 2, :],
                                     X[:, 2 * h:2 * h + 2, cols:TOK], ACT.Square).then_inc(sem(p + "_sq"), 1)
            act.wait_ge(*at(p + "_var", 1))
            nc.scalar.activation(STAT[:, 1, 0:T], STAT[:, 0, 0:T], ACT.Sqrt).then_inc(sem(p + "_std"), 1)
            for j in range(KT):
                if j % 2 == 0:
                    act.wait_ge(*at(p + "_scaled", j // 2 + 1))
                nc.scalar.activation(X[:, j, cols:TOK], X[:, j, cols:TOK], ACT.Identity,
                                     bias=par("ln_b", which * KT + j, 1), scale=par("ln_g", which * KT + j, 1))\
                    .then_inc(sem(p + "_out"), 1)

        def ln_dve(dve, link, p, cols, b=(0, 1)):
            T = TOK - cols
            dve.wait_ge(*at(p + "_mean", 1))
            mean = bank[b[0]][:, 0:T].unsqueeze(1).to_broadcast([P, 2, T])
            for h in range(4):
                xh = X[:, 2 * h:2 * h + 2, cols:TOK]
                nc.vector.scalar_tensor_tensor(xh, mean, -1.0 / D, xh, ALU.mult, ALU.add)\
                    .then_inc(sem(p + "_centred"), 1)
            dve.wait_ge(*at(p + "_sum", 1))
            nc.vector.tensor_scalar(STAT[:, 0, 0:T], bank[b[1]][:, 0:T], 1.0 / D, LN_EPS, ALU.mult, ALU.add)\
                .then_inc(sem(p + "_var"), 1)
            dve.wait_ge(*at(p + "_std", 1))
            link(nc.vector.reciprocal(STAT[:, 2, 0:T], STAT[:, 1, 0:T]))
            dve.wait_ge(*at(p + "_centred", 4))
            rstd = STAT[:, 2, 0:T].unsqueeze(1).to_broadcast([P, 2, T])
            for h in range(4):
                xh = X[:, 2 * h:2 * h + 2, cols:TOK]
                nc.vector.tensor_tensor(xh, xh, rstd, ALU.mult).then_inc(sem(p + "_scaled"), 1)

        def mod_acc(n):
            return [view(HB, 2048 + 1024 * (n % 2) + 512 * i, 512) for i in range(2)]

        def mod_sum(dve, l, c, v):
            n = mod_number[l, c, v]
            w = take(dve, f"mod{l}", c)
            acc = mod_acc(n)
            if n >= 2:
                dve.wait_ge(*at("mod_cols", n - 1))
            for k in range(KT):
                wk, ck, a = w[:, k * 512:(k + 1) * 512], par("cvec", 2 * k + v, 1), acc[k % 2]
                if k < 2:
                    nc.vector.tensor_scalar(a, wk, ck, None, ALU.mult).then_inc(sem("mod_part"), 1)
                else:
                    dve.wait_ge(*at("mod_part", KT * n + k - 1))
                    nc.vector.scalar_tensor_tensor(a, wk, ck, a, ALU.mult, ALU.add).then_inc(sem("mod_part"), 1)
            dve.wait_ge(*at("mod_part", KT * n + KT))
            nc.vector.tensor_tensor(acc[0], acc[0], acc[1], ALU.add).then_inc(sem("mod_sum"), 1)

        def mod_pe(pe, l, c, v):
            n = mod_number[l, c, v]
            pe.wait_ge(*at("mod_sum", n + 1))
            if n >= 1:
                pe.wait_ge(*at("mod_stored", n))
            for t in range(4):
                mm = nc.tensor.matmul(bank[6][:, t * P:(t + 1) * P], mod_acc(n)[0][:, t * P:(t + 1) * P],
                                      ONES[:, :], start=True, stop=True)
            mm.then_inc(sem("mod_cols"), 1)

        def mod_store(dve, l, c, v):
            n = mod_number[l, c, v]
            dve.wait_ge(*at("mod_cols", n + 1))
            nc.vector.tensor_tensor(MOD[:, l, 4 * c:4 * c + 4, v], view(bank[6], 0, 4, P)[:, :, 0],
                                    par("mod_b", 48 * l + 4 * c, 4), ALU.add).then_inc(sem("mod_stored"), 1)

        def mod_stored(dve, n):
            dve.wait_ge(*at("mod_stored", n))

        def coef_dve(l, which, m, col, g, plus):
            return nc.vector.scalar_tensor_tensor(COEF[:, l, which, :], MOD[:, l, 8 * m:8 * m + 8, col],
                                                  plus, par("norm_g", (4 * l + g) * KT, KT),
                                                  ALU.add, ALU.mult)

        def shift(l, m, col=0):
            return lambda j: MOD[:, l, 8 * m + j, col:col + 1]

        CTXB = view(BIG, 4096, KT, CTX)
        HCAT = view(HB, 0, KT, CTX + SEQ)
        H = view(HB, 0, KT, SEQ)

        QT = view(BIG, 0, HEADS, SEQ)
        KTT = view(BIG, 2048, 4, CTX + SEQ)
        VT = view(BIG, 4096, 4, 512)
        SQ = view(BIG, 6144, 4, 512)
        PROB = view(SCR, 0, 3, 512)
        PROT = view(SCR, 2048, P)
        MASK = view(SCR, 2560, 2, SEQ)
        PT = view(Y, 0, 4, SEQ)
        OT = view(HB, 0, HEADS, SEQ)
        normed = [KTT[:, 0, :], KTT[:, 1, :], view(BIG, 0, 512), view(BIG, 512, 512)]
        roped = [KTT[:, 0:2, CTX:], KTT[:, 2:4, CTX:]] + [QT[:, 2 * i:2 * i + 2, :] for i in range(4)]

        q_bank = [bank[i] for i in (4, 5, 7, 0, 1, 2, 3, 4)]
        v_bank = [bank[i] for i in (5, 7, 0, 1)]
        s_bank = [bank[i] for i in (4, 2, 3, 5)]
        rot_bank = [bank[i] for i in (7, 0)]

        def attn_pe(pe):
            pe.wait_ge(*at("n0x_out", KT))
            w = take(pe, "attn_in", 0)
            for n in range(4):
                for k in range(KT):
                    if n == 0:
                        pe.wait_ge(*at("n0c_out", k + 1))
                    mm = nc.tensor.matmul(bank[n][:, :], w[:, (n * KT + k) * P:(n * KT + k + 1) * P],
                                          HCAT[:, k, :], start=(k == 0), stop=(k == KT - 1))
                mm.then_inc(sem("qkv_tile"), 1)
            for n in range(HEADS):
                if n % 4 == 0:
                    w = take(pe, "attn_in", 1 + n // 4)
                if n >= 3:
                    pe.wait_ge(*at("qkv_read", n - 2))
                for k in range(KT):
                    b = (n % 4) * KT + k
                    mm = nc.tensor.matmul(q_bank[n][:, 0:SEQ], w[:, b * P:(b + 1) * P], HCAT[:, k, CTX:],
                                          start=(k == 0), stop=(k == KT - 1))
                mm.then_inc(sem("qkv_tile"), 1)
            w = take(pe, "attn_in", 3)
            for t in range(4):
                pe.wait_ge(*at("qkv_read", 6 + t))
                for k in range(KT):
                    mm = nc.tensor.matmul(v_bank[t][:, :], HCAT[:, k, t * P:(t + 1) * P],
                                          w[:, k * 512:(k + 1) * 512], start=(k == 0), stop=(k == KT - 1))
                mm.then_inc(sem("qkv_tile"), 1)
            for i in range(4):
                pe.wait_ge(*at("qk_sq", i + 1))
                if i == 0:
                    pe.wait_ge(*at("qkv_read", 13))
                nc.tensor.matmul(s_bank[i][:, :], ONES[:, :], SQ[:, i, :], start=True, stop=True)\
                    .then_inc(sem("qk_sum"), 1)
            for i in range(6):
                pe.wait_ge(*at("qk_normed", [2, 2, 3, 4, 4, 4][i]))
                if i < 2:
                    pe.wait_ge(*at("qkv_read", 16))
                else:
                    pe.wait_ge(*at("qk_roped", i - 1))
                nc.tensor.matmul(rot_bank[i % 2][:, :].rearrange("p (a b) -> p a b", a=2), PROT, roped[i],
                                 start=True, stop=True).then_inc(sem("qk_rot"), 1)

            def scores(u):
                h, q = u // 2, u % 2
                if u >= 3:
                    pe.wait_ge(*at("probs", u - 2))
                s = bank[u % 3]
                kv = h // 2
                nc_last = nc.tensor.matmul(s[:, :], QT[:, h, q * P:(q + 1) * P], KTT[:, kv, :],
                                           start=True, stop=(h < 4))
                if h >= 4:
                    nc_last = nc.tensor.matmul(s[:, CTX:], IDENT[:, :], MASK[:, q, :], start=False, stop=True)
                nc_last.then_inc(sem("scores"), 1)

            def turn(u):
                pe.wait_ge(*at("probs_normed", u + 1))
                if u >= 2:
                    pe.wait_ge(*at("turned_read", u - 1))
                for t in range(4):
                    mm = nc.tensor.transpose(bank[3 + u % 2][:, t * P:(t + 1) * P],
                                             PROB[:, u % 3, t * P:(t + 1) * P], IDENT[:, :])
                mm.then_inc(sem("turned"), 1)

            def values(h):
                pe.wait_ge(*at("turned_read", 2 * h + 2))
                if h >= 1:
                    pe.wait_ge(*at("heads_read", h))
                col = (h // 2) * P
                for t in range(4):
                    mm = nc.tensor.matmul(bank[5][:, 0:SEQ], VT[:, t, col:col + P],
                                          view(Y, (h % 2) * 1024, 4, SEQ)[:, t, :],
                                          start=(t == 0), stop=(t == 3))
                mm.then_inc(sem("heads"), 1)

            pe.wait_ge(*at("qk_roped", 6))
            for u in range(2 * HEADS + 3):
                if u < 2 * HEADS:
                    scores(u)
                if u % 2 == 1 and u >= 3:
                    mod_pe(pe, 0, 4 + (u - 3) // 2, 0)
                if 2 <= u < 2 * HEADS + 2:
                    turn(u - 2)
                if u >= 4 and u % 2 == 0:
                    values(u // 2 - 2)
            proj_pe(pe, "attn_out", "mix0", OT, SEQ, [0, 1, 2, 3], lambda: pe.wait_ge(*at("heads_read", HEADS)),
                    "n0y")

        def attn_act(act, link):
            for n in range(4):
                act.wait_ge(*at("qkv_tile", n + 1))
                nc.scalar.activation(KTT[:, n, :], bank[n][:, :], ACT.Copy).then_inc(sem("qkv_read"), 1)
            for n in range(HEADS):
                act.wait_ge(*at("qkv_tile", 5 + n))
                nc.scalar.activation(QT[:, n, :], q_bank[n][:, 0:SEQ], ACT.Copy).then_inc(sem("qkv_read"), 1)
            for t in range(4):
                act.wait_ge(*at("qkv_tile", 13 + t))
                nc.scalar.activation(VT[:, t, :], v_bank[t][:, :], ACT.Copy).then_inc(sem("qkv_read"), 1)
                act.wait_ge(*at("qkv_read", [1, 2, 6, 8][t]))
                nc.scalar.activation(SQ[:, t, :], normed[t], ACT.Square).then_inc(sem("qk_sq"), 1)
            for i in range(4):
                act.wait_ge(*at("qk_var", i + 1))
                nc.scalar.activation(view(Y, 512 * i, 512), view(Y, 512 * i, 512), ACT.Sqrt)\
                    .then_inc(sem("qk_std"), 1)

            def exps(u):
                h = u // 2
                act.wait_ge(*at("maxima", u + 1))
                if u >= 3:
                    act.wait_ge(*at("turned", u - 2))
                nc.scalar.activation(PROB[:, u % 3, :], bank[u % 3][:, :], ACT.Exp, bias=SM[:, 16 + u:17 + u],
                                     scale=SCALE, accum_out=SM[:, 32 + u:33 + u]).then_inc(sem("probs"), 1)
                if h >= 4:
                    nc.scalar.activation(SM[:, 48 + u - 8:49 + u - 8], par("sink", h - 4, 1), ACT.Exp,
                                         bias=SM[:, 16 + u:17 + u]).then_inc(sem("sinks"), 1)

            def turned(u):
                h, q = u // 2, u % 2
                act.wait_ge(*at("turned", u + 1))
                if h >= 2 and q == 0:
                    act.wait_ge(*at("heads", h - 1))
                nc.scalar.activation(view(Y, (h % 2) * 1024, 4, SEQ)[:, :, q * P:(q + 1) * P],
                                     view(bank[3 + u % 2], 0, 4, P), ACT.Copy).then_inc(sem("turned_read"), 1)

            def head(h):
                act.wait_ge(*at("heads", h + 1))
                nc.scalar.activation(OT[:, h, :], bank[5][:, 0:SEQ], ACT.Copy).then_inc(sem("heads_read"), 1)

            for u in range(2 * HEADS + 3):
                if u < 2 * HEADS:
                    exps(u)
                if 2 <= u < 2 * HEADS + 2:
                    turned(u - 2)
                if u >= 4 and u % 2 == 0:
                    head(u // 2 - 2)
            proj_act(act, "mix0", [0, 1, 2, 3], "n0y")

        def attn_dve(dve, link):
            for i in range(4):
                dve.wait_ge(*at("qk_sum", i + 1))
                nc.vector.tensor_scalar(view(Y, 512 * i, 512), s_bank[i][:, :], 1.0 / HD, EPS,
                                        ALU.mult, ALU.add).then_inc(sem("qk_var"), 1)
            for i in range(4):
                dve.wait_ge(*at("qk_std", i + 1))
                link(nc.vector.reciprocal(view(Y, 512 * i, 512), view(Y, 512 * i, 512)))
                nc.vector.scalar_tensor_tensor(normed[i], normed[i], par("kg" if i < 2 else "qg"),
                                               view(Y, 512 * i, 512), ALU.mult, ALU.mult)\
                    .then_inc(sem("qk_normed"), 1)
            dve.wait_ge(*at("qk_normed", 4))
            dve.wait_ge(*at("tables_in", 64))
            cos = ROPE[:, 0, :].unsqueeze(1).to_broadcast([P, 2, SEQ])
            sin = ROPE[:, 1, :].unsqueeze(1).to_broadcast([P, 2, SEQ])
            for i in range(6):
                dve.wait_ge(*at("qk_rot", i + 1))
                t = SQ[:, i % 2, :].rearrange("p (a b) -> p a b", a=2)
                nc.vector.tensor_tensor(t, rot_bank[i % 2][:, :].rearrange("p (a b) -> p a b", a=2), sin,
                                        ALU.mult)
                link(nc.vector.tensor_tensor(roped[i], roped[i], cos, ALU.mult))
                nc.vector.tensor_tensor(roped[i], roped[i], t, ALU.add).then_inc(sem("qk_roped"), 1)
            link(nc.vector.tensor_scalar(SM[:, 56:60], par("sink"), -1.0, None, ALU.mult))

            def maxima(u):
                h = u // 2
                dve.wait_ge(*at("scores", u + 1))
                link(nc.vector.reduce_max(SM[:, u:u + 1], bank[u % 3][:, :], AX.X))
                if h >= 4:
                    nc.vector.tensor_scalar(SM[:, 16 + u:17 + u], SM[:, u:u + 1], -SCALE, SM[:, 52 + h:53 + h],
                                            ALU.mult, ALU.min).then_inc(sem("maxima"), 1)
                else:
                    nc.vector.tensor_scalar(SM[:, 16 + u:17 + u], SM[:, u:u + 1], -SCALE, None, ALU.mult)\
                        .then_inc(sem("maxima"), 1)

            def norms(u):
                h = u // 2
                dve.wait_ge(*at("probs", u + 1))
                total = SM[:, 32 + u:33 + u]
                if h >= 4:
                    dve.wait_ge(*at("sinks", u - 7))
                    link(nc.vector.tensor_tensor(total, total, SM[:, 48 + u - 8:49 + u - 8], ALU.add))
                link(nc.vector.reciprocal(total, total))
                nc.vector.tensor_scalar(PROB[:, u % 3, :], PROB[:, u % 3, :], total, None, ALU.mult)\
                    .then_inc(sem("probs_normed"), 1)

            for u in range(2 * HEADS + 1):
                if u < 2 * HEADS:
                    maxima(u)
                if u >= 1:
                    norms(u - 1)
                if u % 2 == 1:
                    mod_sum(dve, 0, 4 + u // 2, 0)
                    if u >= 3:
                        mod_store(dve, 0, 3 + u // 2, 0)
            mod_store(dve, 0, 11, 0)
            mod_stored(dve, 16)
            coef_dve(0, 2, 2, 0, 1, 0.0)
            coef_dve(0, 3, 4, 0, 2, 1.0)
            link(coef_dve(0, 4, 5, 0, 3, 0.0))

        def conv_bank(j):
            return bank[j % 4]

        UT = view(SCR, 0, 2, 2, SEQ)
        SG = view(SCR, 1024, 2, SEQ)
        ACTB = view(BIG, 0, FF1T, SEQ)

        def ffn_pe(pe, l):
            p = f"ffn{l}"
            for j in range(FF1T):
                if j % PAIRS == 0:
                    w = take(pe, f"up{l}", j // PAIRS)
                if j >= 4:
                    pe.wait_ge(*at(p + "_conv", j - 3))
                for part in range(2):
                    for k in range(KT):
                        if j == 0 and part == 0:
                            pe.wait_ge(*at(f"n{l}f_out", k + 1))
                        b = ((j % PAIRS) * 2 + part) * KT + k
                        mm = nc.tensor.matmul(conv_bank(j)[:, part * SEQ:(part + 1) * SEQ],
                                              w[:, b * P:(b + 1) * P], H[:, k, :],
                                              start=(k == 0), stop=(k == KT - 1))
                mm.then_inc(sem(p + "_up"), 1)
                if l == 0 and j % PAIRS == 0 and j >= PAIRS:
                    mod_pe(pe, 1, j // PAIRS - 1, 0)
            for n in range(KT):
                if n >= 2:
                    pe.wait_ge(*at(p + "_read", n - 1))
                for k in range(FF1T):
                    b = n * FF1T + k
                    if b % BLK == 0:
                        w = take(pe, f"down{l}", b // BLK)
                    if n == 0:
                        pe.wait_ge(*at(p + "_act", k + 1))
                    b %= BLK
                    mm = nc.tensor.matmul(bank[4 + n % 2][:, 0:SEQ], w[:, b * P:(b + 1) * P], ACTB[:, k, :],
                                          start=(k == 0), stop=(k == FF1T - 1))
                mm.then_inc(sem(p + "_down"), 1)
                if n >= 1:
                    square_pe(pe, f"n{l}g", n - 1, SEQ, bank[7])
                if l == 0 and n < 2:
                    mod_pe(pe, 1, 10 + n, 0)
            square_pe(pe, f"n{l}g", KT - 1, SEQ, bank[7])

        def ffn_act(act, l):
            p = f"ffn{l}"
            for j in range(FF1T + 1):
                if j < FF1T:
                    act.wait_ge(*at(p + "_up", j + 1))
                    if j >= 2:
                        act.wait_ge(*at(p + "_act", j - 1))
                    for part in range(2):
                        f = part * FF1T + j
                        a = nc.scalar.activation(UT[:, j % 2, part, :], conv_bank(j)[:, part * SEQ:(part + 1) * SEQ],
                                                 ACT.Identity, bias=par(f"conv_b{l}", f, 1),
                                                 scale=par(f"conv_w{l}", 2 * FF1T + f, 1))
                    a.then_inc(sem(p + "_tap1"), 1)
                if j >= 1:
                    act.wait_ge(*at(p + "_conv", j))
                    nc.scalar.activation(SG[:, (j - 1) % 2, :], UT[:, (j - 1) % 2, 0, :], ACT.Silu)\
                        .then_inc(sem(p + "_silu"), 1)
            for n in range(KT):
                act.wait_ge(*at(p + "_down", n + 1))
                out_act(act, f"n{l}g", n, bank[4 + n % 2][:, 0:SEQ], p + "_read")
            root_act(act, f"n{l}g", SEQ)

        def ffn_dve(dve, l):
            p = f"ffn{l}"

            def conv(j):
                dve.wait_ge(*at(p + "_tap1", j + 1))
                for part in range(2):
                    f = part * FF1T + j
                    u = conv_bank(j)[:, part * SEQ:(part + 1) * SEQ]
                    t = UT[:, j % 2, part, :]
                    nc.vector.scalar_tensor_tensor(t[:, 1:SEQ], u[:, 0:SEQ - 1], par(f"conv_w{l}", f, 1),
                                                   t[:, 1:SEQ], ALU.mult, ALU.add).then_inc(sem(p + "_tap0"), 1)
                for part in range(2):
                    f = part * FF1T + j
                    u = conv_bank(j)[:, part * SEQ:(part + 1) * SEQ]
                    t = UT[:, j % 2, part, :]
                    dve.wait_ge(*at(p + "_tap0", 2 * j + part + 1))
                    a = nc.vector.scalar_tensor_tensor(t[:, 0:SEQ - 1], u[:, 1:SEQ],
                                                       par(f"conv_w{l}", 4 * FF1T + f, 1),
                                                       t[:, 0:SEQ - 1], ALU.mult, ALU.add)
                a.then_inc(sem(p + "_conv"), 1)

            for j in range(FF1T):
                conv(j)
                dve.wait_ge(*at(p + "_silu", j + 1))
                dve.wait_ge(*at(p + "_conv", j + 1))
                nc.vector.tensor_tensor(ACTB[:, j, :], SG[:, j % 2, :], UT[:, j % 2, 1, :], ALU.mult)\
                    .then_inc(sem(p + "_act"), 1)
                if l == 0 and j % PAIRS == 0:
                    c = j // PAIRS
                    mod_sum(dve, 1, c, 0)
                    if c >= 1:
                        mod_store(dve, 1, c - 1, 0)
            if l == 0:
                mod_sum(dve, 1, 11, 0)
                mod_store(dve, 1, 10, 0)
                mod_store(dve, 1, 11, 0)
                mod_stored(dve, len(mod_jobs))

        AB = view(BIG, 0, 2, 4, 512)
        DFTD = view(BIG, 4096, 2, 512)
        DFTL = view(BIG, 5120, 2, 2, SEQ)

        def four_pe(pe):
            pe.wait_ge(*at("dft_in", 32))
            for i in range(8):
                t, g = i // 4, i % 4
                pe.wait_ge(*at("n1x_out", 2 * g + 2 if t == 0 else KT))
                if i >= 4:
                    pe.wait_ge(*at("four_read", i - 3))
                for k in range(2):
                    mm = nc.tensor.matmul(bank[i % 4][:, :], H[:, 2 * g + k, t * P:(t + 1) * P], DFTD[:, k, :],
                                          start=(k == 0), stop=(k == 1))
                mm.then_inc(sem("four_ab"), 1)
            for f in range(KT):
                if f == 0:
                    pe.wait_ge(*at("four_read", 8))
                if f >= 2:
                    pe.wait_ge(*at("four_mixed", f - 1))
                g, half = f // 2, f % 2
                for i in range(4):
                    t, part = i // 2, i % 2
                    mm = nc.tensor.matmul(bank[4 + f % 2][:, 0:SEQ],
                                          AB[:, t, g, part * 256 + half * P:part * 256 + (half + 1) * P],
                                          DFTL[:, part, t, :], start=(i == 0), stop=(i == 3))
                mm.then_inc(sem("four_f"), 1)
            proj_pe(pe, "four_out", "mix1", H, SEQ, [0, 1, 2, 3], lambda: pe.wait_ge(*at("four_mixed", KT)),
                    "n1y")

        def four_act(act):
            for i in range(8):
                act.wait_ge(*at("four_ab", i + 1))
                nc.scalar.activation(AB[:, i // 4, i % 4, :], bank[i % 4][:, :], ACT.Copy)\
                    .then_inc(sem("four_read"), 1)
            for f in range(KT):
                act.wait_ge(*at("four_f", f + 1))
                nc.scalar.activation(H[:, f, :], bank[4 + f % 2][:, 0:SEQ], ACT.Copy)\
                    .then_inc(sem("four_mixed"), 1)
            proj_act(act, "mix1", [0, 1, 2, 3], "n1y")

        XC = view(BIG, 0, RGN, T2)
        RA = view(BIG, 4352, RGN, T2)
        RH = view(SCR, 0, RGN // 2, T2)
        RI = view(SCR, 2176, 2, T2)
        RW = view(Y, 0, RGN // 2, T2)
        LAM = SM
        XM = X[:, :, M0:TOK]

        def rg_pe(pe):
            pe.wait_ge(*at("meta_in", 16))
            w = None

            def proj(n):
                nonlocal w
                if n % 6 == 0:
                    w = take(pe, "rg_in", n // 6)
                if 4 <= n < RGN + 4:
                    pe.wait_ge(*at("rg_conv", n - 3))
                elif n >= 4:
                    pe.wait_ge(*at("rg_gelu", n - RGN - 3))
                for k in range(KT):
                    if n == 0:
                        pe.wait_ge(*at("n1g_res", k + 1))
                    o = ((n % 6) * KT + k) * RGT
                    mm = nc.tensor.matmul(bank[n % 4][0:RGT, 0:T2], w[:, o:o + RGT], XM[:, k, :],
                                          start=(k == 0), stop=(k == KT - 1))
                mm.then_inc(sem("rg_proj"), 1)

            for n in range(RGN):
                proj(n)
            w_keep = w
            for b in range(RGB):
                for i in range(4):
                    n = 4 * b + i
                    if n % 24 == 0:
                        wg = take(pe, "rg_gates", n // 24)
                    if n >= 4:
                        pe.wait_ge(*at("rg_gate_read", n - 3))
                    if i == 0:
                        pe.wait_ge(*at("rg_conv", 2 * b + 2))
                    for c in range(2):
                        o = ((n % 24) * 2 + c) * RGT
                        mm = nc.tensor.matmul(bank[4 + i][0:RGT, 0:T2], wg[0:RGT, o:o + RGT],
                                              XC[0:RGT, 2 * b + c, :], start=(c == 0), stop=(c == 1))
                    mm.then_inc(sem("rg_gate"), 1)
            w = w_keep
            for n in range(RGN, 2 * RGN):
                proj(n)
            for n in range(KT):
                if n % 2 == 0:
                    wo = take(pe, "rg_out", n // 2)
                if n >= 2:
                    pe.wait_ge(*at("mix2_read", n - 1))
                for k in range(RGN):
                    if n == 0:
                        pe.wait_ge(*at("rg_y", k + 1))
                    b = (n % 2) * RGN + k
                    mm = nc.tensor.matmul(bank[4 + n % 2][:, 0:T2], wo[0:RGT, b * P:(b + 1) * P],
                                          XC[0:RGT, k, :], start=(k == 0), stop=(k == RGN - 1))
                mm.then_inc(sem("mix2_tile"), 1)

        def rg_act(act):
            act.wait_ge(*at("lam_abs", 1))
            nc.scalar.activation(LAM[0:RGT, 16:32], LAM[0:RGT, 0:16], ACT.Exp, scale=-1.0)\
                .then_inc(sem("lam_exp"), 1)
            for n in range(RGN):
                act.wait_ge(*at("rg_proj", n + 1))
                nc.scalar.activation(XC[0:RGT, n, :], bank[n % 4][0:RGT, 0:T2], ACT.Identity,
                                     bias=par("rg_cb", n, 1)[0:RGT], scale=par("rg_conv", 3 * RGN + n, 1)[0:RGT])\
                    .then_inc(sem("rg_tap3"), 1)
            for half in range(2):
                for t in range(8):
                    n = 8 * half + t
                    act.wait_ge(*at("rg_gate", 4 * (n // 2) + 2 * (n % 2) + 2))
                    if half == 1 and t == 0:
                        act.wait_ge(*at("rg_w", 8))
                    nc.scalar.activation(RH[0:RGT, t, :], bank[4 + 2 * (n % 2)][0:RGT, 0:T2], ACT.Sigmoid,
                                         bias=par("rg_gb", n, 1)[0:RGT]).then_inc(sem("rg_gate_read"), 1)
                    if n >= 2:
                        act.wait_ge(*at("rg_ix", n - 1))
                    nc.scalar.activation(RI[0:RGT, n % 2, :], bank[5 + 2 * (n % 2)][0:RGT, 0:T2], ACT.Sigmoid,
                                         bias=par("rg_gb", RGN + n, 1)[0:RGT]).then_inc(sem("rg_gate_read"), 1)
                if half == 0:
                    act.wait_ge(*at("lam_ready", 1))
                act.wait_ge(*at("rg_gate_read", 16 * half + 16))
                if half == 1:
                    act.wait_ge(*at("rg_u", 1))
                for t in range(8):
                    n = 8 * half + t
                    nc.scalar.activation(RA[0:RGT, n, :], RH[0:RGT, t, :], ACT.Exp, scale=LAM[0:RGT, 32 + n:33 + n])\
                        .then_inc(sem("rg_a"), 1)
                    nc.scalar.activation(RW[0:RGT, t, :], RH[0:RGT, t, :], ACT.Exp, scale=LAM[0:RGT, 48 + n:49 + n])
                    nc.scalar.activation(RH[0:RGT, t, :], RH[0:RGT, t, :], ACT.Tanh, scale=LAM[0:RGT, 32 + n:33 + n])\
                        .then_inc(sem("rg_tanh"), 1)
                act.wait_ge(*at("rg_w", 8 * half + 8))
                nc.scalar.activation(RW[0:RGT, :, :], RW[0:RGT, :, :], ACT.Sqrt, scale=-1.0)\
                    .then_inc(sem("rg_root"), 1)
            for n in range(RGN):
                act.wait_ge(*at("rg_proj", RGN + n + 1))
                if n >= 2:
                    act.wait_ge(*at("rg_y", n - 1))
                nc.scalar.activation(RI[0:RGT, n % 2, :], bank[n % 4][0:RGT, 0:T2], ACT.Gelu_apprx_tanh)\
                    .then_inc(sem("rg_gelu"), 1)

        def rg_dve(dve, link):
            lam = par("rg_lam")[0:RGT]
            V = nc.vector
            z, s, q, acc = (LAM[0:RGT, i:i + 16] for i in (16, 0, 32, 48))
            link(V.tensor_scalar(q, lam, -1.0, None, ALU.mult))
            V.tensor_tensor(LAM[0:RGT, 0:16], lam, q, ALU.max).then_inc(sem("lam_abs"), 1)
            dve.wait_ge(*at("lam_exp", 1))
            link(V.tensor_scalar(acc, z, 2.0, None, ALU.add))
            link(V.reciprocal(acc, acc))
            link(V.tensor_tensor(s, z, acc, ALU.mult))
            link(V.tensor_tensor(q, s, s, ALU.mult))
            link(V.tensor_scalar(acc, q, 1.0 / 19, 1.0 / 17, ALU.mult, ALU.add))
            for m in (15, 13, 11, 9, 7, 5, 3, 1):
                link(V.tensor_tensor(acc, acc, q, ALU.mult))
                link(V.tensor_scalar(acc, acc, 1.0 / m, None, ALU.add))
            link(V.tensor_tensor(acc, acc, s, ALU.mult))
            link(V.tensor_scalar(q, lam, -1.0, 0.0, ALU.mult, ALU.max))
            link(V.scalar_tensor_tensor(acc, acc, 2.0, q, ALU.mult, ALU.add))
            link(V.tensor_scalar(q, acc, -8.0, None, ALU.mult))
            V.tensor_scalar(acc, q, 2.0, None, ALU.mult).then_inc(sem("lam_ready"), 1)
            for n in range(RGN):
                dve.wait_ge(*at("rg_tap3", n + 1))
                for lag in (1, 2, 3):
                    a = V.scalar_tensor_tensor(XC[0:RGT, n, lag:T2], bank[n % 4][0:RGT, 0:T2 - lag],
                                               par("rg_conv", (3 - lag) * RGN + n, 1)[0:RGT],
                                               XC[0:RGT, n, lag:T2], ALU.mult, ALU.add)
                    if lag < 3:
                        link(a)
                    else:
                        a.then_inc(sem("rg_conv"), 1)
            for half in range(2):
                for t in range(8):
                    n = 8 * half + t
                    dve.wait_ge(*at("rg_gate_read", 2 * n + 2))
                    dve.wait_ge(*at("rg_gate", 4 * (n // 2) + 4))
                    V.tensor_tensor(XC[0:RGT, n, :], XC[0:RGT, n, :], RI[0:RGT, n % 2, :], ALU.mult)\
                        .then_inc(sem("rg_ix"), 1)
                for t in range(8):
                    n = 8 * half + t
                    dve.wait_ge(*at("rg_tanh", n + 1))
                    V.scalar_tensor_tensor(RW[0:RGT, t, :], RW[0:RGT, t, :], 1.0, RH[0:RGT, t, :],
                                           ALU.add, ALU.mult).then_inc(sem("rg_w"), 1)
                dve.wait_ge(*at("rg_root", half + 1))
                dve.wait_ge(*at("rg_ix", 8 * half + 8))
                u = XC[0:RGT, 8 * half:8 * half + 8, :]
                V.tensor_tensor(u, u, RW[0:RGT, :, :], ALU.mult).then_inc(sem("rg_u"), 1)
                dve.wait_ge(*at("rg_u", half + 1))
                for t in range(8):
                    n = 8 * half + t
                    V.tensor_tensor_scan(XC[0:RGT, n, :], RA[0:RGT, n, :], XC[0:RGT, n, :], 0.0,
                                         ALU.mult, ALU.add).then_inc(sem("rg_h"), 1)
            for n in range(RGN):
                dve.wait_ge(*at("rg_gelu", n + 1))
                dve.wait_ge(*at("rg_h", n + 1))
                V.tensor_tensor(XC[0:RGT, n, :], XC[0:RGT, n, :], RI[0:RGT, n % 2, :], ALU.mult)\
                    .then_inc(sem("rg_y"), 1)
            add_dve(dve, "mix2", M0, T2, [4, 5])

        SA = view(SCR, 0, 2, T2)
        ACT2 = view(BIG, 0, FF2T, T2)

        def swiglu_pe(pe):
            for j in range(FF2T):
                if j % PAIRS == 0:
                    w = take(pe, "ffn_in", j // PAIRS)
                if j >= 3:
                    pe.wait_ge(*at("ffn2_act", j - 2))
                for part in range(2):
                    for k in range(KT):
                        if j == 0 and part == 0:
                            pe.wait_ge(*at("ln0_out", k + 1))
                        b = ((j % PAIRS) * 2 + part) * KT + k
                        mm = nc.tensor.matmul(bank[2 * (j % 3) + part][:, 0:T2], w[:, b * P:(b + 1) * P],
                                              XM[:, k, :], start=(k == 0), stop=(k == KT - 1))
                mm.then_inc(sem("ffn2_up"), 1)
            for n in range(KT):
                if n >= 2:
                    pe.wait_ge(*at("ffn2_read", n - 1))
                for k in range(FF2T):
                    b = n * FF2T + k
                    if b % BLK == 0:
                        w = take(pe, "ffn_out", b // BLK)
                    if n == 0:
                        pe.wait_ge(*at("ffn2_act", k + 1))
                    b %= BLK
                    mm = nc.tensor.matmul(bank[6 + n % 2][:, 0:T2], w[:, b * P:(b + 1) * P], ACT2[:, k, :],
                                          start=(k == 0), stop=(k == FF2T - 1))
                mm.then_inc(sem("ffn2_down"), 1)

        def swiglu_act(act):
            for j in range(FF2T):
                act.wait_ge(*at("ffn2_up", j + 1))
                if j >= 2:
                    act.wait_ge(*at("ffn2_act", j - 1))
                nc.scalar.activation(SA[:, j % 2, :], bank[2 * (j % 3)][:, 0:T2], ACT.Silu)\
                    .then_inc(sem("ffn2_silu"), 1)

        def swiglu_dve(dve):
            for j in range(FF2T):
                dve.wait_ge(*at("ffn2_silu", j + 1))
                nc.vector.tensor_tensor(ACT2[:, j, :], SA[:, j % 2, :], bank[2 * (j % 3) + 1][:, 0:T2], ALU.mult)\
                    .then_inc(sem("ffn2_act"), 1)
            add_dve(dve, "ffn2", M0, T2, [6, 7], "_down")

        GQ, GK, GB, GQ1, GK1 = (view(BIG, GH * TOK * i, GH, TOK) for i in range(5))
        GKT = view(BIG, 6400, 2, GH, P)
        GS = view(BIG, 7424, GH, GDV)
        GD, GE = (view(Y, GH * TOK * i, GH, TOK) for i in range(2))
        GO = view(Y, 0, KT, SEQ)
        GV = view(SCR, 0, 3, D)
        GSC = view(HB, 0, 2, GH, GCH)
        GZ = view(HB, 512, TOK)
        GSQ = view(BIG, 0, KT, SEQ)
        GR = view(BIG, GH * TOK * 3, KT, SEQ)
        GDEC = view(HB, 1536, GH, NCH)
        GST = view(HB, 2048, GH, SEQ)

        def flat(v):
            return v.rearrange("p a b -> p (a b)")

        def chunks(v):
            return flat(v).rearrange("p (n c) -> p n c", c=GCH)

        def at_chunk(v, i):
            return chunks(v)[:, :, i:i + 1].to_broadcast([P, GH * NCH, GCH])

        def gla_pe(pe):
            for i in range(8):
                if i % 4 == 0:
                    w = take(pe, "gla_in", i // 4)
                if i >= 4:
                    pe.wait_ge(*at("gla_read", i - 3))
                for k in range(KT):
                    if i == 0:
                        pe.wait_ge(*at("ln1_out", k + 1))
                    b = (i % 4) * KT + k
                    mm = nc.tensor.matmul(bank[i % 4][:, 0:TOK], w[:, b * P:(b + 1) * P], X[:, k, :],
                                          start=(k == 0), stop=(k == KT - 1))
                mm.then_inc(sem("gla_proj"), 1)
            for k in range(KT):
                mm = nc.tensor.matmul(bank[4][0:16, 0:TOK], par("gla_wz", 16 * k, 16), X[:, k, :],
                                      start=(k == 0), stop=(k == KT - 1))
            mm.then_inc(sem("gla_z"), 1)
            pe.wait_ge(*at("gla_z_read", 1))
            for h in range(GH):
                if h == 0:
                    pe.wait_ge(*at("gla_read", 8))
                nc.tensor.matmul(bank[h][:, 0:TOK], par("gla_wg", P * h, P)[0:16], GZ[0:16, :],
                                 start=True, stop=True).then_inc(sem("gla_g"), 1)
            v = 0
            for half in range(2):
                w = take(pe, "gla_in", 2 + half)
                for t in range(3):
                    n = P if t < 2 else GCH
                    if v >= 2:
                        pe.wait_ge(*at("gla_v_read", v - 1))
                    for k in range(KT):
                        mm = nc.tensor.matmul(bank[5 + v % 2][0:n, :], X[:, k, t * P:t * P + n],
                                              w[:, k * 512:(k + 1) * 512], start=(k == 0), stop=(k == KT - 1))
                    v += 1
                    mm.then_inc(sem("gla_v"), 1)
            pe.wait_ge(*at("gla_scaled", 4))
            for c in range(1, NCH):
                lo, slot = (c % 2) * GCH, (c - 1) // 2
                for h in range(GH):
                    mm = nc.tensor.matmul(bank[7][lo:lo + GCH, slot * 256 + h * GCH:slot * 256 + (h + 1) * GCH],
                                          GK1[:, h, c * GCH:(c + 1) * GCH], GQ1[:, h, c * GCH:(c + 1) * GCH],
                                          start=True, stop=True)
            mm.then_inc(sem("gla_scores"), 1)
            for t in range(2):
                for h in range(GH):
                    mm = nc.tensor.transpose(bank[4 if t else 0][:, h * P:(h + 1) * P],
                                             GK[:, h, t * P:(t + 1) * P], IDENT[:, :])
                mm.then_inc(sem("gla_kt"), 1)
            pe.wait_ge(*at("gla_kt_read", 2))
            pe.wait_ge(*at("gla_v_read", 6))
            pe.wait_ge(*at("gla_masked", 2))

            def gate(i):
                w = take(pe, "gla_in", 4 + i // 4)
                if i >= 2:
                    pe.wait_ge(*at("gla_r_read", i - 1))
                for k in range(KT):
                    b = (i % 4) * KT + k
                    mm = nc.tensor.matmul(bank[[1, 6][i % 2]][:, 0:SEQ], w[:, b * P:(b + 1) * P], xs[:, k, :],
                                          start=(k == 0), stop=(k == KT - 1))
                mm.then_inc(sem("gla_r"), 1)

            for c in range(NCH):
                lo, slot, t = (c % 2) * GCH, (c - 1) // 2, c // 2
                if c >= 1:
                    gate(2 * c - 2)
                    pe.wait_ge(*at("gla_state", GH * c))
                    if c >= 2:
                        pe.wait_ge(*at("gla_o_read", c - 1))
                    for h in range(GH):
                        for e in range(2):
                            i = 2 * h + e
                            o = bank[0][:, i * GCH:(i + 1) * GCH]
                            nc.tensor.matmul(o, GV[lo:lo + GCH, t, i * P:(i + 1) * P], GSC[lo:lo + GCH, slot, h, :],
                                             start=True, stop=False)
                            mm = nc.tensor.matmul(o, GS[:, h, e * P:(e + 1) * P], GQ[:, h, c * GCH:(c + 1) * GCH],
                                                  start=False, stop=True)
                    mm.then_inc(sem("gla_o"), 1)
                if c < NCH - 1:
                    for h in range(GH):
                        mm = nc.tensor.matmul(bank[2 + h // 2][:, (h % 2) * GDV:(h % 2 + 1) * GDV],
                                              GKT[lo:lo + GCH, t, h, :],
                                              GV[lo:lo + GCH, t, h * GDV:(h + 1) * GDV], start=True, stop=True)
                    mm.then_inc(sem("gla_kv"), 1)
                if c >= 1:
                    gate(2 * c - 1)
            pe.wait_ge(*at("gla_o_read", NCH - 1))
            for h in range(GH):
                for e in range(2):
                    mm = nc.tensor.matmul(bank[4 + h // 2][:, (h % 2) * SEQ:(h % 2 + 1) * SEQ], ONES[:, :],
                                          GO[:, 2 * h + e, :], start=(e == 0), stop=(e == 1))
            mm.then_inc(sem("gla_mean"), 1)
            pe.wait_ge(*at("gla_r_read", 8))
            for h in range(GH):
                if h % 2 == 0:
                    pe.wait_ge(*at("gla_sq", h // 2 + 1))
                for e in range(2):
                    mm = nc.tensor.matmul(bank[6 + h // 2][:, (h % 2) * SEQ:(h % 2 + 1) * SEQ], ONES[:, :],
                                          GSQ[:, 2 * h + e, :], start=(e == 0), stop=(e == 1))
            mm.then_inc(sem("gla_sum"), 1)
            proj_pe(pe, "gla_out", "mix3", GO, SEQ, [2, 3], lambda: pe.wait_ge(*at("gla_gated", KT)))

        def gla_act(act):
            for i in range(8):
                act.wait_ge(*at("gla_proj", i + 1))
                if i < GH:
                    nc.scalar.activation(GQ[:, i, :], bank[i % 4][:, 0:TOK], ACT.Copy, scale=SCALE)\
                        .then_inc(sem("gla_read"), 1)
                else:
                    nc.scalar.activation(GK[:, i - GH, :], bank[i % 4][:, 0:TOK], ACT.Copy)\
                        .then_inc(sem("gla_read"), 1)
            act.wait_ge(*at("gla_z", 1))
            nc.scalar.activation(GZ[0:16, :], bank[4][0:16, 0:TOK], ACT.Copy).then_inc(sem("gla_z_read"), 1)
            for h in range(GH):
                act.wait_ge(*at("gla_g", h + 1))
                nc.scalar.activation(GE[:, h, :], bank[h][:, 0:TOK], ACT.Identity, bias=par("gla_bg", h, 1))\
                    .then_inc(sem("gla_x"), 1)
            act.wait_ge(*at("gla_x", GH))
            nc.scalar.activation(flat(GD), flat(GE), ACT.Abs).then_inc(sem("gla_x"), 1)
            act.wait_ge(*at("gla_x", GH + 1))
            nc.scalar.activation(flat(GD), flat(GD), ACT.Exp, scale=-1.0).then_inc(sem("gla_x"), 1)
            act.wait_ge(*at("gla_x", GH + 2))
            nc.scalar.activation(flat(GD), flat(GD), ACT.Ln, bias=1.0).then_inc(sem("gla_x"), 1)
            for v in range(6):
                act.wait_ge(*at("gla_v", v + 1))
                half, t = v // 3, v % 3
                n = P if t < 2 else GCH
                nc.scalar.activation(GV[0:n, t, half * 512:(half + 1) * 512], bank[5 + v % 2][0:n, :], ACT.Copy)\
                    .then_inc(sem("gla_v_read"), 1)
                if 1 <= v < 5:
                    i = v - 1
                    src, scale = [(GD, 1 / 16), (GD, -1 / 16), (GB, 1 / 16), (GD, 1 / 16)][i]
                    act.wait_ge(*at("gla_diff", [1, 1, 1, 2][i]))
                    if i >= 1:
                        act.wait_ge(*at("gla_scaled", i))
                    nc.scalar.activation(flat(GE), flat(src), ACT.Exp, scale=scale).then_inc(sem("gla_exp"), 1)
            last = chunks(GB)[:, :, GCH - 1]
            nc.scalar.activation(flat(GDEC), last, ACT.Exp, scale=1 / 16).then_inc(sem("gla_decay"), 1)
            act.wait_ge(*at("gla_scores", 1))
            nc.scalar.activation(view(HB, 0, 512), bank[7][:, :], ACT.Copy).then_inc(sem("gla_sc"), 1)
            for t in range(2):
                act.wait_ge(*at("gla_kt", t + 1))
                nc.scalar.activation(view(BIG, 6400 + 512 * t, 512), bank[4 if t else 0][:, :], ACT.Copy)\
                    .then_inc(sem("gla_kt_read"), 1)

            def gate(i):
                act.wait_ge(*at("gla_r", i + 1))
                nc.scalar.activation(GR[:, i, :], bank[[1, 6][i % 2]][:, 0:SEQ], ACT.Silu)\
                    .then_inc(sem("gla_r_read"), 1)

            for c in range(1, NCH):
                gate(2 * c - 2)
                act.wait_ge(*at("gla_o", c))
                nc.scalar.activation(GO[:, :, (c - 1) * GCH:c * GCH], view(bank[0], 0, KT, GCH), ACT.Copy)\
                    .then_inc(sem("gla_o_read"), 1)
                gate(2 * c - 1)
            for s in range(2):
                act.wait_ge(*at("gla_centred", 2 * s + 2))
                nc.scalar.activation(GSQ[:, 4 * s:4 * s + 4, :], GO[:, 4 * s:4 * s + 4, :], ACT.Square)\
                    .then_inc(sem("gla_sq"), 1)
            act.wait_ge(*at("gla_var", 2))
            nc.scalar.activation(flat(GST), flat(GST), ACT.Sqrt).then_inc(sem("gla_std"), 1)

        def gla_pool(pool):
            pool.wait_ge(*at("gla_sc", 1))
            for lo in (0, GCH):
                s = view(HB, 0, 8, GCH)[lo:lo + GCH]
                nc.gpsimd.affine_select(out=s, in_=s, compare_op=ALU.is_ge, fill=0.0, base=0,
                                        pattern=[[0, 8], [1, GCH]], channel_multiplier=-1)\
                    .then_inc(sem("gla_masked"), 1)

        def gla_dve(dve, link):
            V = nc.vector
            dve.wait_ge(*at("gla_x", GH + 3))
            link(V.scalar_tensor_tensor(flat(GE), flat(GE), 0.0, flat(GD), ALU.min, ALU.subtract))
            link(V.memset(GE[:, :, 0:PADT], 0.0))
            link(V.memset(flat(GD), 1.0))
            link(V.memset(chunks(GD)[:, :, 0:1], 0.0))
            link(V.tensor_tensor_scan(flat(GB), flat(GD), flat(GE), 0.0, ALU.mult, ALU.add))
            V.tensor_tensor(chunks(GD), chunks(GB), at_chunk(GB, GCH // 2 - 1), ALU.subtract)\
                .then_inc(sem("gla_diff"), 1)
            dve.wait_ge(*at("gla_read", 8))
            for i, (dst, src) in enumerate([(GQ1, GQ), (GK1, GK), (GQ, GQ), (GK, GK)]):
                dve.wait_ge(*at("gla_exp", i + 1))
                if i == 2:
                    V.tensor_tensor(chunks(GD), at_chunk(GB, GCH - 1), chunks(GB), ALU.subtract)\
                        .then_inc(sem("gla_diff"), 1)
                V.tensor_tensor(flat(dst), flat(src), flat(GE), ALU.mult).then_inc(sem("gla_scaled"), 1)
            dve.wait_ge(*at("gla_decay", 1))
            for c in range(NCH - 1):
                dve.wait_ge(*at("gla_kv", c + 1))
                if c >= 1:
                    dve.wait_ge(*at("gla_state", GH * c))
                for h in range(GH):
                    kv = bank[2 + h // 2][:, (h % 2) * GDV:(h % 2 + 1) * GDV]
                    if c == 0:
                        V.tensor_copy(GS[:, h, :], kv).then_inc(sem("gla_state"), 1)
                    else:
                        V.scalar_tensor_tensor(GS[:, h, :], GS[:, h, :], GDEC[:, h, c:c + 1], kv,
                                               ALU.mult, ALU.add).then_inc(sem("gla_state"), 1)
            dve.wait_ge(*at("gla_mean", 1))
            for h in range(GH):
                mean = bank[4 + h // 2][:, (h % 2) * SEQ:(h % 2 + 1) * SEQ].unsqueeze(1).to_broadcast([P, 2, SEQ])
                oh = GO[:, 2 * h:2 * h + 2, :]
                V.scalar_tensor_tensor(oh, mean, -1.0 / GDV, oh, ALU.mult, ALU.add)\
                    .then_inc(sem("gla_centred"), 1)
            dve.wait_ge(*at("gla_sum", 1))
            for s in range(2):
                V.tensor_scalar(view(HB, 2048 + 512 * s, 512), bank[6 + s][:, :], 1.0 / GDV, LN_EPS,
                                ALU.mult, ALU.add).then_inc(sem("gla_var"), 1)
            dve.wait_ge(*at("gla_std", 1))
            link(V.reciprocal(flat(GST), flat(GST)))
            dve.wait_ge(*at("gla_centred", 4))
            for i in range(8):
                link(V.scalar_tensor_tensor(GO[:, i, :], GO[:, i, :], par("gla_ng", i, 1), GST[:, i // 2, :],
                                            ALU.mult, ALU.mult))
            dve.wait_ge(*at("gla_r_read", 8))
            for i in range(8):
                V.tensor_tensor(GO[:, i, :], GO[:, i, :], GR[:, i, :], ALU.mult)\
                    .then_inc(sem("gla_gated"), 1)
            add_dve(dve, "mix3", X0, SEQ, [2, 3])

        XTOK = view(BIG, 0, 2, D)
        YS = view(BIG, 2048, D)
        YACC = view(Y, 0, KT, SEQ)
        GW = view(HB, 0, SEQ)
        SEL = view(HB, 256, 2, P)
        SELG = view(HB, 512, 2, P)
        IOTA = view(HB, 768, P)
        SILU = view(HB, 896, 2, 256)
        AS = view(HB, 1408, 2, 256)
        PICK = view(SCR, 1024, 3072 - 1024)
        POS = view(SCR, 1024, 2, 16)
        GATE = view(SCR, 1056, 2, 16)
        U1, U2 = view(SCR, 0, 8, 8), view(SCR, 64, 8, 8)
        LT = view(SCR, 128, 8, 8)
        LG, EX, RK, PM, CN, OV, PX = (view(SCR, 192 + 16 * i, 2, 8) for i in range(7))
        SML = view(SCR, 320, 64)
        TRI = view(SCR, 512, P)
        ITAB = sb("ITAB", [1, 16], I32)
        FTAB = view(SCR, 384, 16)
        M3 = view(SCR, 448, 3, 8)
        IOE = view(SCR, 480, 8)

        def count(eng):
            return eng.value_load(ITAB[0:1, 12:13], min_val=NE, max_val=ITEMS)

        slot0 = MOE0 % RING
        came = [16 * sum(1 for e in plan if e[1] == s) for s in range(RING)]

        def arrival(i, q):
            slot = (slot0 + q) % RING
            return f"weights_in{slot}", i * (16 * MOE_CH // RING) + (came[slot] + 16 * (q // RING + 1)), slot

        def moe_sync(sp, previous):
            src = A["moe"]
            for q in range(MOE_CH):
                name, _, slot = arrival(0, q)
                if q < RING:
                    sp.wait_ge(*at(previous[slot][0], previous[slot][1]))
                else:
                    sp.wait_ge(*at("moe_lo", 2 * (q - RING) + 2))
                sp.dma_start(ring[:, slot, :], src[q, :, :]).then_inc(sem(name), 16)

            def first(e, after):
                name, _, slot = arrival(0, 0)
                chunk = src[bass.ds(e * MOE_CH, 1), :, :].rearrange("a p n -> p (a n)")
                sp.wait_ge(*at("moe_lo", after))
                sp.dma_start(ring[:, slot, :], chunk).then_inc(sem(name), 16)

            first(1, HALVES + 2 - 2 * RING)
            sp.wait_ge(*at("items_ready", 1))
            n = count(sp)
            with sp.Fori(1, n) as i:
                e = sp.value_load(ITAB[0:1, bass.ds(i, 1)], min_val=0, max_val=NE - 1)
                for q in range(1, MOE_CH):
                    name, _, slot = arrival(0, q)
                    chunk = src[bass.ds(e * MOE_CH + q, 1), :, :].rearrange("a p n -> p (a n)")
                    sp.wait_ge(*at("moe_lo", HALVES * i + (2 * (q - RING) + 2)))
                    sp.dma_start(ring[:, slot, :], chunk).then_inc(sem(name), 16)
                e_next = sp.value_load(ITAB[0:1, bass.ds(i + 1, 1)], min_val=0, max_val=NE - 1)
                first(e_next, HALVES * i + (HALVES + 2 - 2 * RING))

        def moe_pe(pe):
            pe.wait_ge(*at("ln2_out", KT))
            for t in range(2):
                for k in range(KT):
                    mm = nc.tensor.matmul(bank[4][:, 8 * t:8 * t + 8], xs[:, k, t * P:(t + 1) * P],
                                          par("router", NE * k, NE), start=(k == 0), stop=(k == KT - 1))
            mm.then_inc(sem("moe_logits"), 1)
            for i in range(4):
                t, q = i // 2, i % 2
                for f in range(4):
                    mm = nc.tensor.transpose(bank[i][:, f * P:(f + 1) * P],
                                             xs[:, 4 * q + f, t * P:(t + 1) * P], IDENT[:, :])
                mm.then_inc(sem("moe_xt"), 1)
            pe.wait_ge(*at("moe_picked", 1))
            nc.tensor.matmul(bank[5][:, 0:8], TRI, RK[:, 0, :], start=True, stop=True)
            nc.tensor.matmul(bank[5][:, 8:16], TRI, RK[:, 1, :], start=True, stop=False)
            nc.tensor.matmul(bank[5][:, 8:16], ONES[:, :], RK[:, 0, :], start=False, stop=True)
            nc.tensor.matmul(bank[5][:, 16:24], ONES[:, :], RK[:, 0, :], start=True, stop=False)
            nc.tensor.matmul(bank[5][:, 16:24], ONES[:, :], RK[:, 1, :], start=False, stop=True)\
                .then_inc(sem("moe_before"), 1)

            def gather(i):
                pe.wait_ge(*at("moe_sel", i + 1))
                for f in range(KT):
                    for t in range(2):
                        mm = nc.tensor.matmul(bank[f // 4][:, (f % 4) * P:(f % 4 + 1) * P],
                                              XTOK[:, t, f * P:(f + 1) * P], SEL[:, t, :],
                                              start=(t == 0), stop=(t == 1))
                    if f % 4 == 3:
                        mm.then_inc(sem("moe_gathered"), 1)

            pe.wait_ge(*at("moe_xt_read", 4))
            gather(0)
            pe.wait_ge(*at("items_ready", 1))
            n = count(pe)
            def halves(i, h, products):
                pe.wait_ge(*at("moe_lo", HALVES * i + (h + 1)))
                for out, (xh, xl), o, start, stop in products:
                    wh, wl = WHI[:, h % SPLIT, o:o + 512], WLO[:, h % SPLIT, o:o + 512]
                    nc.tensor.matmul(out, xh, wh, start=start, stop=False)
                    nc.tensor.matmul(out, xh, wl, start=False, stop=False)
                    mm = nc.tensor.matmul(out, xl, wh, start=False, stop=stop)
                mm.then_inc(sem("moe_half"), 1)

            with pe.Fori(0, n) as i:
                def turn(c):
                    pe.wait_ge(*at("moe_act", MOE_UP * i + (c + 1)))
                    if c >= 2:
                        pe.wait_ge(*at("moe_alo", MOE_UP * i + (c - 1)))
                    else:
                        pe.wait_ge(*at("moe_added", 4 * i + 4))
                    for q in range(2):
                        mm = nc.tensor.transpose(bank[3 + c % 2][:, q * P:(q + 1) * P],
                                                 AS[:, c % 2, q * P:(q + 1) * P], IDENT[:, :])
                    mm.then_inc(sem("moe_turned"), 1)

                pe.wait_ge(*at("moe_hgl", 2 * i + 2))
                for q, (kind, c) in enumerate(MOE_ORDER):
                    if kind == "up":
                        if c >= 2:
                            pe.wait_ge(*at("moe_act", MOE_UP * i + (c - 1)))
                        for h in range(2):
                            ks = range(4 * h, 4 * h + 4)
                            halves(i, 2 * q + h, [(bank[c % 2][:, :], (HGH[:, k, :], HGL[:, k, :]), (k % 4) * 512,
                                                   k == 0, k == KT - 1) for k in ks])
                        if c >= 1:
                            turn(c - 1)
                        continue
                    if c == MOE_DOWN - 1:
                        for t in range(2):
                            mm = nc.tensor.transpose(bank[2][:, t * P:(t + 1) * P], SELG[:, t, :], IDENT[:, :])
                        mm.then_inc(sem("moe_gt"), 1)
                        turn(MOE_UP - 1)
                    pe.wait_ge(*at("moe_alo", MOE_UP * i + 2 * (c + 1)))
                    for h in range(2):
                        halves(i, 2 * q + h, [
                            (bank[6 + n2][:, :], (AHI[:, c % 2, 2 * h + k, :], ALO[:, c % 2, 2 * h + k, :]),
                             k * D + n2 * 512, c == 0 and h == 0 and k == 0,
                             c == MOE_DOWN - 1 and h == 1 and k == 1) for k in range(2) for n2 in range(2)])
                gather(i + 1)
                pe.wait_ge(*at("moe_gw", i + 1))
                pe.wait_ge(*at("moe_ys", 2 * i + 2))
                for f in range(KT):
                    mm = nc.tensor.matmul(bank[2 + f // 2][:, (f % 2) * SEQ:(f % 2 + 1) * SEQ],
                                          YS[:, f * P:(f + 1) * P], GW, start=True, stop=True)
                    if f % 2 == 1:
                        mm.then_inc(sem("moe_spread"), 1)

        def moe_act(act):
            act.wait_ge(*at("moe_max", 1))
            nc.scalar.activation(view(SCR, 208, 16), view(SCR, 208, 16), ACT.Exp).then_inc(sem("moe_exp"), 1)
            for i in range(4):
                act.wait_ge(*at("moe_xt", i + 1))
                nc.scalar.activation(XTOK[:, i // 2, (i % 2) * 512:(i % 2 + 1) * 512], bank[i][:, :], ACT.Copy)\
                    .then_inc(sem("moe_xt_read"), 1)

            def gathered(i):
                for b in range(2):
                    act.wait_ge(*at("moe_gathered", 2 * i + (b + 1)))
                    nc.scalar.activation(flat(HGH[:, 4 * b:4 * b + 4, :]), bank[b][:, :], ACT.Copy)\
                        .then_inc(sem("moe_hgh"), 1)

            def high(i, h):
                name, value, slot = arrival(i, h // 2)
                if h % 2 == 0:
                    act.wait_ge(*at(name, value))
                if h > 2:
                    act.wait_ge(*at("moe_half", HALVES * i + (h - 2)))
                nc.scalar.activation(WHI[:, h % SPLIT, :], ring[:, slot, (h % 2) * HALF:(h % 2 + 1) * HALF],
                                     ACT.Copy).then_inc(sem("moe_hi"), 1)

            high(0, 0)
            high(0, 1)
            gathered(0)
            act.wait_ge(*at("items_ready", 1))
            n = count(act)
            with act.Fori(0, n) as i:
                def turned(c):
                    act.wait_ge(*at("moe_turned", MOE_UP * i + (c + 1)))
                    nc.scalar.activation(flat(AHI[:, (c // 2) % 2, 2 * (c % 2):2 * (c % 2) + 2, :]),
                                         bank[3 + c % 2][:, 0:2 * P], ACT.Copy).then_inc(sem("moe_ahi"), 1)

                for q, (kind, c) in enumerate(MOE_ORDER):
                    if (kind, c) == ("down", MOE_DOWN - 1):
                        act.wait_ge(*at("moe_gt", i + 1))
                        nc.scalar.activation(GW, bank[2][:, 0:SEQ], ACT.Copy).then_inc(sem("moe_gw"), 1)
                        turned(MOE_UP - 1)
                    high(i, 2 * q + 2)
                    high(i, 2 * q + 3)
                    if kind == "up":
                        act.wait_ge(*at("moe_half", HALVES * i + (2 * q + 2)))
                        if c >= 2:
                            act.wait_ge(*at("moe_act", MOE_UP * i + (c - 1)))
                        nc.scalar.activation(SILU[:, c % 2, :], bank[c % 2][:, 0:256], ACT.Silu)\
                            .then_inc(sem("moe_silu"), 1)
                        if c >= 1:
                            turned(c - 1)
                act.wait_ge(*at("moe_half", HALVES * i + HALVES))
                for half in range(2):
                    nc.scalar.activation(YS[:, half * 512:(half + 1) * 512], bank[6 + half][:, :], ACT.Copy)\
                        .then_inc(sem("moe_ys"), 1)
                gathered(i + 1)

        def moe_pool(pool):
            pool.wait_ge(*at("ln2_out", KT))
            nc.gpsimd.memset(TRI, 1.0).then_inc(sem("moe_const"), 1)
            nc.gpsimd.memset(flat(LT), 1.0).then_inc(sem("moe_const"), 1)
            pool.wait_ge(*at("moe_const", 2))
            nc.gpsimd.affine_select(out=TRI, in_=TRI, compare_op=ALU.is_gt, fill=0.0, base=0,
                                    pattern=[[1, P]], channel_multiplier=-1).then_inc(sem("moe_const"), 1)
            nc.gpsimd.affine_select(out=LT, in_=LT, compare_op=ALU.is_gt, fill=0.0, base=0,
                                    pattern=[[1, 8], [-1, 8]], channel_multiplier=0).then_inc(sem("moe_const"), 1)
            nc.gpsimd.iota(IOTA, [[1, P]], base=0, channel_multiplier=0,
                           allow_small_or_imprecise_dtypes=True).then_inc(sem("moe_const"), 1)
            nc.gpsimd.iota(IOE, [[1, 8]], base=0, channel_multiplier=0,
                           allow_small_or_imprecise_dtypes=True).then_inc(sem("moe_const"), 1)
            for q in range(4):
                nc.gpsimd.memset(view(Y, 512 * q, 512), 0.0).then_inc(sem("moe_added"), 1)

        def moe_dve(dve, link):
            V = nc.vector
            dve.wait_ge(*at("moe_logits", 1))
            link(V.tensor_copy(flat(LG), bank[4][:, 0:16]))
            dve.wait_ge(*at("moe_const", 6))
            for t in range(2):
                le = LG[:, t, :].unsqueeze(2).to_broadcast([P, 8, 8])
                lj = LG[:, t, :].unsqueeze(1).to_broadcast([P, 8, 8])
                link(V.tensor_tensor(U1, lj, le, ALU.is_gt))
                link(V.tensor_tensor(U2, lj, le, ALU.is_equal))
                link(V.tensor_tensor(U2, U2, LT, ALU.mult))
                link(V.tensor_tensor(U1, U1, U2, ALU.add))
                link(V.reduce_sum(RK[:, t, :], U1, AX.X))
                link(V.reduce_max(SML[:, t:t + 1], LG[:, t, :], AX.X))
                a = V.tensor_scalar(EX[:, t, :], LG[:, t, :], SML[:, t:t + 1], None, ALU.subtract)
                if t == 0:
                    link(a)
                else:
                    a.then_inc(sem("moe_max"), 1)
            V.tensor_scalar(flat(RK), flat(RK), 2.0, None, ALU.is_lt).then_inc(sem("moe_picked"), 1)
            dve.wait_ge(*at("moe_picked", 1))
            dve.wait_ge(*at("moe_exp", 1))
            link(V.tensor_tensor(flat(EX), flat(EX), flat(RK), ALU.mult))
            link(V.reduce_sum(SML[:, 2:4], EX, AX.X))
            link(V.reciprocal(SML[:, 2:4], SML[:, 2:4]))
            for t in range(2):
                V.tensor_scalar(GATE[:, t, 0:8], EX[:, t, :], SML[:, 2 + t:3 + t], None, ALU.mult)\
                    .then_inc(sem("moe_gates"), 1)
            dve.wait_ge(*at("moe_before", 1))
            link(V.scalar_tensor_tensor(flat(PX), bank[5][:, 0:16], 1.0, flat(RK), ALU.add, ALU.mult))
            link(V.memset(view(SCR, 1024, 32), -1.0))
            link(V.tensor_scalar(POS[:, :, 0:8], PX, -1.0, None, ALU.add))
            link(V.tensor_scalar(OV[:, 0, :], bank[5][:, 16:24], 128.5, None, ALU.is_gt))
            link(V.memset(CN[:, 0, :], 1.0))
            link(V.tensor_tensor_scan(CN[:, 1, :], CN[:, 0, :], OV[:, 0, :], 0.0, ALU.mult, ALU.add))
            for j in range(OVER):
                link(V.scalar_tensor_tensor(M3[:, j, :], CN[:, 1, :], float(j + 1), OV[:, 0, :],
                                            ALU.is_equal, ALU.mult))
            dve.wait_ge(*at("moe_gates", 2))
            for j in range(OVER):
                m = M3[:, j, :].unsqueeze(1).to_broadcast([P, 2, 8])
                link(V.tensor_tensor(PM, POS[:, :, 0:8], m, ALU.mult))
                link(V.reduce_sum(POS[:, :, 8 + j], PM, AX.X))
                link(V.tensor_scalar(POS[:, :, 8 + j], POS[:, :, 8 + j], -128.0, None, ALU.add))
                link(V.tensor_tensor(PM, GATE[:, :, 0:8], m, ALU.mult))
                link(V.reduce_sum(GATE[:, :, 8 + j], PM, AX.X))
            link(V.memset(GATE[:, :, 11:12], 0.0))
            link(V.tensor_copy(FTAB[:, 0:8], IOE))
            m = M3
            ioe = IOE.unsqueeze(1).to_broadcast([P, 3, 8])
            link(V.tensor_tensor(M3, M3, ioe, ALU.mult))
            link(V.reduce_sum(FTAB[:, 8:11], M3, AX.X))
            link(V.memset(FTAB[:, 11:12], 0.0))
            link(V.tensor_scalar(FTAB[:, 12:13], CN[:, 1, 7:8], float(NE), None, ALU.add))
            V.tensor_copy(ITAB[0:1, 0:13], FTAB[0:1, 0:13]).then_inc(sem("items_ready"), 1)
            dve.wait_ge(*at("items_ready", 1))

            def select(i, col):
                for t in range(2):
                    a = V.tensor_scalar(SEL[:, t, :], IOTA, POS[:, t, col], None, ALU.is_equal)
                a.then_inc(sem("moe_sel"), 1)

            def select_gate(i, col):
                for t in range(2):
                    a = V.tensor_scalar(SELG[:, t, :], IOTA, POS[:, t, col], GATE[:, t, col],
                                        ALU.is_equal, ALU.mult)
                a.then_inc(sem("moe_selg"), 1)

            def low(i, h):
                slot = arrival(0, h // 2)[2]
                dve.wait_ge(*at("moe_hi", HALVES * i + (h + 1)))
                V.tensor_tensor(WLO[:, h % SPLIT, :], ring[:, slot, (h % 2) * HALF:(h % 2 + 1) * HALF],
                                WHI[:, h % SPLIT, :].bitcast(F32), ALU.subtract).then_inc(sem("moe_lo"), 1)

            def gathered(i):
                for b in range(2):
                    dve.wait_ge(*at("moe_hgh", 2 * i + (b + 1)))
                    V.tensor_tensor(flat(HGL[:, 4 * b:4 * b + 4, :]), bank[b][:, :],
                                    flat(HGH[:, 4 * b:4 * b + 4, :]).bitcast(F32), ALU.subtract)\
                        .then_inc(sem("moe_hgl"), 1)

            select(0, slice(0, 1))
            select_gate(0, slice(0, 1))
            low(0, 0)
            low(0, 1)
            gathered(0)
            n = count(dve)
            with dve.Fori(0, n) as i:
                def turned(c):
                    rows = slice(2 * (c % 2), 2 * (c % 2) + 2)
                    dve.wait_ge(*at("moe_ahi", MOE_UP * i + (c + 1)))
                    V.tensor_tensor(flat(ALO[:, (c // 2) % 2, rows, :]), bank[3 + c % 2][:, 0:2 * P],
                                    flat(AHI[:, (c // 2) % 2, rows, :]).bitcast(F32), ALU.subtract)\
                        .then_inc(sem("moe_alo"), 1)

                nxt = bass.ds(i + 1, 1)
                for q, (kind, c) in enumerate(MOE_ORDER):
                    if (kind, c) == ("down", MOE_DOWN - 1):
                        dve.wait_ge(*at("moe_gathered", 2 * i + 2))
                        select(i + 1, nxt)
                        dve.wait_ge(*at("moe_gt", i + 1))
                        select_gate(i + 1, nxt)
                        turned(MOE_UP - 1)
                    low(i, 2 * q + 2)
                    low(i, 2 * q + 3)
                    if kind == "up":
                        dve.wait_ge(*at("moe_silu", MOE_UP * i + (c + 1)))
                        if c >= 2:
                            dve.wait_ge(*at("moe_turned", MOE_UP * i + (c - 1)))
                        V.tensor_tensor(AS[:, c % 2, :], SILU[:, c % 2, :], bank[c % 2][:, 256:512], ALU.mult)\
                            .then_inc(sem("moe_act"), 1)
                        if c >= 1:
                            turned(c - 1)
                gathered(i + 1)
                for q in range(4):
                    acc = view(Y, 512 * q, 512)
                    dve.wait_ge(*at("moe_spread", 4 * i + (q + 1)))
                    dve.wait_ge(*at("moe_added", 4 * i + (q + 1)))
                    V.tensor_tensor(acc, acc, bank[2 + q][:, :], ALU.add).then_inc(sem("moe_added"), 1)
            dve.wait_ge(*at("moe_added", n * 4 + 4))
            nc.vector.scalar_tensor_tensor(xs, xs, ALPHA, YACC, ALU.mult, ALU.add).then_inc(sem("moe_res"), KT)

        def out_sync(sp):
            sp.wait_ge(*at("out_ready", 1))
            sp.dma_start(OUT, xs).then_inc(sem("out_stored"), 16)
            sp.wait_ge(*at("out_stored", 16))

        block = ctx.enter_context(nc.Block())

        @block.sync
        def _(sp):
            need = {"norm0": 4, "attn": 18, "ffn0": 18 + 23 + 6, "norm1": 47, "four": 49, "ffn1": 49 + 17,
                    "rg": 66 + 12, "ffn2": 78 + 21, "gla": 99 + 8}
            count = need.get(last, len(plan))
            assert MOE0 == need["gla"]
            previous = {}
            for src, slot, rows, words, used, value in plan[:count]:
                if slot in previous:
                    sp.wait_ge(*at(previous[slot][0], previous[slot][1]))
                previous[slot] = (used, value)
                sp.dma_start(ring[0:rows, slot, 0:words], src).then_inc(sem(f"weights_in{slot}"), 16)
            if on("moe"):
                moe_sync(sp, previous)
            out_sync(sp)

        @block.tensor
        def _(pe):
            pe.wait_ge(*at("tables_in", 64))
            pe.wait_ge(*at("silu_c", 1))
            pe.wait_ge(*at("consts", 2))
            for job in mod_jobs[:8]:
                mod_pe(pe, *job)
            rms_pe(pe, "n0x", SEQ, bank[4])
            rms_pe(pe, "n0c", SEQ, bank[5])
            if on("attn"):
                attn_pe(pe)
            if on("ffn0"):
                rms_pe(pe, "n0f", SEQ, bank[7])
                ffn_pe(pe, 0)
            if on("norm1"):
                rms_pe(pe, "n1x", SEQ, bank[7])
            if on("four"):
                four_pe(pe)
            if on("ffn1"):
                rms_pe(pe, "n1f", SEQ, bank[7])
                ffn_pe(pe, 1)
            if on("rg"):
                rg_pe(pe)
                ln_pe(pe, "ln0", M0, "mix2_read")
            if on("ffn2"):
                swiglu_pe(pe)
                ln_pe(pe, "ln1", M0, "ffn2_read")
            if on("gla"):
                gla_pe(pe)
                ln_pe(pe, "ln2", X0, "mix3_read")
            if on("moe"):
                moe_pe(pe)
                ln_pe(pe, "ln3", X0, "moe_res", (6, 7))

        @block.scalar
        def _(act):
            tin = sem("tables_in")
            act.dma_start(PAR[:, :], A["params"]).then_inc(sem("params_in"), 16)
            act.dma_start(xs, A["xT"]).then_inc(sem("x_in"), 16)
            act.dma_start(CTXB, A["ctxT"]).then_inc(sem("x_in"), 16)
            act.dma_start(X[:, :, M0:X0], A["metaT"]).then_inc(sem("meta_in"), 16)
            act.dma_start(ROPE[:, :, :], A["rope"]).then_inc(tin, 16)
            act.dma_start(PROT, A["prot"]).then_inc(tin, 16)
            act.dma_start(IDENT[:, :], A["ident"]).then_inc(tin, 16)
            act.dma_start(MASK, A["mask"]).then_inc(tin, 16)
            act.wait_ge(*at("params_in", 16))
            nc.scalar.activation(par("cvec"), par("cvec"), ACT.Silu).then_inc(sem("silu_c"), 1)
            rms_act(act, "n0x", xs, SEQ, ("x_in", 32, 0), shift(0, 0), HCAT[:, :, CTX:])
            rms_act(act, "n0c", CTXB, CTX, ("n0x_sum", 1, 0), shift(0, 0, 1), HCAT[:, :, 0:CTX])
            if on("attn"):
                attn_act(act, None)
            if on("ffn0"):
                rms_act(act, "n0f", xs, SEQ, ("n0y_res", 1, 1), shift(0, 3), H)
                ffn_act(act, 0)
            if on("norm1"):
                act.dma_start(DFTD, A["dftd"]).then_inc(sem("dft_in"), 16)
                act.dma_start(DFTL, A["dftl"]).then_inc(sem("dft_in"), 16)
                rms_act(act, "n1x", xs, SEQ, ("n0g_res", 1, 1), shift(1, 0), H)
            if on("four"):
                four_act(act)
            if on("ffn1"):
                rms_act(act, "n1f", xs, SEQ, ("n1y_res", 1, 1), shift(1, 3), H)
                ffn_act(act, 1)
            if on("rg"):
                rg_act(act)
                ln_act(act, "ln0", M0, 0)
            if on("ffn2"):
                swiglu_act(act)
                ln_act(act, "ln1", M0, 1)
            if on("gla"):
                gla_act(act)
                ln_act(act, "ln2", X0, 2)
            if on("moe"):
                moe_act(act)
                ln_act(act, "ln3", X0, 3)

        @block.gpsimd
        def _(pool):
            nc.gpsimd.memset(ONES[:, :], 1.0).then_inc(sem("consts"), 1)
            nc.gpsimd.memset(X[:, :, 0:PADT], 0.0).then_inc(sem("consts"), 1)
            if on("gla"):
                gla_pool(pool)
            if on("moe"):
                moe_pool(pool)

        @block.vector
        def _(dve):
            chain = [0]

            def link(ins):
                chain[0] += 1
                ins.then_inc(sem("dve_chain"), 1)
                dve.wait_ge(*at("dve_chain", chain[0]))

            dve.wait_ge(*at("params_in", 16))
            dve.wait_ge(*at("silu_c", 1))
            for n, job in enumerate(mod_jobs[:8]):
                mod_sum(dve, *job)
                if n >= 1:
                    mod_store(dve, *mod_jobs[n - 1])
            mod_store(dve, *mod_jobs[7])
            mod_stored(dve, 8)
            coef_dve(0, 0, 1, 0, 0, 1.0)
            link(coef_dve(0, 1, 1, 1, 0, 1.0))
            rms_dve(dve, link, "n0x", xs, SEQ, bank[4], lambda j: COEF[:, 0, 0, j:j + 1], HCAT[:, :, CTX:])
            rms_dve(dve, link, "n0c", CTXB, CTX, bank[5], lambda j: COEF[:, 0, 1, j:j + 1], HCAT[:, :, 0:CTX])
            if on("attn"):
                attn_dve(dve, link)
                res_dve(dve, link, "n0y", bank[7], 0, 2)
            if on("ffn0"):
                rms_dve(dve, link, "n0f", xs, SEQ, bank[7], lambda j: COEF[:, 0, 3, j:j + 1], H)
                ffn_dve(dve, 0)
                res_dve(dve, link, "n0g", bank[7], 0, 4)
                coef_dve(1, 0, 1, 0, 0, 1.0)
                coef_dve(1, 2, 2, 0, 1, 0.0)
                coef_dve(1, 3, 4, 0, 2, 1.0)
                link(coef_dve(1, 4, 5, 0, 3, 0.0))
            if on("norm1"):
                rms_dve(dve, link, "n1x", xs, SEQ, bank[7], lambda j: COEF[:, 1, 0, j:j + 1], H)
            if on("four"):
                res_dve(dve, link, "n1y", bank[7], 1, 2)
            if on("ffn1"):
                rms_dve(dve, link, "n1f", xs, SEQ, bank[7], lambda j: COEF[:, 1, 3, j:j + 1], H)
                ffn_dve(dve, 1)
                res_dve(dve, link, "n1g", bank[7], 1, 4)
            if on("rg"):
                rg_dve(dve, link)
                ln_dve(dve, link, "ln0", M0)
            if on("ffn2"):
                swiglu_dve(dve)
                ln_dve(dve, link, "ln1", M0)
            if on("gla"):
                gla_dve(dve, link)
                ln_dve(dve, link, "ln2", X0)
            if on("moe"):
                moe_dve(dve, link)
                ln_dve(dve, link, "ln3", X0, (6, 7))
            final = {"norm0": ("n0c_out", KT), "attn": ("n0y_res", KT), "ffn0": ("n0g_res", KT),
                     "norm1": ("n1x_out", KT), "four": ("n1y_res", KT), "ffn1": ("n1g_res", KT),
                     "rg": ("ln0_out", KT), "ffn2": ("ln1_out", KT), "gla": ("ln2_out", KT),
                     "moe": ("ln3_out", KT)}[stages[-1]]
            dve.wait_ge(*at(final[0], final[1]))
            nc.vector.memset(SM[:, 0:1], 0.0).then_inc(sem("out_ready"), 1)


def _feature_major(a):
    return np.ascontiguousarray(a.T.reshape(-1, P, a.shape[0]).transpose(1, 0, 2))


def _columns(v, tile=P):
    c = v.reshape(-1, tile).T
    return np.concatenate([c, np.zeros((P - tile, c.shape[1]), v.dtype)]) if tile < P else c


def _blocks(w):
    return w.reshape(w.shape[0] // P, P, w.shape[1] // P, P).transpose(0, 2, 1, 3)


def _chunked(pieces):
    n, p, w = pieces.shape
    per = CHUNK // w
    chunks = -(-n // per)
    out = np.zeros((chunks, p, CHUNK), pieces.dtype)
    for c in range(chunks):
        got = pieces[c * per:(c + 1) * per]
        out[c, :, :got.shape[0] * w] = got.transpose(1, 0, 2).reshape(p, -1)
    return out


def _by_tile(w):
    return _chunked(_blocks(w).transpose(1, 0, 2, 3).reshape(-1, P, P))


def _pairs(w):
    b = _blocks(w)
    k, n = b.shape[:2]
    return _chunked(b.reshape(k, 2, n // 2, P, P).transpose(2, 1, 0, 3, 4).reshape(-1, P, P))


def _rows(w):
    return np.ascontiguousarray(w.reshape(KT, P, -1, 512).transpose(2, 1, 0, 3)).reshape(-1, P, CHUNK)


def _constants():
    f = np.float32
    n_freq = HD // 4
    inv = f(10000.0) ** (-np.arange(n_freq, dtype=f) / f(n_freq))
    tok = np.arange(SEQ)
    ang = np.stack([(tok // 64).astype(f)[:, None] * inv, (tok % 64).astype(f)[:, None] * inv])
    ang = np.repeat(ang[:, None], 2, axis=1).transpose(0, 1, 3, 2).reshape(HD, SEQ)
    rope = np.stack([np.cos(ang), np.sin(ang)], axis=1).astype(f)
    prot = np.zeros((HD, HD), f)
    for a in range(2):
        for j in range(n_freq):
            x1, x2 = a * 64 + j, a * 64 + n_freq + j
            prot[x2, x1] = -1.0
            prot[x1, x2] = 1.0
    q, k = np.arange(SEQ)[:, None], np.arange(SEQ)[None, :]
    mask = np.where(np.abs(q - k) <= 128, 0.0, -1e30).astype(f).reshape(2, P, SEQ).transpose(1, 0, 2)
    n = np.arange(256)
    a = 2 * np.pi * ((n[:, None] * n[None, :]) % 256) / 256
    c, s = np.cos(a), np.sin(a)
    dftd = np.concatenate([c, s], axis=1).reshape(2, P, 512).transpose(1, 0, 2)
    dftl = np.stack([c, -s]).reshape(2, 2, P, 256).transpose(2, 0, 1, 3) / 256
    return {"rope": rope, "prot": prot, "ident": np.eye(P, dtype=f), "mask": np.ascontiguousarray(mask),
            "dftd": np.ascontiguousarray(dftd, dtype=f), "dftl": np.ascontiguousarray(dftl, dtype=f)}


def layout(i):
    i = {k: np.asarray(v) for k, v in i.items()}
    out = _constants()
    out["xT"] = _feature_major(i["x"][0])
    out["ctxT"] = _feature_major(i["ctx"][0])
    out["metaT"] = _feature_major(i["meta_tokens_2"])
    for l in range(2):
        out[f"mod{l}"] = _rows(i["mod_w"][l])
        out[f"up{l}"] = _pairs(i["ffn_w_up"][l])
        out[f"down{l}"] = _by_tile(i["ffn_w_down"][l])
    w = i["attn_w_in"][0]
    q, kv = w[:, :1024], w[:, 1024:]
    keys = np.concatenate([kv[:, 0:256], kv[:, 512:768]], axis=1)
    vals = np.concatenate([kv[:, 256:512], kv[:, 768:1024]], axis=1)
    out["attn_in"] = np.concatenate([_by_tile(keys), _by_tile(q), _rows(vals)])
    out["attn_out"] = _by_tile(i["attn_w_out"][0])
    out["four_out"] = _by_tile(i["fourier_w_out"][0])
    w = i["rg_w_in_2"][0]
    w = np.concatenate([w[:, RGW:], w[:, :RGW]], axis=1)
    w = w.reshape(KT, P, 2 * RGN, RGT).transpose(2, 1, 0, 3).reshape(2 * RGN, P, KT * RGT)
    out["rg_in"] = _chunked(w)
    g = i["rg_w_gates_2"][0].reshape(2, RGB, 2, RGT, 2, RGT)
    g = g.transpose(1, 4, 0, 3, 2, 5).reshape(4 * RGB, RGT, 2 * RGT)
    out["rg_gates"] = _chunked(g)
    w = i["rg_w_out_2"][0].reshape(RGN, RGT, KT, P).transpose(2, 0, 1, 3).reshape(-1, RGT, P)
    out["rg_out"] = _chunked(w)
    out["ffn_in"] = _pairs(i["ffn_w_in_2"][0])
    out["ffn_out"] = _by_tile(i["ffn_w_out_2"][0])
    w = i["gla_w_in_2"][0]
    out["gla_in"] = np.concatenate([_by_tile(w[:, :1024]), _rows(w[:, 1024:2048]), _by_tile(w[:, 2048:3072])])
    out["gla_out"] = _by_tile(i["gla_w_out_2"][0])
    wi, wo = i["moe_w_in_2"][0], i["moe_w_out_2"][0]
    moe = np.empty((NE, MOE_CH, P, CHUNK), np.float32)
    ups = [q for q, (kind, _) in enumerate(MOE_ORDER) if kind == "up"]
    downs = [q for q, (kind, _) in enumerate(MOE_ORDER) if kind == "down"]
    moe[:, ups] = wi.reshape(NE, KT, P, 2, MOE_UP, 256).transpose(0, 4, 2, 1, 3, 5).reshape(NE, MOE_UP, P, CHUNK)
    moe[:, downs] = wo.reshape(NE, MOE_DOWN, 4, P, D).transpose(0, 1, 3, 2, 4).reshape(NE, MOE_DOWN, P, CHUNK)
    out["moe"] = moe.reshape(NE * MOE_CH, P, CHUNK)

    par = np.zeros((P, NPAR), np.float32)

    def put(name, a):
        at, n = PCOLS[name]
        assert a.shape[1] == n, (name, a.shape, n)
        par[:a.shape[0], at:at + n] = a

    put("cvec", np.stack([_columns(i["c"][0]), _columns(i["c_ctx"])], axis=2).reshape(P, -1))
    put("mod_b", _columns(i["mod_b"].reshape(-1)))
    put("norm_g", _columns(i["norm_g"].reshape(-1)))
    put("qg", i["q_norm_g"][0][:, None])
    put("kg", i["k_norm_g"][0][:, None])
    put("sink", np.broadcast_to(i["sink"], (P, 4)))
    for l in range(2):
        put(f"conv_w{l}", _columns(i["ffn_conv_w"][l].reshape(-1)))
        put(f"conv_b{l}", _columns(i["ffn_conv_b"][l]))
    put("ln_g", _columns(i["ln_gain_2"].reshape(-1)))
    put("ln_b", _columns(i["ln_bias_2"].reshape(-1)))
    put("rg_conv", _columns(i["rg_conv_w_2"][0].reshape(-1), RGT))
    put("rg_cb", _columns(i["rg_conv_b_2"][0], RGT))
    put("rg_gb", _columns(i["rg_b_gates_2"][0].reshape(-1), RGT))
    put("rg_lam", _columns(i["rg_lambda_2"][0], RGT))
    put("gla_bg", _columns(i["gla_b_gate_2"][0]))
    put("gla_ng", _columns(i["gla_norm_g_2"][0].reshape(-1)))
    put("router", i["moe_router_2"][0].reshape(KT, P, NE).transpose(1, 0, 2).reshape(P, -1))
    put("gla_wz", i["gla_w_in_2"][0][:, 3072:].reshape(KT, P, 16).transpose(1, 0, 2).reshape(P, -1))
    put("gla_wg", i["gla_w_gate_up_2"][0])
    out["params"] = par
    return out


def kernel(**inputs):
    import concourse.bacc as bacc
    from concourse.bass_utils import run_bass_kernel_spmd

    arrays = layout(inputs)
    nc = bacc.Bacc("TRN2", target_bir_lowering=False, num_devices=1)
    aps = {n: nc.dram_tensor(f"in_{n}", a.shape, F32, kind="ExternalInput").ap() for n, a in arrays.items()}
    out = nc.dram_tensor("out", (P, KT, SEQ), F32, kind="ExternalOutput").ap()
    block_program(nc, aps, out)
    r = run_bass_kernel_spmd(nc, [{f"in_{n}": a for n, a in arrays.items()}], core_ids=[0])
    o = r.results[0]["out"]
    return np.ascontiguousarray(o.transpose(2, 1, 0)).reshape(1, SEQ, D)
```

```python
from contextlib import ExitStack

import numpy as np
import concourse.bass as bass
from concourse import mybir

F32 = mybir.dt.float32
I32 = mybir.dt.int32
F32R = mybir.dt.float32r
ACT = mybir.ActivationFunctionType
ALU = mybir.AluOpType
AX = mybir.AxisListType

P = 128
D = 1024
KT = D // P
SEQ, CTX, META = 256, 256, 16
HEADS, HD = 8, 128
FF1, FF1T = 2816, 2816 // P
FF2, FF2T = 3584, 3584 // P
RGW, RGT = 1344, 84
RGN = RGW // RGT
RGB = 8
GH, GDV, GCH = 4, 256, 64
NE = 8
PADT = 48
TOK = PADT + META + SEQ
M0, X0 = PADT, PADT + META
T2 = META + SEQ
NCH = TOK // GCH
EPS, LN_EPS = 1e-6, 1e-5
ALPHA = (2 * 2) ** 0.25
SCALE = HD ** -0.5
CHUNK = 4096
RING = 3
BLK = CHUNK // P
PAIRS = CHUNK // (2 * D)
MOE_UP, MOE_DOWN = FF2 // 256, FF2 * D // P // CHUNK
MOE_CH = MOE_UP + MOE_DOWN
MOE_ORDER = []
for _c in range(MOE_UP):
    MOE_ORDER.append(("up", _c))
    if _c % 2 == 1 and _c >= 3:
        MOE_ORDER.append(("down", (_c - 3) // 2))
MOE_ORDER.append(("down", MOE_DOWN - 1))
HALF = CHUNK // 2
HALVES = 2 * MOE_CH
SPLIT = 3
OVER = 3
ITEMS = NE + OVER

PCOLS = {}


def _cols():
    at = 0
    for name, n in [("cvec", 2 * KT), ("mod_b", 2 * 48), ("norm_g", 2 * 4 * KT), ("qg", 1), ("kg", 1),
                    ("sink", 4), ("conv_w0", 3 * 2 * FF1T), ("conv_b0", 2 * FF1T),
                    ("conv_w1", 3 * 2 * FF1T), ("conv_b1", 2 * FF1T), ("ln_g", 4 * KT), ("ln_b", 4 * KT),
                    ("rg_conv", 4 * RGN), ("rg_cb", RGN), ("rg_gb", 2 * RGN), ("rg_lam", RGN),
                    ("gla_bg", GH), ("gla_ng", KT), ("router", KT * NE), ("gla_wz", KT * 16),
                    ("gla_wg", GH * P)]:
        PCOLS[name] = (at, n)
        at += n
    return at


NPAR = _cols()

SHARED = {}


def _share(family, stages, **signals):
    for kind, times in signals.items():
        for n, stage in enumerate(stages):
            SHARED[f"{stage}_{kind}"] = (f"{family}_{kind}", n * times)


_share("rms", ["n0x", "n0c", "n0y", "n0f", "n0g", "n1x", "n1y", "n1f", "n1g"], sq=KT, sum=1, var=1, std=1, scaled=KT)
_share("rms", ["n0x", "n0c", "n0f", "n1x", "n1f"], out=KT)
_share("rms", ["n0f", "n1f"], lo=KT)
_share("rms", ["n0y", "n0g", "n1y", "n1g"], res=KT)
_share("ln", ["ln0", "ln1", "ln2", "ln3"], mean=1, centred=4, sq=4, sum=1, var=1, std=1, scaled=4, out=KT)
_share("ffn", ["ffn0", "ffn1"], up=FF1T, tap1=FF1T, tap0=2 * FF1T, conv=FF1T, silu=FF1T, act=FF1T, down=KT, read=KT)
_share("mix", ["mix0", "mix1", "mix2", "mix3"], tile=KT, read=KT)


def block_program(nc, A, OUT):
    ctx = ExitStack()
    with ctx:
        def sb(name, shape, dt=F32):
            return ctx.enter_context(nc.sbuf_tensor(name, shape, dt))

        sems = {}

        def sem(name):
            name = SHARED.get(name, (name, 0))[0]
            if name not in sems:
                sems[name] = ctx.enter_context(nc.semaphore(name))
            return sems[name]

        def at(name, value):
            return sem(name), value + SHARED.get(name, (name, 0))[1]

        ring = sb("ring", [P, RING, CHUNK])
        WHI = sb("WHI", [P, SPLIT, HALF], F32R)
        WLO = sb("WLO", [P, SPLIT, HALF], F32R)
        AHIGH = sb("AHIGH", [P, KT * T2], F32R)
        ALOW = sb("ALOW", [P, KT * T2], F32R)
        X = sb("X", [P, KT, TOK])
        HB = sb("HB", [P, 4096])
        Y = sb("Y", [P, 2560])
        BIG = sb("BIG", [P, 8704])
        SCR = sb("SCR", [P, 3072])
        PAR = sb("PAR", [P, NPAR])
        STAT = sb("STAT", [P, 3, 320])
        ONES = sb("ONES", [P, P])
        IDENT = sb("IDENT", [P, P])
        MOD = sb("MOD", [P, 2, 48, 2])
        COEF = sb("COEF", [P, 2, 5, KT])
        SM = sb("SM", [P, 64])
        bank = [ctx.enter_context(nc.psum_tensor(f"bank{i}", [P, 512], F32)) for i in range(8)]

        def par(name, a=0, n=None):
            at, size = PCOLS[name]
            return PAR[:, at + a:at + (size if n is None else a + n)]

        def view(buf, at, *dims):
            n = int(np.prod(dims))
            v = buf[:, at:at + n]
            if len(dims) == 2:
                return v.rearrange("p (a b) -> p a b", b=dims[1])
            if len(dims) == 3:
                return v.rearrange("p (a b c) -> p a b c", b=dims[1], c=dims[2])
            return v

        xs = X[:, :, X0:TOK]
        HHI, HLO = view(AHIGH, 0, KT, SEQ), view(ALOW, 0, KT, SEQ)
        XHI, XLO = view(AHIGH, 0, KT, T2), view(ALOW, 0, KT, T2)
        HGH, HGL = view(AHIGH, 0, KT, P), view(ALOW, 0, KT, P)
        AHI, ALO = view(AHIGH, KT * P, 2, 4, P), view(ALOW, KT * P, 2, 4, P)

        plan, where = [], {}

        def one(name, c, rows=P, words=lambda c: CHUNK, used=None, value=None):
            slot, turn = len(plan) % RING, len(plan) // RING + 1
            where[name, c] = (slot, 16 * turn)
            plan.append((A[name][c, 0:rows, 0:words(c)], slot, rows, words(c), used, value(c)))

        def weights(name, n, rows, words, used, value):
            for c in range(n):
                one(name, c, rows, words, used, value)


        def down_words(c):
            return min(CHUNK, FF1T * KT * P - c * CHUNK)

        def rg_words(c):
            return min(6, 2 * RGN - 6 * c) * KT * RGT

        mod_jobs = [(0, c, v) for c in (1, 3) for v in range(2)] + [(0, c, 0) for c in range(4, 12)] + \
                   [(1, c, 0) for c in range(12)]
        mod_number = {job: n for n, job in enumerate(mod_jobs)}

        def mod_used(l):
            return lambda c: mod_number[l, c, 1 if l == 0 and c < 4 else 0] + 1

        for c in range(4):
            if c % 2 == 0:
                one("mod0", c, used="mod_direct", value=lambda c: c // 2 + 1)
            else:
                one("mod0", c, used="mod_sum", value=mod_used(0))
        weights("attn_in", 4, P, lambda c: CHUNK, "qkv_tile", lambda c: [4, 8, 12, 16][c])
        for c in range(4, 12):
            one("mod0", c, used="mod_sum", value=mod_used(0))
        weights("attn_out", 2, P, lambda c: CHUNK, "mix0_tile", lambda c: 4 * c + 4)

        split_first = {"ffn0": 0, "ffn1": FF1T, "ffn2": 2 * FF1T}

        def plan_ffn(l):
            for c in range(FF1T // PAIRS):
                one(f"up{l}", c, used="split_lo", value=lambda c: split_first[f"ffn{l}"] + PAIRS * (c + 1))
                if l == 1 and c in (2, 4):
                    one("mod1", 9 + c // 2, used="mod_sum", value=mod_used(1))
                if l == 0 and c % 2 == 0:
                    one("mod1", c // 2, used="mod_sum", value=mod_used(1))
            if l == 0:
                one("mod1", 6, used="mod_sum", value=mod_used(1))
            for c in range(6):
                one(f"down{l}", c, words=down_words, used=f"ffn{l}_down",
                    value=lambda c: min(KT, (BLK * (c + 1) - 1) // FF1T + 1))
                if l == 0 and c < 3:
                    one("mod1", 7 + c, used="mod_sum", value=mod_used(1))

        plan_ffn(0)
        weights("four_out", 2, P, lambda c: CHUNK, "mix1_tile", lambda c: 4 * c + 4)
        plan_ffn(1)
        for name, c in [("rg_in", 0), ("rg_in", 1), ("rg_in", 2), ("rg_gates", 0), ("rg_gates", 1),
                        ("rg_in", 3), ("rg_in", 4), ("rg_in", 5)]:
            if name == "rg_in":
                one(name, c, words=rg_words, used="rg_proj", value=lambda c: min(2 * RGN, 6 * c + 6))
            else:
                one(name, c, rows=RGT, words=lambda c: 48 * RGT if c < 1 else 16 * RGT,
                    used="rg_gate", value=lambda c: 24 if c < 1 else 32)
        weights("rg_out", 4, RGT, lambda c: CHUNK, "mix2_tile", lambda c: 2 * c + 2)
        weights("ffn_in", FF2T // PAIRS, P, lambda c: CHUNK, "split_lo",
                lambda c: split_first["ffn2"] + PAIRS * (c + 1))
        weights("ffn_out", FF2T * KT // BLK, P, lambda c: CHUNK, "ffn2_down",
                lambda c: min(KT, (BLK * (c + 1) - 1) // FF2T + 1))
        for c, (used, value) in enumerate([("gla_proj", 4), ("gla_proj", 8), ("gla_v", 3), ("gla_v", 6),
                                           ("gla_r", 4), ("gla_r", 8)]):
            one("gla_in", c, used=used, value=lambda c, v=value: v)
        weights("gla_out", 2, P, lambda c: CHUNK, "mix3_tile", lambda c: 4 * c + 4)
        MOE0 = len(plan)

        def take(pe, name, c):
            slot, value = where[name, c]
            pe.wait_ge(*at(f"weights_in{slot}", value))
            return ring[:, slot, :]

        def high(act, name, p, j, count):
            if j >= count:
                return
            w = take(act, name, j // PAIRS)
            if j >= SPLIT:
                act.wait_ge(*at(p + "_up", j - SPLIT + 1))
            elif p == "ffn1":
                act.wait_ge(*at("ffn0_up", FF1T))
            elif p == "ffn2":
                act.wait_ge(*at("ffn1_up", FF1T))
            nc.scalar.activation(WHI[:, j % SPLIT, :], w[:, (j % PAIRS) * HALF:(j % PAIRS + 1) * HALF], ACT.Copy)\
                .then_inc(sem("split_hi"), 1)

        def low(dve, name, p, j, count):
            if j >= count:
                return
            w = take(dve, name, j // PAIRS)
            dve.wait_ge(*at("split_hi", split_first[p] + j + 1))
            nc.vector.tensor_tensor(WLO[:, j % SPLIT, :], w[:, (j % PAIRS) * HALF:(j % PAIRS + 1) * HALF],
                                    WHI[:, j % SPLIT, :].bitcast(F32), ALU.subtract).then_inc(sem("split_lo"), 1)

        def split_start(eng, part, l):
            for j in range(PAIRS):
                part(eng, f"up{l}", f"ffn{l}", j, FF1T)

        def pair_pe(pe, p, j, outs, hi, lo, ready):
            pe.wait_ge(*at("split_lo", split_first[p] + j + 1))
            for part in range(2):
                for k in range(KT):
                    if j == 0 and part == 0:
                        pe.wait_ge(*at(ready, k + 1))
                    o = (part * KT + k) * P
                    wh, wl = WHI[:, j % SPLIT, o:o + P], WLO[:, j % SPLIT, o:o + P]
                    nc.tensor.matmul(outs[part], wh, hi[:, k, :], start=(k == 0), stop=False)
                    nc.tensor.matmul(outs[part], wl, hi[:, k, :], start=False, stop=False)
                    mm = nc.tensor.matmul(outs[part], wh, lo[:, k, :], start=False, stop=(k == KT - 1))
            mm.then_inc(sem(p + "_up"), 1)

        def squares_act(act, p, src, T, after):
            name, value, each = after
            for j in range(KT):
                act.wait_ge(*at(name, value + each * j))
                nc.scalar.activation(view(SCR, 0, KT, T)[:, j, :], src[:, j, :], ACT.Square)\
                    .then_inc(sem(p + "_sq"), 1)

        def shift_act(act, p, shift, dst, out=None):
            for j in range(KT):
                act.wait_ge(*at(p + "_scaled", j + 1))
                nc.scalar.activation((dst if out is None else out)[:, j, :], dst[:, j, :], ACT.Identity, bias=shift(j))\
                    .then_inc(sem(p + "_out"), 1)

        def rms_act(act, p, src, T, after, shift, dst, out=None):
            squares_act(act, p, src, T, after)
            root_act(act, p, T)
            shift_act(act, p, shift, dst, out)

        def root_act(act, p, T):
            act.wait_ge(*at(p + "_var", 1))
            st = STATC if p == "n0c" else STAT
            nc.scalar.activation(st[:, 1, 0:T], st[:, 0, 0:T], ACT.Sqrt).then_inc(sem(p + "_std"), 1)

        def out_act(act, norm, n, src, read):
            nc.scalar.activation(view(SCR, 0, KT, SEQ)[:, n, :], src, ACT.Square).then_inc(sem(norm + "_sq"), 1)
            nc.scalar.activation(view(Y, 0, KT, SEQ)[:, n, :], src, ACT.Copy).then_inc(sem(read), 1)

        def square_pe(pe, p, k, T, stat):
            pe.wait_ge(*at(p + "_sq", k + 1))
            mm = nc.tensor.matmul(stat[:, 0:T], ONES[:, :], view(SCR, 0, KT, T)[:, k, :],
                                  start=(k == 0), stop=(k == KT - 1))
            if k == KT - 1:
                mm.then_inc(sem(p + "_sum"), 1)

        def rms_pe(pe, p, T, stat):
            for k in range(KT):
                square_pe(pe, p, k, T, stat)

        def rms_dve(dve, link, p, src, T, stat, scale, dst, add=None):
            root_dve(dve, link, p, T, stat)
            scale_dve(dve, p, src, T, scale, dst, add)

        def root_dve(dve, link, p, T, stat):
            st = STATC if p == "n0c" else STAT
            dve.wait_ge(*at(p + "_sum", 1))
            nc.vector.tensor_scalar(st[:, 0, 0:T], stat[:, 0:T], 1.0 / D, EPS, ALU.mult, ALU.add)\
                .then_inc(sem(p + "_var"), 1)
            dve.wait_ge(*at(p + "_std", 1))
            link(nc.vector.reciprocal(st[:, 2, 0:T], st[:, 1, 0:T]))

        def scale_dve(dve, p, src, T, scale, dst, add=None):
            st = STATC if p == "n0c" else STAT
            for j in range(KT):
                nc.vector.scalar_tensor_tensor(dst[:, j, :], src[:, j, :], scale(j), st[:, 2, 0:T],
                                               ALU.mult, ALU.mult).then_inc(sem(p + "_scaled"), 1)
                if add is not None and j >= 1:
                    add(j - 1)
            if add is not None:
                add(KT - 1)

        def lo_dve(dve, l):
            for j in range(KT):
                dve.wait_ge(*at(f"n{l}f_out", j + 1))
                nc.vector.scalar_tensor_tensor(HLO[:, j, :], H[:, j, :], shift(l, 3)(j), HHI[:, j, :].bitcast(F32),
                                               ALU.add, ALU.subtract).then_inc(sem(f"n{l}f_lo"), 1)

        def res_dve(dve, link, p, stat, l, g):
            yv = view(Y, 0, KT, SEQ)

            def add(j):
                dve.wait_ge(*at(p + "_scaled", j + 1))
                nc.vector.tensor_tensor(xs[:, j, :], xs[:, j, :], yv[:, j, :], ALU.add).then_inc(sem(p + "_res"), 1)

            rms_dve(dve, link, p, yv, SEQ, stat, lambda j: COEF[:, l, g, j:j + 1], yv, add)

        def proj_pe(pe, name, p, rhs, T, banks, ready, norm=None):
            for n in range(KT):
                if n % 4 == 0:
                    w = take(pe, name, n // 4)
                if n >= len(banks):
                    pe.wait_ge(*at(p + "_read", n - len(banks) + 1))
                if n == 0:
                    ready()
                for k in range(KT):
                    b = (n % 4) * KT + k
                    mm = nc.tensor.matmul(bank[banks[n % len(banks)]][:, 0:T], w[:, b * P:(b + 1) * P],
                                          rhs[:, k, :], start=(k == 0), stop=(k == KT - 1))
                mm.then_inc(sem(p + "_tile"), 1)
                if norm is not None and n >= 1:
                    square_pe(pe, norm, n - 1, T, bank[7])
            if norm is not None:
                square_pe(pe, norm, KT - 1, T, bank[7])

        def proj_act(act, p, banks, norm, early=None):
            for n in range(KT):
                act.wait_ge(*at(p + "_tile", n + 1))
                out_act(act, norm, n, bank[banks[n % len(banks)]][:, 0:SEQ], p + "_read")
                if n == KT // 2 and early is not None:
                    early()
            root_act(act, norm, SEQ)

        def add_dve(dve, p, cols, T, banks, tile="_tile", read="_read", early=None):
            for n in range(KT):
                dve.wait_ge(*at(p + tile, n + 1))
                nc.vector.scalar_tensor_tensor(X[:, n, cols:TOK], X[:, n, cols:TOK], ALPHA,
                                               bank[banks[n % len(banks)]][:, 0:T], ALU.mult, ALU.add)\
                    .then_inc(sem(p + read), 1)
                if n == KT - 2 and early is not None:
                    early()

        def ln_pe(pe, p, cols, added, b=(0, 1)):
            T = TOK - cols
            for k in range(KT):
                pe.wait_ge(*at(added, k + 1))
                mm = nc.tensor.matmul(bank[b[0]][:, 0:T], ONES[:, :], X[:, k, cols:TOK],
                                      start=(k == 0), stop=(k == KT - 1))
            mm.then_inc(sem(p + "_mean"), 1)
            for k in range(KT):
                if k % 2 == 0:
                    pe.wait_ge(*at(p + "_sq", k // 2 + 1))
                mm = nc.tensor.matmul(bank[b[1]][:, 0:T], ONES[:, :], view(SCR, 0, KT, T)[:, k, :],
                                      start=(k == 0), stop=(k == KT - 1))
            mm.then_inc(sem(p + "_sum"), 1)

        def ln_act(act, p, cols, which):
            T = TOK - cols
            for h in range(4):
                act.wait_ge(*at(p + "_centred", h + 1))
                nc.scalar.activation(view(SCR, 0, KT, T)[:, 2 * h:2 * h + 2, :],
                                     X[:, 2 * h:2 * h + 2, cols:TOK], ACT.Square).then_inc(sem(p + "_sq"), 1)
            act.wait_ge(*at(p + "_var", 1))
            nc.scalar.activation(STAT[:, 1, 0:T], STAT[:, 0, 0:T], ACT.Sqrt).then_inc(sem(p + "_std"), 1)
            for j in range(KT):
                if j % 2 == 0:
                    act.wait_ge(*at(p + "_scaled", j // 2 + 1))
                nc.scalar.activation(X[:, j, cols:TOK], X[:, j, cols:TOK], ACT.Identity,
                                     bias=par("ln_b", which * KT + j, 1), scale=par("ln_g", which * KT + j, 1))\
                    .then_inc(sem(p + "_out"), 1)

        def ln_dve(dve, link, p, cols, b=(0, 1)):
            T = TOK - cols
            dve.wait_ge(*at(p + "_mean", 1))
            mean = bank[b[0]][:, 0:T].unsqueeze(1).to_broadcast([P, 2, T])
            for h in range(4):
                xh = X[:, 2 * h:2 * h + 2, cols:TOK]
                nc.vector.scalar_tensor_tensor(xh, mean, -1.0 / D, xh, ALU.mult, ALU.add)\
                    .then_inc(sem(p + "_centred"), 1)
            dve.wait_ge(*at(p + "_sum", 1))
            nc.vector.tensor_scalar(STAT[:, 0, 0:T], bank[b[1]][:, 0:T], 1.0 / D, LN_EPS, ALU.mult, ALU.add)\
                .then_inc(sem(p + "_var"), 1)
            dve.wait_ge(*at(p + "_std", 1))
            link(nc.vector.reciprocal(STAT[:, 2, 0:T], STAT[:, 1, 0:T]))
            dve.wait_ge(*at(p + "_centred", 4))
            rstd = STAT[:, 2, 0:T].unsqueeze(1).to_broadcast([P, 2, T])
            for h in range(4):
                xh = X[:, 2 * h:2 * h + 2, cols:TOK]
                nc.vector.tensor_tensor(xh, xh, rstd, ALU.mult).then_inc(sem(p + "_scaled"), 1)

        def mod_acc(n):
            buf, o = (HB, 2048) if n < 12 else (BIG, FF1T * SEQ)
            return [view(buf, o + 1024 * (n % 2) + 512 * i, 512) for i in range(2)]

        def mod_sum(dve, l, c, v):
            n = mod_number[l, c, v]
            w = take(dve, f"mod{l}", c)
            acc = mod_acc(n)
            if n >= 2:
                dve.wait_ge(*at("mod_cols", n - 1))
            for k in range(KT):
                wk, ck, a = w[:, k * 512:(k + 1) * 512], par("cvec", 2 * k + v, 1), acc[k % 2]
                if k < 2:
                    nc.vector.tensor_scalar(a, wk, ck, None, ALU.mult).then_inc(sem("mod_part"), 1)
                else:
                    dve.wait_ge(*at("mod_part", KT * n + k - 1))
                    nc.vector.scalar_tensor_tensor(a, wk, ck, a, ALU.mult, ALU.add).then_inc(sem("mod_part"), 1)
            dve.wait_ge(*at("mod_part", KT * n + KT))
            nc.vector.tensor_tensor(acc[0], acc[0], acc[1], ALU.add).then_inc(sem("mod_sum"), 1)

        def mod_pe(pe, l, c, v):
            n = mod_number[l, c, v]
            pe.wait_ge(*at("mod_sum", n + 1))
            if n >= 1:
                pe.wait_ge(*at("mod_stored", n))
            for t in range(4):
                mm = nc.tensor.matmul(bank[6][:, t * P:(t + 1) * P], mod_acc(n)[0][:, t * P:(t + 1) * P],
                                      ONES[:, :], start=True, stop=True)
            mm.then_inc(sem("mod_cols"), 1)

        def mod_store(dve, l, c, v):
            n = mod_number[l, c, v]
            dve.wait_ge(*at("mod_cols", n + 1))
            nc.vector.tensor_tensor(MOD[:, l, 4 * c:4 * c + 4, v], view(bank[6], 0, 4, P)[:, :, 0],
                                    par("mod_b", 48 * l + 4 * c, 4), ALU.add).then_inc(sem("mod_stored"), 1)

        def direct_pe(pe, c):
            w = take(pe, "mod0", c)
            for t in range(4):
                o = 2 * (2 * c + t)
                for k in range(KT):
                    mm = nc.tensor.matmul(bank[7 if c == 0 else 3][:, o:o + 2],
                                          w[:, k * 512 + t * P:k * 512 + (t + 1) * P], par("cvec", 2 * k, 2), start=(k == 0), stop=(k == KT - 1))
            mm.then_inc(sem("mod_direct"), 1)

        def direct_store(dve, c):
            dve.wait_ge(*at("mod_direct", c // 2 + 1))
            nc.vector.tensor_tensor(MOD[:, 0, 4 * c:4 * c + 4, :], view(bank[7 if c == 0 else 3], 4 * c, 4, 2),
                                    par("mod_b", 4 * c, 4).unsqueeze(2).to_broadcast([P, 4, 2]), ALU.add)\
                .then_inc(sem("direct_stored"), 1)

        def mod_stored(dve, n):
            dve.wait_ge(*at("mod_stored", n))

        def coef_dve(l, which, m, col, g, plus):
            return nc.vector.scalar_tensor_tensor(COEF[:, l, which, :], MOD[:, l, 8 * m:8 * m + 8, col],
                                                  plus, par("norm_g", (4 * l + g) * KT, KT),
                                                  ALU.add, ALU.mult)

        def shift(l, m, col=0):
            return lambda j: MOD[:, l, 8 * m + j, col:col + 1]

        STATC = view(Y, 0, 3, CTX)
        CTXB = view(BIG, 4096, KT, CTX)
        HCAT = view(HB, 0, KT, CTX + SEQ)
        H = view(HB, 0, KT, SEQ)

        QT = view(BIG, 0, HEADS, SEQ)
        KTT = view(BIG, 2048, 4, CTX + SEQ)
        VT = view(BIG, 4096, 4, 512)
        SQ = view(BIG, 6144, 4, 512)
        PROB = view(SCR, 0, 3, 512)
        ROPE = view(SCR, 1536, 2, SEQ)
        PROT = view(SCR, 2048, P)
        MASK = view(SCR, 2560, 2, SEQ)
        PT = view(Y, 0, 4, SEQ)
        OT = view(HB, 0, HEADS, SEQ)
        normed = [KTT[:, 0, :], KTT[:, 1, :], view(BIG, 0, 512), view(BIG, 512, 512)]
        roped = [KTT[:, 0:2, CTX:], KTT[:, 2:4, CTX:]] + [QT[:, 2 * i:2 * i + 2, :] for i in range(4)]

        q_bank = [bank[i] for i in (4, 5, 7, 0, 1, 2, 3, 4)]
        v_bank = [bank[i] for i in (5, 7, 0, 1)]
        s_bank = [bank[i] for i in (2, 3, 4, 6)]
        rot_bank = [bank[i] for i in (2, 3)]
        ROPE_ORDER = [1, 4, 5, 0, 2, 3]
        ROPE_NORMED = {0: 2, 2: 3, 3: 4}

        def attn_pe(pe):
            pe.wait_ge(*at("n0x_out", KT))
            w = take(pe, "attn_in", 0)
            for n in range(4):
                for k in range(KT):
                    if n == 0:
                        pe.wait_ge(*at("n0c_out", k + 1))
                    mm = nc.tensor.matmul(bank[n][:, :], w[:, (n * KT + k) * P:(n * KT + k + 1) * P],
                                          HCAT[:, k, :], start=(k == 0), stop=(k == KT - 1))
                mm.then_inc(sem("qkv_tile"), 1)
            for n in range(HEADS):
                if n % 4 == 0:
                    w = take(pe, "attn_in", 1 + n // 4)
                if n >= 3:
                    pe.wait_ge(*at("qkv_read", n - 2))
                for k in range(KT):
                    b = (n % 4) * KT + k
                    mm = nc.tensor.matmul(q_bank[n][:, 0:SEQ], w[:, b * P:(b + 1) * P], HCAT[:, k, CTX:],
                                          start=(k == 0), stop=(k == KT - 1))
                mm.then_inc(sem("qkv_tile"), 1)
            w = take(pe, "attn_in", 3)

            def value_tile(t):
                pe.wait_ge(*at("qkv_read", 6 + t))
                for k in range(KT):
                    mm = nc.tensor.matmul(v_bank[t][:, :], HCAT[:, k, t * P:(t + 1) * P],
                                          w[:, k * 512:(k + 1) * 512], start=(k == 0), stop=(k == KT - 1))
                mm.then_inc(sem("qkv_tile"), 1)

            def square_sum(i):
                pe.wait_ge(*at("qk_sq", i + 1))
                pe.wait_ge(*at("qkv_read", [10, 11, 12, 12][i]))
                nc.tensor.matmul(s_bank[i][:, :], ONES[:, :], SQ[:, i, :], start=True, stop=True)\
                    .then_inc(sem("qk_sum"), 1)

            def rotate(n):
                i = ROPE_ORDER[n]
                pe.wait_ge(*at("qk_var", 2))
                if i in ROPE_NORMED:
                    pe.wait_ge(*at("qk_normed", ROPE_NORMED[i]))
                if n >= 2:
                    pe.wait_ge(*at("qk_roped", n - 1))
                nc.tensor.matmul(rot_bank[n % 2][:, :].rearrange("p (a b) -> p a b", a=2), PROT, roped[i],
                                 start=True, stop=True).then_inc(sem("qk_rot"), 1)

            value_tile(0)
            square_sum(0)
            square_sum(1)
            value_tile(1)
            square_sum(2)
            square_sum(3)
            rotate(0)
            value_tile(2)
            rotate(1)
            rotate(2)
            value_tile(3)
            for n in range(3, 6):
                rotate(n)
            pe.wait_ge(*at("qkv_read", 16))

            def scores(u):
                h, q = u // 2, u % 2
                if u >= 3:
                    pe.wait_ge(*at("probs", u - 2))
                s = bank[u % 3]
                kv = h // 2
                nc_last = nc.tensor.matmul(s[:, :], QT[:, h, q * P:(q + 1) * P], KTT[:, kv, :],
                                           start=True, stop=(h < 4))
                if h >= 4:
                    nc_last = nc.tensor.matmul(s[:, CTX:], IDENT[:, :], MASK[:, q, :], start=False, stop=True)
                nc_last.then_inc(sem("scores"), 1)

            def turn(u):
                pe.wait_ge(*at("probs_normed", u + 1))
                if u >= 2:
                    pe.wait_ge(*at("turned_read", u - 1))
                for t in range(4):
                    mm = nc.tensor.transpose(bank[3 + u % 2][:, t * P:(t + 1) * P],
                                             PROB[:, u % 3, t * P:(t + 1) * P], IDENT[:, :])
                mm.then_inc(sem("turned"), 1)

            def values(h):
                pe.wait_ge(*at("turned_read", 2 * h + 2))
                if h >= 1:
                    pe.wait_ge(*at("heads_read", h))
                col = (h // 2) * P
                for t in range(4):
                    mm = nc.tensor.matmul(bank[5][:, 0:SEQ], VT[:, t, col:col + P],
                                          view(Y, (h % 2) * 1024, 4, SEQ)[:, t, :],
                                          start=(t == 0), stop=(t == 3))
                mm.then_inc(sem("heads"), 1)

            pe.wait_ge(*at("qk_roped", 6))
            for u in range(2 * HEADS + 3):
                if u < 2 * HEADS:
                    scores(u)
                if u % 2 == 1 and u >= 3:
                    mod_pe(pe, 0, 4 + (u - 3) // 2, 0)
                if 2 <= u < 2 * HEADS + 2:
                    turn(u - 2)
                if u >= 4 and u % 2 == 0:
                    values(u // 2 - 2)
            proj_pe(pe, "attn_out", "mix0", OT, SEQ, [0, 1, 2, 3], lambda: pe.wait_ge(*at("heads_read", HEADS)),
                    "n0y")

        def attn_act(act):
            for n in range(4):
                act.wait_ge(*at("qkv_tile", n + 1))
                nc.scalar.activation(KTT[:, n, :], bank[n][:, :], ACT.Copy).then_inc(sem("qkv_read"), 1)
            for n in range(HEADS):
                act.wait_ge(*at("qkv_tile", 5 + n))
                nc.scalar.activation(QT[:, n, :], q_bank[n][:, 0:SEQ], ACT.Copy).then_inc(sem("qkv_read"), 1)
                if n in (1, 2, 3, 4):
                    i = n - 1
                    act.wait_ge(*at("qkv_read", [1, 2, 6, 8][i]))
                    nc.scalar.activation(SQ[:, i, :], normed[i], ACT.Square).then_inc(sem("qk_sq"), 1)
            for t in range(4):
                act.wait_ge(*at("qkv_tile", 13 + t))
                nc.scalar.activation(VT[:, t, :], v_bank[t][:, :], ACT.Copy).then_inc(sem("qkv_read"), 1)
                for i in [(), (0, 1), (2, 3), ()][t]:
                    act.wait_ge(*at("qk_var", i + 1))
                    nc.scalar.activation(view(Y, 512 * i, 512), view(Y, 512 * i, 512), ACT.Sqrt)\
                        .then_inc(sem("qk_std"), 1)

            def exps(u):
                h = u // 2
                act.wait_ge(*at("maxima", u + 1))
                if u >= 3:
                    act.wait_ge(*at("turned", u - 2))
                nc.scalar.activation(PROB[:, u % 3, :], bank[u % 3][:, :], ACT.Exp, bias=SM[:, 16 + u:17 + u],
                                     scale=SCALE, accum_out=SM[:, 32 + u:33 + u]).then_inc(sem("probs"), 1)
                if h >= 4:
                    nc.scalar.activation(SM[:, 48 + u - 8:49 + u - 8], par("sink", h - 4, 1), ACT.Exp,
                                         bias=SM[:, 16 + u:17 + u]).then_inc(sem("sinks"), 1)

            def turned(u):
                h, q = u // 2, u % 2
                act.wait_ge(*at("turned", u + 1))
                if h >= 2 and q == 0:
                    act.wait_ge(*at("heads", h - 1))
                nc.scalar.activation(view(Y, (h % 2) * 1024, 4, SEQ)[:, :, q * P:(q + 1) * P],
                                     view(bank[3 + u % 2], 0, 4, P), ACT.Copy).then_inc(sem("turned_read"), 1)

            def head(h):
                act.wait_ge(*at("heads", h + 1))
                nc.scalar.activation(OT[:, h, :], bank[5][:, 0:SEQ], ACT.Copy).then_inc(sem("heads_read"), 1)

            for u in range(2 * HEADS + 3):
                if u < 2 * HEADS:
                    exps(u)
                if 2 <= u < 2 * HEADS + 2:
                    turned(u - 2)
                if u >= 4 and u % 2 == 0:
                    head(u // 2 - 2)
            proj_act(act, "mix0", [0, 1, 2, 3], "n0y", lambda: split_start(act, high, 0))

        def attn_dve(dve, link):
            def mean_square(i):
                dve.wait_ge(*at("qk_sum", i + 1))
                nc.vector.tensor_scalar(view(Y, 512 * i, 512), s_bank[i][:, :], 1.0 / HD, EPS,
                                        ALU.mult, ALU.add).then_inc(sem("qk_var"), 1)

            def norm(i):
                dve.wait_ge(*at("qk_std", i + 1))
                link(nc.vector.reciprocal(view(Y, 512 * i, 512), view(Y, 512 * i, 512)))
                nc.vector.scalar_tensor_tensor(normed[i], normed[i], par("kg" if i < 2 else "qg"),
                                               view(Y, 512 * i, 512), ALU.mult, ALU.mult)\
                    .then_inc(sem("qk_normed"), 1)

            def rope(n):
                i = ROPE_ORDER[n]
                cos = ROPE[:, 0, :].unsqueeze(1).to_broadcast([P, 2, SEQ])
                sin = ROPE[:, 1, :].unsqueeze(1).to_broadcast([P, 2, SEQ])
                if i in ROPE_NORMED:
                    dve.wait_ge(*at("qk_normed", ROPE_NORMED[i]))
                dve.wait_ge(*at("qk_rot", n + 1))
                t = SQ[:, n % 2, :].rearrange("p (a b) -> p a b", a=2)
                nc.vector.tensor_tensor(t, rot_bank[n % 2][:, :].rearrange("p (a b) -> p a b", a=2), sin,
                                        ALU.mult)
                link(nc.vector.tensor_tensor(roped[i], roped[i], cos, ALU.mult))
                nc.vector.tensor_tensor(roped[i], roped[i], t, ALU.add).then_inc(sem("qk_roped"), 1)

            dve.wait_ge(*at("rope_in", 16))
            for i in range(4):
                mean_square(i)
            norm(0)
            rope(0)
            norm(1)
            norm(2)
            rope(1)
            rope(2)
            norm(3)
            for n in range(3, 6):
                rope(n)
            link(nc.vector.tensor_scalar(SM[:, 56:60], par("sink"), -1.0, None, ALU.mult))

            def maxima(u):
                h = u // 2
                dve.wait_ge(*at("scores", u + 1))
                link(nc.vector.reduce_max(SM[:, u:u + 1], bank[u % 3][:, :], AX.X))
                if h >= 4:
                    nc.vector.tensor_scalar(SM[:, 16 + u:17 + u], SM[:, u:u + 1], -SCALE, SM[:, 52 + h:53 + h],
                                            ALU.mult, ALU.min).then_inc(sem("maxima"), 1)
                else:
                    nc.vector.tensor_scalar(SM[:, 16 + u:17 + u], SM[:, u:u + 1], -SCALE, None, ALU.mult)\
                        .then_inc(sem("maxima"), 1)

            def norms(u):
                h = u // 2
                dve.wait_ge(*at("probs", u + 1))
                total = SM[:, 32 + u:33 + u]
                if h >= 4:
                    dve.wait_ge(*at("sinks", u - 7))
                    link(nc.vector.tensor_tensor(total, total, SM[:, 48 + u - 8:49 + u - 8], ALU.add))
                link(nc.vector.reciprocal(total, total))
                nc.vector.tensor_scalar(PROB[:, u % 3, :], PROB[:, u % 3, :], total, None, ALU.mult)\
                    .then_inc(sem("probs_normed"), 1)

            for u in range(2 * HEADS + 1):
                if u < 2 * HEADS:
                    maxima(u)
                if u >= 1:
                    norms(u - 1)
                if u % 2 == 1:
                    mod_sum(dve, 0, 4 + u // 2, 0)
                    if u >= 3:
                        mod_store(dve, 0, 3 + u // 2, 0)
            mod_store(dve, 0, 11, 0)
            mod_stored(dve, 12)
            coef_dve(0, 2, 2, 0, 1, 0.0)
            coef_dve(0, 3, 4, 0, 2, 1.0)
            link(coef_dve(0, 4, 5, 0, 3, 0.0))

        def conv_bank(j):
            return bank[j % 4]

        UT = view(SCR, 0, 2, 2, SEQ)
        SG = view(SCR, 1024, 2, SEQ)
        ACTB = view(BIG, 0, FF1T, SEQ)

        def ffn_pe(pe, l):
            p = f"ffn{l}"
            for j in range(FF1T):
                if j >= 4:
                    pe.wait_ge(*at(p + "_conv", j - 3))
                pair_pe(pe, p, j, [conv_bank(j)[:, part * SEQ:(part + 1) * SEQ] for part in range(2)],
                        HHI, HLO, f"n{l}f_lo")
                if l == 0 and j % 4 == 3:
                    mod_pe(pe, 1, j // 4, 0)
                if l == 1 and j in (7, 11):
                    mod_pe(pe, 1, 9 + j // 4, 0)
            for n in range(KT):
                if n >= 2:
                    pe.wait_ge(*at(p + "_read", n - 1))
                for k in range(FF1T):
                    b = n * FF1T + k
                    if b % BLK == 0:
                        w = take(pe, f"down{l}", b // BLK)
                    if n == 0:
                        pe.wait_ge(*at(p + "_act", k + 1))
                    b %= BLK
                    mm = nc.tensor.matmul(bank[4 + n % 2][:, 0:SEQ], w[:, b * P:(b + 1) * P], ACTB[:, k, :],
                                          start=(k == 0), stop=(k == FF1T - 1))
                mm.then_inc(sem(p + "_down"), 1)
                if n >= 1:
                    square_pe(pe, f"n{l}g", n - 1, SEQ, bank[7])
                if l == 0 and n < 5:
                    mod_pe(pe, 1, 5 + n, 0)
            square_pe(pe, f"n{l}g", KT - 1, SEQ, bank[7])

        def ffn_act(act, l):
            p = f"ffn{l}"
            high(act, f"up{l}", p, 2, FF1T)
            for j in range(FF1T + 1):
                if j < FF1T:
                    act.wait_ge(*at(p + "_up", j + 1))
                    if j >= 2:
                        act.wait_ge(*at(p + "_act", j - 1))
                    for part in range(2):
                        f = part * FF1T + j
                        a = nc.scalar.activation(UT[:, j % 2, part, :], conv_bank(j)[:, part * SEQ:(part + 1) * SEQ],
                                                 ACT.Identity, bias=par(f"conv_b{l}", f, 1),
                                                 scale=par(f"conv_w{l}", 2 * FF1T + f, 1))
                    a.then_inc(sem(p + "_tap1"), 1)
                if j >= 1:
                    act.wait_ge(*at(p + "_conv", j))
                    nc.scalar.activation(SG[:, (j - 1) % 2, :], UT[:, (j - 1) % 2, 0, :], ACT.Silu)\
                        .then_inc(sem(p + "_silu"), 1)
                high(act, f"up{l}", p, j + SPLIT, FF1T)
            for n in range(KT):
                act.wait_ge(*at(p + "_down", n + 1))
                out_act(act, f"n{l}g", n, bank[4 + n % 2][:, 0:SEQ], p + "_read")
            root_act(act, f"n{l}g", SEQ)

        def ffn_dve(dve, l):
            p = f"ffn{l}"

            def conv(j):
                dve.wait_ge(*at(p + "_tap1", j + 1))
                for part in range(2):
                    f = part * FF1T + j
                    u = conv_bank(j)[:, part * SEQ:(part + 1) * SEQ]
                    t = UT[:, j % 2, part, :]
                    nc.vector.scalar_tensor_tensor(t[:, 1:SEQ], u[:, 0:SEQ - 1], par(f"conv_w{l}", f, 1),
                                                   t[:, 1:SEQ], ALU.mult, ALU.add).then_inc(sem(p + "_tap0"), 1)
                for part in range(2):
                    f = part * FF1T + j
                    u = conv_bank(j)[:, part * SEQ:(part + 1) * SEQ]
                    t = UT[:, j % 2, part, :]
                    dve.wait_ge(*at(p + "_tap0", 2 * j + part + 1))
                    a = nc.vector.scalar_tensor_tensor(t[:, 0:SEQ - 1], u[:, 1:SEQ],
                                                       par(f"conv_w{l}", 4 * FF1T + f, 1),
                                                       t[:, 0:SEQ - 1], ALU.mult, ALU.add)
                a.then_inc(sem(p + "_conv"), 1)

            low(dve, f"up{l}", p, 2, FF1T)
            for j in range(FF1T):
                conv(j)
                low(dve, f"up{l}", p, j + SPLIT, FF1T)
                dve.wait_ge(*at(p + "_silu", j + 1))
                dve.wait_ge(*at(p + "_conv", j + 1))
                nc.vector.tensor_tensor(ACTB[:, j, :], SG[:, j % 2, :], UT[:, j % 2, 1, :], ALU.mult)\
                    .then_inc(sem(p + "_act"), 1)
                if l == 0 and j % 4 == 0:
                    c = j // 4
                    mod_sum(dve, 1, c, 0)
                    if c >= 1:
                        mod_store(dve, 1, c - 1, 0)
                if l == 1 and j in (4, 8, 12):
                    if j < 12:
                        mod_sum(dve, 1, 9 + j // 4, 0)
                    if j > 4:
                        mod_store(dve, 1, 8 + j // 4, 0)
            if l == 0:
                for c in range(6, 10):
                    mod_sum(dve, 1, c, 0)
                    mod_store(dve, 1, c - 1, 0)
                mod_store(dve, 1, 9, 0)
            mod_stored(dve, len(mod_jobs) - (2 if l == 0 else 0))

        AB = view(BIG, 0, 2, 4, 512)
        DFTD = view(BIG, 4096, 2, 512)
        DFTL = view(BIG, 5120, 2, 2, SEQ)

        def four_pe(pe):
            pe.wait_ge(*at("dft_in", 32))
            for i in range(8):
                t, g = i // 4, i % 4
                pe.wait_ge(*at("n1x_out", 2 * g + 2 if t == 0 else KT))
                if i >= 4:
                    pe.wait_ge(*at("four_read", i - 3))
                for k in range(2):
                    mm = nc.tensor.matmul(bank[i % 4][:, :], H[:, 2 * g + k, t * P:(t + 1) * P], DFTD[:, k, :],
                                          start=(k == 0), stop=(k == 1))
                mm.then_inc(sem("four_ab"), 1)
            for f in range(KT):
                if f == 0:
                    pe.wait_ge(*at("four_read", 8))
                if f >= 2:
                    pe.wait_ge(*at("four_mixed", f - 1))
                g, half = f // 2, f % 2
                for i in range(4):
                    t, part = i // 2, i % 2
                    mm = nc.tensor.matmul(bank[4 + f % 2][:, 0:SEQ],
                                          AB[:, t, g, part * 256 + half * P:part * 256 + (half + 1) * P],
                                          DFTL[:, part, t, :], start=(i == 0), stop=(i == 3))
                mm.then_inc(sem("four_f"), 1)
            proj_pe(pe, "four_out", "mix1", H, SEQ, [0, 1, 2, 3], lambda: pe.wait_ge(*at("four_mixed", KT)),
                    "n1y")

        def four_act(act):
            for i in range(8):
                act.wait_ge(*at("four_ab", i + 1))
                nc.scalar.activation(AB[:, i // 4, i % 4, :], bank[i % 4][:, :], ACT.Copy)\
                    .then_inc(sem("four_read"), 1)
            for f in range(KT):
                act.wait_ge(*at("four_f", f + 1))
                nc.scalar.activation(H[:, f, :], bank[4 + f % 2][:, 0:SEQ], ACT.Copy)\
                    .then_inc(sem("four_mixed"), 1)
            proj_act(act, "mix1", [0, 1, 2, 3], "n1y", lambda: split_start(act, high, 1))

        XC = view(BIG, 0, RGN, T2)
        RA = view(BIG, 4352, RGN, T2)
        RH = view(SCR, 0, RGN // 2, T2)
        RI = view(SCR, 2176, 2, T2)
        RW = view(Y, 0, RGN // 2, T2)
        LAM = SM
        XM = X[:, :, M0:TOK]

        def rg_pe(pe):
            pe.wait_ge(*at("meta_in", 16))
            w = None

            def proj(n):
                nonlocal w
                if n % 6 == 0:
                    w = take(pe, "rg_in", n // 6)
                if 4 <= n < RGN + 4:
                    pe.wait_ge(*at("rg_conv", n - 3))
                elif n >= 4:
                    pe.wait_ge(*at("rg_gelu", n - RGN - 3))
                for k in range(KT):
                    if n == 0:
                        pe.wait_ge(*at("n1g_res", k + 1))
                    o = ((n % 6) * KT + k) * RGT
                    mm = nc.tensor.matmul(bank[n % 4][0:RGT, 0:T2], w[:, o:o + RGT], XM[:, k, :],
                                          start=(k == 0), stop=(k == KT - 1))
                mm.then_inc(sem("rg_proj"), 1)

            for n in range(RGN):
                proj(n)
            for b in range(RGB):
                for i in range(4):
                    n = 4 * b + i
                    if n % 24 == 0:
                        wg = take(pe, "rg_gates", n // 24)
                    if n >= 4:
                        pe.wait_ge(*at("rg_gate_read", n - 3))
                    if i == 0:
                        pe.wait_ge(*at("rg_conv", 2 * b + 2))
                    for c in range(2):
                        o = ((n % 24) * 2 + c) * RGT
                        mm = nc.tensor.matmul(bank[4 + i][0:RGT, 0:T2], wg[0:RGT, o:o + RGT],
                                              XC[0:RGT, 2 * b + c, :], start=(c == 0), stop=(c == 1))
                    mm.then_inc(sem("rg_gate"), 1)
            for n in range(RGN, 2 * RGN):
                proj(n)
            for n in range(KT):
                if n % 2 == 0:
                    wo = take(pe, "rg_out", n // 2)
                if n >= 2:
                    pe.wait_ge(*at("mix2_read", n - 1))
                for k in range(RGN):
                    if n == 0:
                        pe.wait_ge(*at("rg_y", k + 1))
                    b = (n % 2) * RGN + k
                    mm = nc.tensor.matmul(bank[4 + n % 2][:, 0:T2], wo[0:RGT, b * P:(b + 1) * P],
                                          XC[0:RGT, k, :], start=(k == 0), stop=(k == RGN - 1))
                mm.then_inc(sem("mix2_tile"), 1)

        def rg_act(act):
            act.wait_ge(*at("lam_abs", 1))
            nc.scalar.activation(LAM[0:RGT, 16:32], LAM[0:RGT, 0:16], ACT.Exp, scale=-1.0)\
                .then_inc(sem("lam_exp"), 1)
            for n in range(RGN):
                act.wait_ge(*at("rg_proj", n + 1))
                nc.scalar.activation(XC[0:RGT, n, :], bank[n % 4][0:RGT, 0:T2], ACT.Identity,
                                     bias=par("rg_cb", n, 1)[0:RGT], scale=par("rg_conv", 3 * RGN + n, 1)[0:RGT])\
                    .then_inc(sem("rg_tap3"), 1)
            for half in range(2):
                for t in range(8):
                    n = 8 * half + t
                    act.wait_ge(*at("rg_gate", 4 * (n // 2) + 2 * (n % 2) + 2))
                    if half == 1 and t == 0:
                        act.wait_ge(*at("rg_w", 8))
                    nc.scalar.activation(RH[0:RGT, t, :], bank[4 + 2 * (n % 2)][0:RGT, 0:T2], ACT.Sigmoid,
                                         bias=par("rg_gb", n, 1)[0:RGT]).then_inc(sem("rg_gate_read"), 1)
                    if n >= 2:
                        act.wait_ge(*at("rg_ix", n - 1))
                    nc.scalar.activation(RI[0:RGT, n % 2, :], bank[5 + 2 * (n % 2)][0:RGT, 0:T2], ACT.Sigmoid,
                                         bias=par("rg_gb", RGN + n, 1)[0:RGT]).then_inc(sem("rg_gate_read"), 1)
                if half == 0:
                    act.wait_ge(*at("lam_ready", 1))
                act.wait_ge(*at("rg_gate_read", 16 * half + 16))
                if half == 1:
                    act.wait_ge(*at("rg_u", 1))
                for t in range(8):
                    n = 8 * half + t
                    nc.scalar.activation(RA[0:RGT, n, :], RH[0:RGT, t, :], ACT.Exp, scale=LAM[0:RGT, 32 + n:33 + n])\
                        .then_inc(sem("rg_a"), 1)
                    nc.scalar.activation(RW[0:RGT, t, :], RH[0:RGT, t, :], ACT.Exp, scale=LAM[0:RGT, 48 + n:49 + n])
                    nc.scalar.activation(RH[0:RGT, t, :], RH[0:RGT, t, :], ACT.Tanh, scale=LAM[0:RGT, 32 + n:33 + n])\
                        .then_inc(sem("rg_tanh"), 1)
                act.wait_ge(*at("rg_w", 8 * half + 8))
                nc.scalar.activation(RW[0:RGT, :, :], RW[0:RGT, :, :], ACT.Sqrt, scale=-1.0)\
                    .then_inc(sem("rg_root"), 1)
            for n in range(RGN):
                act.wait_ge(*at("rg_proj", RGN + n + 1))
                if n >= 2:
                    act.wait_ge(*at("rg_y", n - 1))
                nc.scalar.activation(RI[0:RGT, n % 2, :], bank[n % 4][0:RGT, 0:T2], ACT.Gelu_apprx_tanh)\
                    .then_inc(sem("rg_gelu"), 1)

        def rg_dve(dve, link):
            lam = par("rg_lam")[0:RGT]
            V = nc.vector
            z, s, q, acc = (LAM[0:RGT, i:i + 16] for i in (16, 0, 32, 48))
            link(V.tensor_scalar(q, lam, -1.0, None, ALU.mult))
            V.tensor_tensor(LAM[0:RGT, 0:16], lam, q, ALU.max).then_inc(sem("lam_abs"), 1)
            dve.wait_ge(*at("lam_exp", 1))
            link(V.tensor_scalar(acc, z, 2.0, None, ALU.add))
            link(V.reciprocal(acc, acc))
            link(V.tensor_tensor(s, z, acc, ALU.mult))
            link(V.tensor_tensor(q, s, s, ALU.mult))
            link(V.tensor_scalar(acc, q, 1.0 / 19, 1.0 / 17, ALU.mult, ALU.add))
            for m in (15, 13, 11, 9, 7, 5, 3, 1):
                link(V.tensor_tensor(acc, acc, q, ALU.mult))
                link(V.tensor_scalar(acc, acc, 1.0 / m, None, ALU.add))
            link(V.tensor_tensor(acc, acc, s, ALU.mult))
            link(V.tensor_scalar(q, lam, -1.0, 0.0, ALU.mult, ALU.max))
            link(V.scalar_tensor_tensor(acc, acc, 2.0, q, ALU.mult, ALU.add))
            link(V.tensor_scalar(q, acc, -8.0, None, ALU.mult))
            V.tensor_scalar(acc, q, 2.0, None, ALU.mult).then_inc(sem("lam_ready"), 1)
            for n in range(RGN):
                dve.wait_ge(*at("rg_tap3", n + 1))
                for lag in (1, 2, 3):
                    a = V.scalar_tensor_tensor(XC[0:RGT, n, lag:T2], bank[n % 4][0:RGT, 0:T2 - lag],
                                               par("rg_conv", (3 - lag) * RGN + n, 1)[0:RGT],
                                               XC[0:RGT, n, lag:T2], ALU.mult, ALU.add)
                    if lag < 3:
                        link(a)
                    else:
                        a.then_inc(sem("rg_conv"), 1)
            for half in range(2):
                for t in range(8):
                    n = 8 * half + t
                    dve.wait_ge(*at("rg_gate_read", 2 * n + 2))
                    dve.wait_ge(*at("rg_gate", 4 * (n // 2) + 4))
                    V.tensor_tensor(XC[0:RGT, n, :], XC[0:RGT, n, :], RI[0:RGT, n % 2, :], ALU.mult)\
                        .then_inc(sem("rg_ix"), 1)
                for t in range(8):
                    n = 8 * half + t
                    dve.wait_ge(*at("rg_tanh", n + 1))
                    V.scalar_tensor_tensor(RW[0:RGT, t, :], RW[0:RGT, t, :], 1.0, RH[0:RGT, t, :],
                                           ALU.add, ALU.mult).then_inc(sem("rg_w"), 1)
                dve.wait_ge(*at("rg_root", half + 1))
                dve.wait_ge(*at("rg_ix", 8 * half + 8))
                u = XC[0:RGT, 8 * half:8 * half + 8, :]
                V.tensor_tensor(u, u, RW[0:RGT, :, :], ALU.mult).then_inc(sem("rg_u"), 1)
                dve.wait_ge(*at("rg_u", half + 1))
                for t in range(8):
                    n = 8 * half + t
                    V.tensor_tensor_scan(XC[0:RGT, n, :], RA[0:RGT, n, :], XC[0:RGT, n, :], 0.0,
                                         ALU.mult, ALU.add).then_inc(sem("rg_h"), 1)
            for n in range(RGN):
                dve.wait_ge(*at("rg_gelu", n + 1))
                dve.wait_ge(*at("rg_h", n + 1))
                V.tensor_tensor(XC[0:RGT, n, :], XC[0:RGT, n, :], RI[0:RGT, n % 2, :], ALU.mult)\
                    .then_inc(sem("rg_y"), 1)
            add_dve(dve, "mix2", M0, T2, [4, 5],
                    early=lambda: [low(dve, "ffn_in", "ffn2", j, FF2T) for j in range(PAIRS)])

        SA = view(SCR, 0, 2, T2)
        ACT2 = view(BIG, 0, FF2T, T2)

        def swiglu_pe(pe):
            for j in range(FF2T):
                if j >= 3:
                    pe.wait_ge(*at("ffn2_act", j - 2))
                pair_pe(pe, "ffn2", j, [bank[2 * (j % 3) + part][:, 0:T2] for part in range(2)], XHI, XLO, "ln0_lo")
            for n in range(KT):
                if n >= 2:
                    pe.wait_ge(*at("ffn2_read", n - 1))
                for k in range(FF2T):
                    b = n * FF2T + k
                    if b % BLK == 0:
                        w = take(pe, "ffn_out", b // BLK)
                    if n == 0:
                        pe.wait_ge(*at("ffn2_act", k + 1))
                    b %= BLK
                    mm = nc.tensor.matmul(bank[6 + n % 2][:, 0:T2], w[:, b * P:(b + 1) * P], ACT2[:, k, :],
                                          start=(k == 0), stop=(k == FF2T - 1))
                mm.then_inc(sem("ffn2_down"), 1)

        def swiglu_act(act):
            for j in range(KT):
                act.wait_ge(*at("ln0_out", j + 1))
                nc.scalar.activation(XHI[:, j, :], XM[:, j, :], ACT.Copy).then_inc(sem("ln0_hi"), 1)
            high(act, "ffn_in", "ffn2", 2, FF2T)
            for j in range(FF2T):
                act.wait_ge(*at("ffn2_up", j + 1))
                if j >= 2:
                    act.wait_ge(*at("ffn2_act", j - 1))
                nc.scalar.activation(SA[:, j % 2, :], bank[2 * (j % 3)][:, 0:T2], ACT.Silu)\
                    .then_inc(sem("ffn2_silu"), 1)
                high(act, "ffn_in", "ffn2", j + SPLIT, FF2T)

        def swiglu_dve(dve):
            for j in range(KT):
                dve.wait_ge(*at("ln0_hi", j + 1))
                nc.vector.tensor_tensor(XLO[:, j, :], XM[:, j, :], XHI[:, j, :].bitcast(F32), ALU.subtract)\
                    .then_inc(sem("ln0_lo"), 1)
            low(dve, "ffn_in", "ffn2", 2, FF2T)
            for j in range(FF2T):
                dve.wait_ge(*at("ffn2_silu", j + 1))
                nc.vector.tensor_tensor(ACT2[:, j, :], SA[:, j % 2, :], bank[2 * (j % 3) + 1][:, 0:T2], ALU.mult)\
                    .then_inc(sem("ffn2_act"), 1)
                low(dve, "ffn_in", "ffn2", j + SPLIT, FF2T)
            add_dve(dve, "ffn2", M0, T2, [6, 7], "_down")

        GQ, GK, GB, GQ1, GK1 = (view(BIG, GH * TOK * i, GH, TOK) for i in range(5))
        GKT = view(BIG, 6400, 2, GH, P)
        GS = view(BIG, 7424, GH, GDV)
        GD, GE = (view(Y, GH * TOK * i, GH, TOK) for i in range(2))
        GO = view(Y, 0, KT, SEQ)
        GV = view(SCR, 0, 3, D)
        GSC = view(HB, 0, 2, GH, GCH)
        GZ = view(HB, 512, TOK)
        GSQ = view(BIG, 0, KT, SEQ)
        GR = view(BIG, GH * TOK * 3, KT, SEQ)
        GDEC = view(HB, 1536, GH, NCH)
        GST = view(HB, 2048, GH, SEQ)

        def flat(v):
            return v.rearrange("p a b -> p (a b)")

        def chunks(v):
            return flat(v).rearrange("p (n c) -> p n c", c=GCH)

        def at_chunk(v, i):
            return chunks(v)[:, :, i:i + 1].to_broadcast([P, GH * NCH, GCH])

        def gla_pe(pe):
            for i in range(8):
                if i % 4 == 0:
                    w = take(pe, "gla_in", i // 4)
                if i >= 4:
                    pe.wait_ge(*at("gla_read", i - 3))
                for k in range(KT):
                    if i == 0:
                        pe.wait_ge(*at("ln1_out", k + 1))
                    b = (i % 4) * KT + k
                    mm = nc.tensor.matmul(bank[i % 4][:, 0:TOK], w[:, b * P:(b + 1) * P], X[:, k, :],
                                          start=(k == 0), stop=(k == KT - 1))
                mm.then_inc(sem("gla_proj"), 1)
            for k in range(KT):
                mm = nc.tensor.matmul(bank[4][0:16, 0:TOK], par("gla_wz", 16 * k, 16), X[:, k, :],
                                      start=(k == 0), stop=(k == KT - 1))
            mm.then_inc(sem("gla_z"), 1)
            pe.wait_ge(*at("gla_z_read", 1))
            for h in range(GH):
                if h == 0:
                    pe.wait_ge(*at("gla_read", 8))
                nc.tensor.matmul(bank[h][:, 0:TOK], par("gla_wg", P * h, P)[0:16], GZ[0:16, :],
                                 start=True, stop=True).then_inc(sem("gla_g"), 1)
            v = 0
            for half in range(2):
                w = take(pe, "gla_in", 2 + half)
                for t in range(3):
                    n = P if t < 2 else GCH
                    if v >= 2:
                        pe.wait_ge(*at("gla_v_read", v - 1))
                    for k in range(KT):
                        mm = nc.tensor.matmul(bank[5 + v % 2][0:n, :], X[:, k, t * P:t * P + n],
                                              w[:, k * 512:(k + 1) * 512], start=(k == 0), stop=(k == KT - 1))
                    v += 1
                    mm.then_inc(sem("gla_v"), 1)
            pe.wait_ge(*at("gla_scaled", 4))
            for c in range(1, NCH):
                lo, slot = (c % 2) * GCH, (c - 1) // 2
                for h in range(GH):
                    mm = nc.tensor.matmul(bank[7][lo:lo + GCH, slot * 256 + h * GCH:slot * 256 + (h + 1) * GCH],
                                          GK1[:, h, c * GCH:(c + 1) * GCH], GQ1[:, h, c * GCH:(c + 1) * GCH],
                                          start=True, stop=True)
            mm.then_inc(sem("gla_scores"), 1)
            for t in range(2):
                for h in range(GH):
                    mm = nc.tensor.transpose(bank[4 if t else 0][:, h * P:(h + 1) * P],
                                             GK[:, h, t * P:(t + 1) * P], IDENT[:, :])
                mm.then_inc(sem("gla_kt"), 1)
            pe.wait_ge(*at("gla_kt_read", 2))
            pe.wait_ge(*at("gla_v_read", 6))
            pe.wait_ge(*at("gla_masked", 2))

            def gate(i):
                w = take(pe, "gla_in", 4 + i // 4)
                if i >= 2:
                    pe.wait_ge(*at("gla_r_read", i - 1))
                for k in range(KT):
                    b = (i % 4) * KT + k
                    mm = nc.tensor.matmul(bank[[1, 6][i % 2]][:, 0:SEQ], w[:, b * P:(b + 1) * P], xs[:, k, :],
                                          start=(k == 0), stop=(k == KT - 1))
                mm.then_inc(sem("gla_r"), 1)

            for c in range(NCH):
                lo, slot, t = (c % 2) * GCH, (c - 1) // 2, c // 2
                if c >= 1:
                    gate(2 * c - 2)
                    pe.wait_ge(*at("gla_state", GH * c))
                    if c >= 2:
                        pe.wait_ge(*at("gla_o_read", c - 1))
                    for h in range(GH):
                        for e in range(2):
                            i = 2 * h + e
                            o = bank[0][:, i * GCH:(i + 1) * GCH]
                            nc.tensor.matmul(o, GV[lo:lo + GCH, t, i * P:(i + 1) * P], GSC[lo:lo + GCH, slot, h, :],
                                             start=True, stop=False)
                            mm = nc.tensor.matmul(o, GS[:, h, e * P:(e + 1) * P], GQ[:, h, c * GCH:(c + 1) * GCH],
                                                  start=False, stop=True)
                    mm.then_inc(sem("gla_o"), 1)
                if c < NCH - 1:
                    for h in range(GH):
                        mm = nc.tensor.matmul(bank[2 + h // 2][:, (h % 2) * GDV:(h % 2 + 1) * GDV],
                                              GKT[lo:lo + GCH, t, h, :],
                                              GV[lo:lo + GCH, t, h * GDV:(h + 1) * GDV], start=True, stop=True)
                    mm.then_inc(sem("gla_kv"), 1)
                if c >= 1:
                    gate(2 * c - 1)
            pe.wait_ge(*at("gla_o_read", NCH - 1))
            for h in range(GH):
                for e in range(2):
                    mm = nc.tensor.matmul(bank[4 + h // 2][:, (h % 2) * SEQ:(h % 2 + 1) * SEQ], ONES[:, :],
                                          GO[:, 2 * h + e, :], start=(e == 0), stop=(e == 1))
            mm.then_inc(sem("gla_mean"), 1)
            pe.wait_ge(*at("gla_r_read", 8))
            for h in range(GH):
                if h % 2 == 0:
                    pe.wait_ge(*at("gla_sq", h // 2 + 1))
                for e in range(2):
                    mm = nc.tensor.matmul(bank[6 + h // 2][:, (h % 2) * SEQ:(h % 2 + 1) * SEQ], ONES[:, :],
                                          GSQ[:, 2 * h + e, :], start=(e == 0), stop=(e == 1))
            mm.then_inc(sem("gla_sum"), 1)
            proj_pe(pe, "gla_out", "mix3", GO, SEQ, [2, 3], lambda: pe.wait_ge(*at("gla_gated", KT)))

        def gla_act(act):
            for i in range(8):
                act.wait_ge(*at("gla_proj", i + 1))
                if i < GH:
                    nc.scalar.activation(GQ[:, i, :], bank[i % 4][:, 0:TOK], ACT.Copy, scale=SCALE)\
                        .then_inc(sem("gla_read"), 1)
                else:
                    nc.scalar.activation(GK[:, i - GH, :], bank[i % 4][:, 0:TOK], ACT.Copy)\
                        .then_inc(sem("gla_read"), 1)
            act.wait_ge(*at("gla_z", 1))
            nc.scalar.activation(GZ[0:16, :], bank[4][0:16, 0:TOK], ACT.Copy).then_inc(sem("gla_z_read"), 1)
            for h in range(GH):
                act.wait_ge(*at("gla_g", h + 1))
                nc.scalar.activation(GE[:, h, :], bank[h][:, 0:TOK], ACT.Identity, bias=par("gla_bg", h, 1))\
                    .then_inc(sem("gla_x"), 1)
            act.wait_ge(*at("gla_x", GH))
            nc.scalar.activation(flat(GD), flat(GE), ACT.Abs).then_inc(sem("gla_x"), 1)
            act.wait_ge(*at("gla_x", GH + 1))
            nc.scalar.activation(flat(GD), flat(GD), ACT.Exp, scale=-1.0).then_inc(sem("gla_x"), 1)
            act.wait_ge(*at("gla_x", GH + 2))
            nc.scalar.activation(flat(GD), flat(GD), ACT.Ln, bias=1.0).then_inc(sem("gla_x"), 1)
            for v in range(6):
                act.wait_ge(*at("gla_v", v + 1))
                half, t = v // 3, v % 3
                n = P if t < 2 else GCH
                nc.scalar.activation(GV[0:n, t, half * 512:(half + 1) * 512], bank[5 + v % 2][0:n, :], ACT.Copy)\
                    .then_inc(sem("gla_v_read"), 1)
                if 1 <= v < 5:
                    i = v - 1
                    src, scale = [(GD, 1 / 16), (GD, -1 / 16), (GB, 1 / 16), (GD, 1 / 16)][i]
                    act.wait_ge(*at("gla_diff", [1, 1, 1, 2][i]))
                    if i >= 1:
                        act.wait_ge(*at("gla_scaled", i))
                    nc.scalar.activation(flat(GE), flat(src), ACT.Exp, scale=scale).then_inc(sem("gla_exp"), 1)
            last = chunks(GB)[:, :, GCH - 1]
            nc.scalar.activation(flat(GDEC), last, ACT.Exp, scale=1 / 16).then_inc(sem("gla_decay"), 1)
            act.wait_ge(*at("gla_scores", 1))
            nc.scalar.activation(view(HB, 0, 512), bank[7][:, :], ACT.Copy).then_inc(sem("gla_sc"), 1)
            for t in range(2):
                act.wait_ge(*at("gla_kt", t + 1))
                nc.scalar.activation(view(BIG, 6400 + 512 * t, 512), bank[4 if t else 0][:, :], ACT.Copy)\
                    .then_inc(sem("gla_kt_read"), 1)

            def gate(i):
                act.wait_ge(*at("gla_r", i + 1))
                nc.scalar.activation(GR[:, i, :], bank[[1, 6][i % 2]][:, 0:SEQ], ACT.Silu)\
                    .then_inc(sem("gla_r_read"), 1)

            for c in range(1, NCH):
                gate(2 * c - 2)
                act.wait_ge(*at("gla_o", c))
                nc.scalar.activation(GO[:, :, (c - 1) * GCH:c * GCH], view(bank[0], 0, KT, GCH), ACT.Copy)\
                    .then_inc(sem("gla_o_read"), 1)
                gate(2 * c - 1)
            for s in range(2):
                act.wait_ge(*at("gla_centred", 2 * s + 2))
                nc.scalar.activation(GSQ[:, 4 * s:4 * s + 4, :], GO[:, 4 * s:4 * s + 4, :], ACT.Square)\
                    .then_inc(sem("gla_sq"), 1)
            act.wait_ge(*at("gla_var", 2))
            nc.scalar.activation(flat(GST), flat(GST), ACT.Sqrt).then_inc(sem("gla_std"), 1)

        def gla_pool(pool):
            pool.wait_ge(*at("gla_sc", 1))
            for lo in (0, GCH):
                s = view(HB, 0, 8, GCH)[lo:lo + GCH]
                nc.gpsimd.affine_select(out=s, in_=s, compare_op=ALU.is_ge, fill=0.0, base=0,
                                        pattern=[[0, 8], [1, GCH]], channel_multiplier=-1)\
                    .then_inc(sem("gla_masked"), 1)

        def gla_dve(dve, link):
            V = nc.vector
            dve.wait_ge(*at("gla_x", GH + 3))
            link(V.scalar_tensor_tensor(flat(GE), flat(GE), 0.0, flat(GD), ALU.min, ALU.subtract))
            link(V.memset(GE[:, :, 0:PADT], 0.0))
            link(V.memset(flat(GD), 1.0))
            link(V.memset(chunks(GD)[:, :, 0:1], 0.0))
            link(V.tensor_tensor_scan(flat(GB), flat(GD), flat(GE), 0.0, ALU.mult, ALU.add))
            V.tensor_tensor(chunks(GD), chunks(GB), at_chunk(GB, GCH // 2 - 1), ALU.subtract)\
                .then_inc(sem("gla_diff"), 1)
            dve.wait_ge(*at("gla_read", 8))
            for i, (dst, src) in enumerate([(GQ1, GQ), (GK1, GK), (GQ, GQ), (GK, GK)]):
                dve.wait_ge(*at("gla_exp", i + 1))
                if i == 2:
                    V.tensor_tensor(chunks(GD), at_chunk(GB, GCH - 1), chunks(GB), ALU.subtract)\
                        .then_inc(sem("gla_diff"), 1)
                V.tensor_tensor(flat(dst), flat(src), flat(GE), ALU.mult).then_inc(sem("gla_scaled"), 1)
            dve.wait_ge(*at("gla_decay", 1))
            for c in range(NCH - 1):
                dve.wait_ge(*at("gla_kv", c + 1))
                if c >= 1:
                    dve.wait_ge(*at("gla_state", GH * c))
                for h in range(GH):
                    kv = bank[2 + h // 2][:, (h % 2) * GDV:(h % 2 + 1) * GDV]
                    if c == 0:
                        V.tensor_copy(GS[:, h, :], kv).then_inc(sem("gla_state"), 1)
                    else:
                        V.scalar_tensor_tensor(GS[:, h, :], GS[:, h, :], GDEC[:, h, c:c + 1], kv,
                                               ALU.mult, ALU.add).then_inc(sem("gla_state"), 1)
            dve.wait_ge(*at("gla_mean", 1))
            for h in range(GH):
                mean = bank[4 + h // 2][:, (h % 2) * SEQ:(h % 2 + 1) * SEQ].unsqueeze(1).to_broadcast([P, 2, SEQ])
                oh = GO[:, 2 * h:2 * h + 2, :]
                V.scalar_tensor_tensor(oh, mean, -1.0 / GDV, oh, ALU.mult, ALU.add)\
                    .then_inc(sem("gla_centred"), 1)
            dve.wait_ge(*at("gla_sum", 1))
            for s in range(2):
                V.tensor_scalar(view(HB, 2048 + 512 * s, 512), bank[6 + s][:, :], 1.0 / GDV, LN_EPS,
                                ALU.mult, ALU.add).then_inc(sem("gla_var"), 1)
            dve.wait_ge(*at("gla_std", 1))
            link(V.reciprocal(flat(GST), flat(GST)))
            dve.wait_ge(*at("gla_centred", 4))
            for i in range(8):
                link(V.scalar_tensor_tensor(GO[:, i, :], GO[:, i, :], par("gla_ng", i, 1), GST[:, i // 2, :],
                                            ALU.mult, ALU.mult))
            dve.wait_ge(*at("gla_r_read", 8))
            for i in range(8):
                V.tensor_tensor(GO[:, i, :], GO[:, i, :], GR[:, i, :], ALU.mult)\
                    .then_inc(sem("gla_gated"), 1)
            add_dve(dve, "mix3", X0, SEQ, [2, 3])

        XTOK = view(BIG, 0, 2, D)
        YS = view(BIG, 2048, D)
        YACC = view(Y, 0, KT, SEQ)
        GW = view(HB, 0, SEQ)
        SEL = view(HB, 256, 2, P)
        SELG = view(HB, 512, 2, P)
        IOTA = view(HB, 768, P)
        SILU = view(HB, 896, 2, 256)
        AS = view(HB, 1408, 2, 256)
        POS = view(SCR, 1024, 2, 16)
        GATE = view(SCR, 1056, 2, 16)
        U1, U2 = view(SCR, 0, 8, 8), view(SCR, 64, 8, 8)
        LT = view(SCR, 128, 8, 8)
        LG, EX, RK, PM, CN, OV, PX = (view(SCR, 192 + 16 * i, 2, 8) for i in range(7))
        SML = view(SCR, 320, 64)
        TRI = view(SCR, 512, P)
        ITAB = sb("ITAB", [1, 16], I32)
        FTAB = view(SCR, 384, 16)
        M3 = view(SCR, 448, 3, 8)
        IOE = view(SCR, 480, 8)

        def count(eng):
            return eng.value_load(ITAB[0:1, 12:13], min_val=NE, max_val=ITEMS)

        slot0 = MOE0 % RING
        came = [16 * sum(1 for e in plan if e[1] == s) for s in range(RING)]

        def arrival(i, q):
            slot = (slot0 + q) % RING
            return f"weights_in{slot}", i * (16 * MOE_CH // RING) + (came[slot] + 16 * (q // RING + 1)), slot

        def moe_sync(sp, previous):
            src = A["moe"]
            for q in range(MOE_CH):
                name, _, slot = arrival(0, q)
                if q < RING:
                    sp.wait_ge(*at(previous[slot][0], previous[slot][1]))
                else:
                    sp.wait_ge(*at("moe_lo", 2 * (q - RING) + 2))
                sp.dma_start(ring[:, slot, :], src[q, :, :]).then_inc(sem(name), 16)

            def first(e, after):
                name, _, slot = arrival(0, 0)
                chunk = src[bass.ds(e * MOE_CH, 1), :, :].rearrange("a p n -> p (a n)")
                sp.wait_ge(*at("moe_lo", after))
                sp.dma_start(ring[:, slot, :], chunk).then_inc(sem(name), 16)

            first(1, HALVES + 2 - 2 * RING)
            sp.wait_ge(*at("items_ready", 1))
            n = count(sp)
            with sp.Fori(1, n) as i:
                e = sp.value_load(ITAB[0:1, bass.ds(i, 1)], min_val=0, max_val=NE - 1)
                for q in range(1, MOE_CH):
                    name, _, slot = arrival(0, q)
                    chunk = src[bass.ds(e * MOE_CH + q, 1), :, :].rearrange("a p n -> p (a n)")
                    sp.wait_ge(*at("moe_lo", HALVES * i + (2 * (q - RING) + 2)))
                    sp.dma_start(ring[:, slot, :], chunk).then_inc(sem(name), 16)
                e_next = sp.value_load(ITAB[0:1, bass.ds(i + 1, 1)], min_val=0, max_val=NE - 1)
                first(e_next, HALVES * i + (HALVES + 2 - 2 * RING))

        def moe_pe(pe):
            pe.wait_ge(*at("ln2_out", KT))
            for t in range(2):
                for k in range(KT):
                    mm = nc.tensor.matmul(bank[4][:, 8 * t:8 * t + 8], xs[:, k, t * P:(t + 1) * P],
                                          par("router", NE * k, NE), start=(k == 0), stop=(k == KT - 1))
            mm.then_inc(sem("moe_logits"), 1)
            for i in range(4):
                t, q = i // 2, i % 2
                for f in range(4):
                    mm = nc.tensor.transpose(bank[i][:, f * P:(f + 1) * P],
                                             xs[:, 4 * q + f, t * P:(t + 1) * P], IDENT[:, :])
                mm.then_inc(sem("moe_xt"), 1)
            pe.wait_ge(*at("moe_picked", 1))
            nc.tensor.matmul(bank[5][:, 0:8], TRI, RK[:, 0, :], start=True, stop=True)
            nc.tensor.matmul(bank[5][:, 8:16], TRI, RK[:, 1, :], start=True, stop=False)
            nc.tensor.matmul(bank[5][:, 8:16], ONES[:, :], RK[:, 0, :], start=False, stop=True)
            nc.tensor.matmul(bank[5][:, 16:24], ONES[:, :], RK[:, 0, :], start=True, stop=False)
            nc.tensor.matmul(bank[5][:, 16:24], ONES[:, :], RK[:, 1, :], start=False, stop=True)\
                .then_inc(sem("moe_before"), 1)

            def gather(i):
                pe.wait_ge(*at("moe_sel", i + 1))
                for f in range(KT):
                    for t in range(2):
                        mm = nc.tensor.matmul(bank[f // 4][:, (f % 4) * P:(f % 4 + 1) * P],
                                              XTOK[:, t, f * P:(f + 1) * P], SEL[:, t, :],
                                              start=(t == 0), stop=(t == 1))
                    if f % 4 == 3:
                        mm.then_inc(sem("moe_gathered"), 1)

            pe.wait_ge(*at("moe_xt_read", 4))
            gather(0)
            pe.wait_ge(*at("items_ready", 1))
            n = count(pe)
            def halves(i, h, products):
                pe.wait_ge(*at("moe_lo", HALVES * i + (h + 1)))
                for out, (xh, xl), o, start, stop in products:
                    wh, wl = WHI[:, h % SPLIT, o:o + 512], WLO[:, h % SPLIT, o:o + 512]
                    nc.tensor.matmul(out, xh, wh, start=start, stop=False)
                    nc.tensor.matmul(out, xh, wl, start=False, stop=False)
                    mm = nc.tensor.matmul(out, xl, wh, start=False, stop=stop)
                mm.then_inc(sem("moe_half"), 1)

            with pe.Fori(0, n) as i:
                def turn(c):
                    pe.wait_ge(*at("moe_act", MOE_UP * i + (c + 1)))
                    if c >= 2:
                        pe.wait_ge(*at("moe_alo", MOE_UP * i + (c - 1)))
                    else:
                        pe.wait_ge(*at("moe_added", 4 * i + 4))
                    for q in range(2):
                        mm = nc.tensor.transpose(bank[3 + c % 2][:, q * P:(q + 1) * P],
                                                 AS[:, c % 2, q * P:(q + 1) * P], IDENT[:, :])
                    mm.then_inc(sem("moe_turned"), 1)

                pe.wait_ge(*at("moe_hgl", 2 * i + 2))
                for q, (kind, c) in enumerate(MOE_ORDER):
                    if kind == "up":
                        if c >= 2:
                            pe.wait_ge(*at("moe_act", MOE_UP * i + (c - 1)))
                        for h in range(2):
                            ks = range(4 * h, 4 * h + 4)
                            halves(i, 2 * q + h, [(bank[c % 2][:, :], (HGH[:, k, :], HGL[:, k, :]), (k % 4) * 512,
                                                   k == 0, k == KT - 1) for k in ks])
                        if c >= 1:
                            turn(c - 1)
                        continue
                    if c == MOE_DOWN - 1:
                        for t in range(2):
                            mm = nc.tensor.transpose(bank[2][:, t * P:(t + 1) * P], SELG[:, t, :], IDENT[:, :])
                        mm.then_inc(sem("moe_gt"), 1)
                        turn(MOE_UP - 1)
                    pe.wait_ge(*at("moe_alo", MOE_UP * i + 2 * (c + 1)))
                    for h in range(2):
                        halves(i, 2 * q + h, [
                            (bank[6 + n2][:, :], (AHI[:, c % 2, 2 * h + k, :], ALO[:, c % 2, 2 * h + k, :]),
                             k * D + n2 * 512, c == 0 and h == 0 and k == 0,
                             c == MOE_DOWN - 1 and h == 1 and k == 1) for k in range(2) for n2 in range(2)])
                gather(i + 1)
                pe.wait_ge(*at("moe_gw", i + 1))
                pe.wait_ge(*at("moe_ys", 2 * i + 2))
                for f in range(KT):
                    mm = nc.tensor.matmul(bank[2 + f // 2][:, (f % 2) * SEQ:(f % 2 + 1) * SEQ],
                                          YS[:, f * P:(f + 1) * P], GW, start=True, stop=True)
                    if f % 2 == 1:
                        mm.then_inc(sem("moe_spread"), 1)

        def moe_act(act):
            act.wait_ge(*at("moe_max", 1))
            nc.scalar.activation(view(SCR, 208, 16), view(SCR, 208, 16), ACT.Exp).then_inc(sem("moe_exp"), 1)
            for i in range(4):
                act.wait_ge(*at("moe_xt", i + 1))
                nc.scalar.activation(XTOK[:, i // 2, (i % 2) * 512:(i % 2 + 1) * 512], bank[i][:, :], ACT.Copy)\
                    .then_inc(sem("moe_xt_read"), 1)

            def gathered(i):
                for b in range(2):
                    act.wait_ge(*at("moe_gathered", 2 * i + (b + 1)))
                    nc.scalar.activation(flat(HGH[:, 4 * b:4 * b + 4, :]), bank[b][:, :], ACT.Copy)\
                        .then_inc(sem("moe_hgh"), 1)

            def high(i, h):
                name, value, slot = arrival(i, h // 2)
                if h % 2 == 0:
                    act.wait_ge(*at(name, value))
                if h > 2:
                    act.wait_ge(*at("moe_half", HALVES * i + (h - 2)))
                nc.scalar.activation(WHI[:, h % SPLIT, :], ring[:, slot, (h % 2) * HALF:(h % 2 + 1) * HALF],
                                     ACT.Copy).then_inc(sem("moe_hi"), 1)

            high(0, 0)
            high(0, 1)
            gathered(0)
            act.wait_ge(*at("items_ready", 1))
            n = count(act)
            with act.Fori(0, n) as i:
                def turned(c):
                    act.wait_ge(*at("moe_turned", MOE_UP * i + (c + 1)))
                    nc.scalar.activation(flat(AHI[:, (c // 2) % 2, 2 * (c % 2):2 * (c % 2) + 2, :]),
                                         bank[3 + c % 2][:, 0:2 * P], ACT.Copy).then_inc(sem("moe_ahi"), 1)

                for q, (kind, c) in enumerate(MOE_ORDER):
                    if (kind, c) == ("down", MOE_DOWN - 1):
                        act.wait_ge(*at("moe_gt", i + 1))
                        nc.scalar.activation(GW, bank[2][:, 0:SEQ], ACT.Copy).then_inc(sem("moe_gw"), 1)
                        turned(MOE_UP - 1)
                    high(i, 2 * q + 2)
                    high(i, 2 * q + 3)
                    if kind == "up":
                        act.wait_ge(*at("moe_half", HALVES * i + (2 * q + 2)))
                        if c >= 2:
                            act.wait_ge(*at("moe_act", MOE_UP * i + (c - 1)))
                        nc.scalar.activation(SILU[:, c % 2, :], bank[c % 2][:, 0:256], ACT.Silu)\
                            .then_inc(sem("moe_silu"), 1)
                        if c >= 1:
                            turned(c - 1)
                act.wait_ge(*at("moe_half", HALVES * i + HALVES))
                for half in range(2):
                    nc.scalar.activation(YS[:, half * 512:(half + 1) * 512], bank[6 + half][:, :], ACT.Copy)\
                        .then_inc(sem("moe_ys"), 1)
                gathered(i + 1)

        def moe_pool(pool):
            pool.wait_ge(*at("ln2_out", KT))
            nc.gpsimd.memset(TRI, 1.0).then_inc(sem("moe_const"), 1)
            nc.gpsimd.memset(flat(LT), 1.0).then_inc(sem("moe_const"), 1)
            pool.wait_ge(*at("moe_const", 2))
            nc.gpsimd.affine_select(out=TRI, in_=TRI, compare_op=ALU.is_gt, fill=0.0, base=0,
                                    pattern=[[1, P]], channel_multiplier=-1).then_inc(sem("moe_const"), 1)
            nc.gpsimd.affine_select(out=LT, in_=LT, compare_op=ALU.is_gt, fill=0.0, base=0,
                                    pattern=[[1, 8], [-1, 8]], channel_multiplier=0).then_inc(sem("moe_const"), 1)
            nc.gpsimd.iota(IOTA, [[1, P]], base=0, channel_multiplier=0,
                           allow_small_or_imprecise_dtypes=True).then_inc(sem("moe_const"), 1)
            nc.gpsimd.iota(IOE, [[1, 8]], base=0, channel_multiplier=0,
                           allow_small_or_imprecise_dtypes=True).then_inc(sem("moe_const"), 1)
            for q in range(4):
                nc.gpsimd.memset(view(Y, 512 * q, 512), 0.0).then_inc(sem("moe_added"), 1)

        def moe_dve(dve, link):
            V = nc.vector
            dve.wait_ge(*at("moe_logits", 1))
            link(V.tensor_copy(flat(LG), bank[4][:, 0:16]))
            dve.wait_ge(*at("moe_const", 6))
            for t in range(2):
                le = LG[:, t, :].unsqueeze(2).to_broadcast([P, 8, 8])
                lj = LG[:, t, :].unsqueeze(1).to_broadcast([P, 8, 8])
                link(V.tensor_tensor(U1, lj, le, ALU.is_gt))
                link(V.tensor_tensor(U2, lj, le, ALU.is_equal))
                link(V.tensor_tensor(U2, U2, LT, ALU.mult))
                link(V.tensor_tensor(U1, U1, U2, ALU.add))
                link(V.reduce_sum(RK[:, t, :], U1, AX.X))
                link(V.reduce_max(SML[:, t:t + 1], LG[:, t, :], AX.X))
                a = V.tensor_scalar(EX[:, t, :], LG[:, t, :], SML[:, t:t + 1], None, ALU.subtract)
                if t == 0:
                    link(a)
                else:
                    a.then_inc(sem("moe_max"), 1)
            V.tensor_scalar(flat(RK), flat(RK), 2.0, None, ALU.is_lt).then_inc(sem("moe_picked"), 1)
            dve.wait_ge(*at("moe_picked", 1))
            dve.wait_ge(*at("moe_exp", 1))
            link(V.tensor_tensor(flat(EX), flat(EX), flat(RK), ALU.mult))
            link(V.reduce_sum(SML[:, 2:4], EX, AX.X))
            link(V.reciprocal(SML[:, 2:4], SML[:, 2:4]))
            for t in range(2):
                V.tensor_scalar(GATE[:, t, 0:8], EX[:, t, :], SML[:, 2 + t:3 + t], None, ALU.mult)\
                    .then_inc(sem("moe_gates"), 1)
            dve.wait_ge(*at("moe_before", 1))
            link(V.scalar_tensor_tensor(flat(PX), bank[5][:, 0:16], 1.0, flat(RK), ALU.add, ALU.mult))
            link(V.memset(view(SCR, 1024, 32), -1.0))
            link(V.tensor_scalar(POS[:, :, 0:8], PX, -1.0, None, ALU.add))
            link(V.tensor_scalar(OV[:, 0, :], bank[5][:, 16:24], 128.5, None, ALU.is_gt))
            link(V.memset(CN[:, 0, :], 1.0))
            link(V.tensor_tensor_scan(CN[:, 1, :], CN[:, 0, :], OV[:, 0, :], 0.0, ALU.mult, ALU.add))
            for j in range(OVER):
                link(V.scalar_tensor_tensor(M3[:, j, :], CN[:, 1, :], float(j + 1), OV[:, 0, :],
                                            ALU.is_equal, ALU.mult))
            dve.wait_ge(*at("moe_gates", 2))
            for j in range(OVER):
                m = M3[:, j, :].unsqueeze(1).to_broadcast([P, 2, 8])
                link(V.tensor_tensor(PM, POS[:, :, 0:8], m, ALU.mult))
                link(V.reduce_sum(POS[:, :, 8 + j], PM, AX.X))
                link(V.tensor_scalar(POS[:, :, 8 + j], POS[:, :, 8 + j], -128.0, None, ALU.add))
                link(V.tensor_tensor(PM, GATE[:, :, 0:8], m, ALU.mult))
                link(V.reduce_sum(GATE[:, :, 8 + j], PM, AX.X))
            link(V.memset(GATE[:, :, 11:12], 0.0))
            link(V.tensor_copy(FTAB[:, 0:8], IOE))
            m = M3
            ioe = IOE.unsqueeze(1).to_broadcast([P, 3, 8])
            link(V.tensor_tensor(M3, M3, ioe, ALU.mult))
            link(V.reduce_sum(FTAB[:, 8:11], M3, AX.X))
            link(V.memset(FTAB[:, 11:12], 0.0))
            link(V.tensor_scalar(FTAB[:, 12:13], CN[:, 1, 7:8], float(NE), None, ALU.add))
            V.tensor_copy(ITAB[0:1, 0:13], FTAB[0:1, 0:13]).then_inc(sem("items_ready"), 1)
            dve.wait_ge(*at("items_ready", 1))

            def select(i, col):
                for t in range(2):
                    a = V.tensor_scalar(SEL[:, t, :], IOTA, POS[:, t, col], None, ALU.is_equal)
                a.then_inc(sem("moe_sel"), 1)

            def select_gate(i, col):
                for t in range(2):
                    a = V.tensor_scalar(SELG[:, t, :], IOTA, POS[:, t, col], GATE[:, t, col],
                                        ALU.is_equal, ALU.mult)
                a.then_inc(sem("moe_selg"), 1)

            def low(i, h):
                slot = arrival(0, h // 2)[2]
                dve.wait_ge(*at("moe_hi", HALVES * i + (h + 1)))
                V.tensor_tensor(WLO[:, h % SPLIT, :], ring[:, slot, (h % 2) * HALF:(h % 2 + 1) * HALF],
                                WHI[:, h % SPLIT, :].bitcast(F32), ALU.subtract).then_inc(sem("moe_lo"), 1)

            def gathered(i):
                for b in range(2):
                    dve.wait_ge(*at("moe_hgh", 2 * i + (b + 1)))
                    V.tensor_tensor(flat(HGL[:, 4 * b:4 * b + 4, :]), bank[b][:, :],
                                    flat(HGH[:, 4 * b:4 * b + 4, :]).bitcast(F32), ALU.subtract)\
                        .then_inc(sem("moe_hgl"), 1)

            select(0, slice(0, 1))
            select_gate(0, slice(0, 1))
            low(0, 0)
            low(0, 1)
            gathered(0)
            n = count(dve)
            with dve.Fori(0, n) as i:
                def turned(c):
                    rows = slice(2 * (c % 2), 2 * (c % 2) + 2)
                    dve.wait_ge(*at("moe_ahi", MOE_UP * i + (c + 1)))
                    V.tensor_tensor(flat(ALO[:, (c // 2) % 2, rows, :]), bank[3 + c % 2][:, 0:2 * P],
                                    flat(AHI[:, (c // 2) % 2, rows, :]).bitcast(F32), ALU.subtract)\
                        .then_inc(sem("moe_alo"), 1)

                nxt = bass.ds(i + 1, 1)
                for q, (kind, c) in enumerate(MOE_ORDER):
                    if (kind, c) == ("down", MOE_DOWN - 1):
                        dve.wait_ge(*at("moe_gathered", 2 * i + 2))
                        select(i + 1, nxt)
                        dve.wait_ge(*at("moe_gt", i + 1))
                        select_gate(i + 1, nxt)
                        turned(MOE_UP - 1)
                    low(i, 2 * q + 2)
                    low(i, 2 * q + 3)
                    if kind == "up":
                        dve.wait_ge(*at("moe_silu", MOE_UP * i + (c + 1)))
                        if c >= 2:
                            dve.wait_ge(*at("moe_turned", MOE_UP * i + (c - 1)))
                        V.tensor_tensor(AS[:, c % 2, :], SILU[:, c % 2, :], bank[c % 2][:, 256:512], ALU.mult)\
                            .then_inc(sem("moe_act"), 1)
                        if c >= 1:
                            turned(c - 1)
                gathered(i + 1)
                for q in range(4):
                    acc = view(Y, 512 * q, 512)
                    dve.wait_ge(*at("moe_spread", 4 * i + (q + 1)))
                    dve.wait_ge(*at("moe_added", 4 * i + (q + 1)))
                    V.tensor_tensor(acc, acc, bank[2 + q][:, :], ALU.add).then_inc(sem("moe_added"), 1)
            dve.wait_ge(*at("moe_added", n * 4 + 4))
            nc.vector.scalar_tensor_tensor(xs, xs, ALPHA, YACC, ALU.mult, ALU.add).then_inc(sem("moe_res"), KT)

        def out_sync(sp):
            sp.wait_ge(*at("ln3_out", KT))
            sp.dma_start(OUT, xs).then_inc(sem("out_stored"), 16)
            sp.wait_ge(*at("out_stored", 16))

        block = ctx.enter_context(nc.Block())

        @block.sync
        def _(sp):
            previous = {}
            for src, slot, rows, words, used, value in plan:
                if slot in previous:
                    sp.wait_ge(*at(previous[slot][0], previous[slot][1]))
                previous[slot] = (used, value)
                sp.dma_start(ring[0:rows, slot, 0:words], src).then_inc(sem(f"weights_in{slot}"), 16)
            moe_sync(sp, previous)
            out_sync(sp)

        @block.tensor
        def _(pe):
            pe.wait_ge(*at("silu_c", 1))
            pe.wait_ge(*at("consts", 2))
            direct_pe(pe, 0)
            rms_pe(pe, "n0x", SEQ, bank[4])
            rms_pe(pe, "n0c", SEQ, bank[5])
            for job in mod_jobs[:2]:
                mod_pe(pe, *job)
            direct_pe(pe, 2)
            for job in mod_jobs[2:4]:
                mod_pe(pe, *job)
            pe.wait_ge(*at("tables_in", 48))
            attn_pe(pe)
            rms_pe(pe, "n0f", SEQ, bank[7])
            ffn_pe(pe, 0)
            rms_pe(pe, "n1x", SEQ, bank[7])
            four_pe(pe)
            rms_pe(pe, "n1f", SEQ, bank[7])
            ffn_pe(pe, 1)
            rg_pe(pe)
            ln_pe(pe, "ln0", M0, "mix2_read")
            swiglu_pe(pe)
            ln_pe(pe, "ln1", M0, "ffn2_read")
            gla_pe(pe)
            ln_pe(pe, "ln2", X0, "mix3_read")
            moe_pe(pe)
            ln_pe(pe, "ln3", X0, "moe_res", (6, 7))

        @block.scalar
        def _(act):
            tin = sem("tables_in")
            act.dma_start(PAR[:, :], A["params"]).then_inc(sem("params_in"), 16)
            act.dma_start(xs, A["xT"]).then_inc(sem("x_in"), 16)
            act.dma_start(CTXB, A["ctxT"]).then_inc(sem("x_in"), 16)
            act.dma_start(X[:, :, M0:X0], A["metaT"]).then_inc(sem("meta_in"), 16)
            act.dma_start(PROT, A["prot"]).then_inc(tin, 16)
            act.dma_start(IDENT[:, :], A["ident"]).then_inc(tin, 16)
            act.dma_start(MASK, A["mask"]).then_inc(tin, 16)
            act.wait_ge(*at("params_in", 16))
            nc.scalar.activation(par("cvec"), par("cvec"), ACT.Silu).then_inc(sem("silu_c"), 1)
            squares_act(act, "n0x", xs, SEQ, ("x_in", 32, 0))
            squares_act(act, "n0c", CTXB, CTX, ("n0x_sum", 1, 0))
            root_act(act, "n0x", SEQ)
            root_act(act, "n0c", CTX)
            act.dma_start(ROPE, A["rope"]).then_inc(sem("rope_in"), 16)
            shift_act(act, "n0x", shift(0, 0), HCAT[:, :, CTX:])
            shift_act(act, "n0c", shift(0, 0, 1), HCAT[:, :, 0:CTX])
            attn_act(act)
            rms_act(act, "n0f", xs, SEQ, ("n0y_res", 1, 1), shift(0, 3), H, HHI)
            ffn_act(act, 0)
            act.dma_start(DFTD, A["dftd"]).then_inc(sem("dft_in"), 16)
            act.dma_start(DFTL, A["dftl"]).then_inc(sem("dft_in"), 16)
            rms_act(act, "n1x", xs, SEQ, ("n0g_res", 1, 1), shift(1, 0), H)
            four_act(act)
            rms_act(act, "n1f", xs, SEQ, ("n1y_res", 1, 1), shift(1, 3), H, HHI)
            ffn_act(act, 1)
            rg_act(act)
            for j in range(PAIRS):
                high(act, "ffn_in", "ffn2", j, FF2T)
            ln_act(act, "ln0", M0, 0)
            swiglu_act(act)
            ln_act(act, "ln1", M0, 1)
            gla_act(act)
            ln_act(act, "ln2", X0, 2)
            moe_act(act)
            ln_act(act, "ln3", X0, 3)

        @block.gpsimd
        def _(pool):
            nc.gpsimd.memset(ONES[:, :], 1.0).then_inc(sem("consts"), 1)
            nc.gpsimd.memset(X[:, :, 0:PADT], 0.0).then_inc(sem("consts"), 1)
            gla_pool(pool)
            moe_pool(pool)

        @block.vector
        def _(dve):
            chain = [0]

            def link(ins):
                chain[0] += 1
                ins.then_inc(sem("dve_chain"), 1)
                dve.wait_ge(*at("dve_chain", chain[0]))

            dve.wait_ge(*at("params_in", 16))
            dve.wait_ge(*at("silu_c", 1))
            for job in mod_jobs[:2]:
                mod_sum(dve, *job)
            root_dve(dve, link, "n0x", SEQ, bank[4])
            root_dve(dve, link, "n0c", CTX, bank[5])
            for job in mod_jobs[:2]:
                mod_store(dve, *job)
            for job in mod_jobs[2:4]:
                mod_sum(dve, *job)
            direct_store(dve, 0)
            direct_store(dve, 2)
            for job in mod_jobs[2:4]:
                mod_store(dve, *job)
            mod_stored(dve, 4)
            dve.wait_ge(*at("direct_stored", 2))
            coef_dve(0, 0, 1, 0, 0, 1.0)
            link(coef_dve(0, 1, 1, 1, 0, 1.0))
            scale_dve(dve, "n0x", xs, SEQ, lambda j: COEF[:, 0, 0, j:j + 1], HCAT[:, :, CTX:])
            scale_dve(dve, "n0c", CTXB, CTX, lambda j: COEF[:, 0, 1, j:j + 1], HCAT[:, :, 0:CTX])
            attn_dve(dve, link)
            split_start(dve, low, 0)
            res_dve(dve, link, "n0y", bank[7], 0, 2)
            rms_dve(dve, link, "n0f", xs, SEQ, bank[7], lambda j: COEF[:, 0, 3, j:j + 1], H)
            lo_dve(dve, 0)
            ffn_dve(dve, 0)
            res_dve(dve, link, "n0g", bank[7], 0, 4)
            coef_dve(1, 0, 1, 0, 0, 1.0)
            coef_dve(1, 2, 2, 0, 1, 0.0)
            link(coef_dve(1, 3, 4, 0, 2, 1.0))
            rms_dve(dve, link, "n1x", xs, SEQ, bank[7], lambda j: COEF[:, 1, 0, j:j + 1], H)
            split_start(dve, low, 1)
            res_dve(dve, link, "n1y", bank[7], 1, 2)
            rms_dve(dve, link, "n1f", xs, SEQ, bank[7], lambda j: COEF[:, 1, 3, j:j + 1], H)
            lo_dve(dve, 1)
            ffn_dve(dve, 1)
            link(coef_dve(1, 4, 5, 0, 3, 0.0))
            res_dve(dve, link, "n1g", bank[7], 1, 4)
            rg_dve(dve, link)
            ln_dve(dve, link, "ln0", M0)
            swiglu_dve(dve)
            ln_dve(dve, link, "ln1", M0)
            gla_dve(dve, link)
            ln_dve(dve, link, "ln2", X0)
            moe_dve(dve, link)
            ln_dve(dve, link, "ln3", X0, (6, 7))


def _feature_major(a):
    return np.ascontiguousarray(a.T.reshape(-1, P, a.shape[0]).transpose(1, 0, 2))


def _columns(v, tile=P):
    c = v.reshape(-1, tile).T
    return np.concatenate([c, np.zeros((P - tile, c.shape[1]), v.dtype)]) if tile < P else c


def _blocks(w):
    return w.reshape(w.shape[0] // P, P, w.shape[1] // P, P).transpose(0, 2, 1, 3)


def _chunked(pieces):
    n, p, w = pieces.shape
    per = CHUNK // w
    chunks = -(-n // per)
    out = np.zeros((chunks, p, CHUNK), pieces.dtype)
    for c in range(chunks):
        got = pieces[c * per:(c + 1) * per]
        out[c, :, :got.shape[0] * w] = got.transpose(1, 0, 2).reshape(p, -1)
    return out


def _by_tile(w):
    return _chunked(_blocks(w).transpose(1, 0, 2, 3).reshape(-1, P, P))


def _pairs(w):
    b = _blocks(w)
    k, n = b.shape[:2]
    return _chunked(b.reshape(k, 2, n // 2, P, P).transpose(2, 1, 0, 3, 4).reshape(-1, P, P))


def _rows(w):
    return np.ascontiguousarray(w.reshape(KT, P, -1, 512).transpose(2, 1, 0, 3)).reshape(-1, P, CHUNK)


def _constants():
    f = np.float32
    n_freq = HD // 4
    inv = f(10000.0) ** (-np.arange(n_freq, dtype=f) / f(n_freq))
    tok = np.arange(SEQ)
    ang = np.stack([(tok // 64).astype(f)[:, None] * inv, (tok % 64).astype(f)[:, None] * inv])
    ang = np.repeat(ang[:, None], 2, axis=1).transpose(0, 1, 3, 2).reshape(HD, SEQ)
    rope = np.stack([np.cos(ang), np.sin(ang)], axis=1).astype(f)
    prot = np.zeros((HD, HD), f)
    for a in range(2):
        for j in range(n_freq):
            x1, x2 = a * 64 + j, a * 64 + n_freq + j
            prot[x2, x1] = -1.0
            prot[x1, x2] = 1.0
    q, k = np.arange(SEQ)[:, None], np.arange(SEQ)[None, :]
    mask = np.where(np.abs(q - k) <= 128, 0.0, -1e30).astype(f).reshape(2, P, SEQ).transpose(1, 0, 2)
    n = np.arange(256)
    a = 2 * np.pi * ((n[:, None] * n[None, :]) % 256) / 256
    c, s = np.cos(a), np.sin(a)
    dftd = np.concatenate([c, s], axis=1).reshape(2, P, 512).transpose(1, 0, 2)
    dftl = np.stack([c, -s]).reshape(2, 2, P, 256).transpose(2, 0, 1, 3) / 256
    return {"rope": rope, "prot": prot, "ident": np.eye(P, dtype=f), "mask": np.ascontiguousarray(mask),
            "dftd": np.ascontiguousarray(dftd, dtype=f), "dftl": np.ascontiguousarray(dftl, dtype=f)}


def layout(i):
    i = {k: np.asarray(v) for k, v in i.items()}
    out = _constants()
    out["xT"] = _feature_major(i["x"][0])
    out["ctxT"] = _feature_major(i["ctx"][0])
    out["metaT"] = _feature_major(i["meta_tokens_2"])
    for l in range(2):
        out[f"mod{l}"] = _rows(i["mod_w"][l])
        out[f"up{l}"] = _pairs(i["ffn_w_up"][l])
        out[f"down{l}"] = _by_tile(i["ffn_w_down"][l])
    w = i["attn_w_in"][0]
    q, kv = w[:, :1024], w[:, 1024:]
    keys = np.concatenate([kv[:, 0:256], kv[:, 512:768]], axis=1)
    vals = np.concatenate([kv[:, 256:512], kv[:, 768:1024]], axis=1)
    out["attn_in"] = np.concatenate([_by_tile(keys), _by_tile(q), _rows(vals)])
    out["attn_out"] = _by_tile(i["attn_w_out"][0])
    out["four_out"] = _by_tile(i["fourier_w_out"][0])
    w = i["rg_w_in_2"][0]
    w = np.concatenate([w[:, RGW:], w[:, :RGW]], axis=1)
    w = w.reshape(KT, P, 2 * RGN, RGT).transpose(2, 1, 0, 3).reshape(2 * RGN, P, KT * RGT)
    out["rg_in"] = _chunked(w)
    g = i["rg_w_gates_2"][0].reshape(2, RGB, 2, RGT, 2, RGT)
    g = g.transpose(1, 4, 0, 3, 2, 5).reshape(4 * RGB, RGT, 2 * RGT)
    out["rg_gates"] = _chunked(g)
    w = i["rg_w_out_2"][0].reshape(RGN, RGT, KT, P).transpose(2, 0, 1, 3).reshape(-1, RGT, P)
    out["rg_out"] = _chunked(w)
    out["ffn_in"] = _pairs(i["ffn_w_in_2"][0])
    out["ffn_out"] = _by_tile(i["ffn_w_out_2"][0])
    w = i["gla_w_in_2"][0]
    out["gla_in"] = np.concatenate([_by_tile(w[:, :1024]), _rows(w[:, 1024:2048]), _by_tile(w[:, 2048:3072])])
    out["gla_out"] = _by_tile(i["gla_w_out_2"][0])
    wi, wo = i["moe_w_in_2"][0], i["moe_w_out_2"][0]
    moe = np.empty((NE, MOE_CH, P, CHUNK), np.float32)
    ups = [q for q, (kind, _) in enumerate(MOE_ORDER) if kind == "up"]
    downs = [q for q, (kind, _) in enumerate(MOE_ORDER) if kind == "down"]
    moe[:, ups] = wi.reshape(NE, KT, P, 2, MOE_UP, 256).transpose(0, 4, 2, 1, 3, 5).reshape(NE, MOE_UP, P, CHUNK)
    moe[:, downs] = wo.reshape(NE, MOE_DOWN, 4, P, D).transpose(0, 1, 3, 2, 4).reshape(NE, MOE_DOWN, P, CHUNK)
    out["moe"] = moe.reshape(NE * MOE_CH, P, CHUNK)

    par = np.zeros((P, NPAR), np.float32)

    def put(name, a):
        at, n = PCOLS[name]
        assert a.shape[1] == n, (name, a.shape, n)
        par[:a.shape[0], at:at + n] = a

    put("cvec", np.stack([_columns(i["c"][0]), _columns(i["c_ctx"])], axis=2).reshape(P, -1))
    put("mod_b", _columns(i["mod_b"].reshape(-1)))
    put("norm_g", _columns(i["norm_g"].reshape(-1)))
    put("qg", i["q_norm_g"][0][:, None])
    put("kg", i["k_norm_g"][0][:, None])
    put("sink", np.broadcast_to(i["sink"], (P, 4)))
    for l in range(2):
        put(f"conv_w{l}", _columns(i["ffn_conv_w"][l].reshape(-1)))
        put(f"conv_b{l}", _columns(i["ffn_conv_b"][l]))
    put("ln_g", _columns(i["ln_gain_2"].reshape(-1)))
    put("ln_b", _columns(i["ln_bias_2"].reshape(-1)))
    put("rg_conv", _columns(i["rg_conv_w_2"][0].reshape(-1), RGT))
    put("rg_cb", _columns(i["rg_conv_b_2"][0], RGT))
    put("rg_gb", _columns(i["rg_b_gates_2"][0].reshape(-1), RGT))
    put("rg_lam", _columns(i["rg_lambda_2"][0], RGT))
    put("gla_bg", _columns(i["gla_b_gate_2"][0]))
    put("gla_ng", _columns(i["gla_norm_g_2"][0].reshape(-1)))
    put("router", i["moe_router_2"][0].reshape(KT, P, NE).transpose(1, 0, 2).reshape(P, -1))
    put("gla_wz", i["gla_w_in_2"][0][:, 3072:].reshape(KT, P, 16).transpose(1, 0, 2).reshape(P, -1))
    put("gla_wg", i["gla_w_gate_up_2"][0])
    out["params"] = par
    return out


def kernel(**inputs):
    import concourse.bacc as bacc
    from concourse.bass_utils import run_bass_kernel_spmd

    arrays = layout(inputs)
    nc = bacc.Bacc("TRN2", target_bir_lowering=False, num_devices=1)
    aps = {n: nc.dram_tensor(f"in_{n}", a.shape, F32, kind="ExternalInput").ap() for n, a in arrays.items()}
    out = nc.dram_tensor("out", (P, KT, SEQ), F32, kind="ExternalOutput").ap()
    block_program(nc, aps, out)
    r = run_bass_kernel_spmd(nc, [{f"in_{n}": a for n, a in arrays.items()}], core_ids=[0])
    o = r.results[0]["out"]
    return np.ascontiguousarray(o.transpose(2, 1, 0)).reshape(1, SEQ, D)
```
